# Optimizing a Trainium2 kernel written in Bass

```python
import functools
import jax, jax.numpy as jnp
from jax import lax
import numpy as np

D_MODEL = 1024
BATCH = 1
SEQ = 128
DEPTH = 2
DEC_BATCH = 1
DEC_SEQ = 256
PAST_LEN = 128

GRID_W = 64
CONV_W = D_MODEL
CONV_K = 3
NA_HEADS = 8
NA_HEAD_DIM = D_MODEL // NA_HEADS
NA_WIDTH = NA_HEADS * NA_HEAD_DIM
NA_MAX_ROWS = 8
NA_COLS = 16
COL_BLOCK = 16
COL_BAND = 2 * COL_BLOCK
FNET_GROUPS = 4
FNET_GROUP_DIM = D_MODEL // FNET_GROUPS
FNET_WIDTH = FNET_GROUPS * FNET_GROUP_DIM
N_BRANCH = 3
IN_SPLITS = (CONV_W, 2 * CONV_W, 3 * CONV_W,
             3 * CONV_W + NA_WIDTH, 3 * CONV_W + 2 * NA_WIDTH, 3 * CONV_W + 3 * NA_WIDTH,
             3 * CONV_W + 3 * NA_WIDTH + FNET_WIDTH)
IN_COLS = 3 * CONV_W + 3 * NA_WIDTH + FNET_WIDTH + N_BRANCH * D_MODEL
PEER_HEADS = 8
PEER_KEYS = 128
PEER_EXPERTS = PEER_KEYS * PEER_KEYS
PEER_KEY_DIM = 128
PEER_TOPK = 16
TOKEN_BLOCK = 128
Q_BLOCK = 128
N_MOD = 6
RMS_EPS = 1e-6
NEG_INF = -1e30

kernel_name = 'hybrid_natten_conv_fnet_peer_diffusion_step'

def rmsnorm(x, g):
    xf = x.astype(jnp.float32)
    y = xf * lax.rsqrt(jnp.mean(xf * xf, axis=-1, keepdims=True) + RMS_EPS)
    return (y * g.astype(jnp.float32)).astype(x.dtype)

def modulate(h, shift, scale):
    return h * (1 + scale) + shift

def short_conv(u, w):
    C = u.shape[-1]
    return lax.conv_general_dilated(u, w[:, None, :].astype(u.dtype), window_strides=(1,),
                                    padding=((CONV_K // 2, CONV_K // 2),),
                                    dimension_numbers=('NWC', 'WIO', 'NWC'),
                                    feature_group_count=C)

def fourier_mix(u):
    B, S, _ = u.shape
    ug = u.reshape(B, S, FNET_GROUPS, FNET_GROUP_DIM).astype(jnp.float32)
    f = jnp.fft.fft2(ug, axes=(1, 3), norm='ortho').real
    return f.reshape(B, S, FNET_WIDTH).astype(u.dtype)

def context_attention(q, k, v):
    B, S, H, dh = q.shape
    nb = S // Q_BLOCK
    scale = dh ** -0.5
    kf = k.astype(jnp.float32)
    vf = v.astype(jnp.float32)
    qb = q.astype(jnp.float32).reshape(B, nb, Q_BLOCK, H, dh).transpose(1, 0, 2, 3, 4)

    def one_block(qi):
        s = jnp.einsum('bqhd,bkhd->bhqk', qi, kf) * scale
        p = jax.nn.softmax(s, axis=-1)
        return jnp.einsum('bhqk,bkhd->bqhd', p, vf)

    o = lax.map(one_block, qb)
    return o.transpose(1, 0, 2, 3, 4).reshape(B, S, H * dh).astype(q.dtype)

def neighbourhood_attention(q, k, v, k_ctx, v_ctx, rpb):
    B, S, H, dh = q.shape
    rows = S // GRID_W
    kr = min(NA_MAX_ROWS, rows)
    ncb = GRID_W // COL_BLOCK
    scale = dh ** -0.5
    r = jnp.arange(rows)
    r0 = jnp.clip(r - kr // 2, 0, rows - kr)
    row_idx = r0[:, None] + jnp.arange(kr)
    j = jnp.arange(ncb)
    b0 = jnp.clip(j * COL_BLOCK - COL_BLOCK // 2, 0, GRID_W - COL_BAND)
    col_idx = b0[:, None] + jnp.arange(COL_BAND)
    qcol = j[:, None] * COL_BLOCK + jnp.arange(COL_BLOCK)
    c0 = jnp.clip(qcol - NA_COLS // 2, 0, GRID_W - NA_COLS)
    kcol = col_idx[:, None, :]
    in_win = (kcol >= c0[..., None]) & (kcol < c0[..., None] + NA_COLS)
    dr = row_idx - r[:, None] + (NA_MAX_ROWS - 1)
    dc = jnp.clip(kcol - qcol[..., None] + (NA_COLS - 1), 0, 2 * NA_COLS - 2)
    bias = rpb[:, dr[:, None, None, :, None], dc[None, :, :, None, :]]
    bias = jnp.transpose(bias, (1, 2, 3, 0, 4, 5)).astype(jnp.float32)
    bias = jnp.where(in_win[None, :, :, None, None, :], bias, NEG_INF)

    qg = q.astype(jnp.float32).reshape(B, rows, ncb, COL_BLOCK, H, dh)
    gather = lambda t: t.astype(jnp.float32).reshape(B, rows, GRID_W, H, dh)[
        :, row_idx[:, :, None, None], col_idx[None, None, :, :]]
    kg = gather(k)
    vg = gather(v)
    kc = k_ctx.astype(jnp.float32)
    vc = v_ctx.astype(jnp.float32)
    s_loc = jnp.einsum('brjqhd,brkjchd->brjqhkc', qg, kg) * scale + bias[None]
    s_ctx = jnp.einsum('brjqhd,blhd->brjqhl', qg, kc) * scale
    n_loc = kr * COL_BAND
    s = jnp.concatenate([s_loc.reshape(s_loc.shape[:5] + (n_loc,)), s_ctx], axis=-1)
    p = jax.nn.softmax(s, axis=-1)
    p_loc = p[..., :n_loc].reshape(s_loc.shape)
    p_ctx = p[..., n_loc:]
    o = (jnp.einsum('brjqhkc,brkjchd->brjqhd', p_loc, vg)
         + jnp.einsum('brjqhl,blhd->brjqhd', p_ctx, vc))
    return o.reshape(B, S, H * dh).astype(q.dtype)

def peer_ffn(h, w_pq, sub_keys, peer_u, peer_v):
    B, S, D = h.shape
    T = B * S
    hf = h.reshape(T, D)
    q = (hf @ w_pq).reshape(T, PEER_HEADS, 2, PEER_KEY_DIM)
    s = jnp.einsum('thpd,hpnd->thpn', q.astype(jnp.float32), sub_keys.astype(jnp.float32))
    s1, i1 = lax.top_k(s[:, :, 0], PEER_TOPK)
    s2, i2 = lax.top_k(s[:, :, 1], PEER_TOPK)
    cand_s = (s1[..., :, None] + s2[..., None, :]).reshape(T, PEER_HEADS, PEER_TOPK * PEER_TOPK)
    cand_i = (i1[..., :, None] * PEER_KEYS + i2[..., None, :]).reshape(T, PEER_HEADS, PEER_TOPK * PEER_TOPK)
    top_s, pos = lax.top_k(cand_s, PEER_TOPK)
    e_idx = jnp.take_along_axis(cand_i, pos, axis=-1).reshape(T, PEER_HEADS * PEER_TOPK)
    gate = jax.nn.softmax(top_s, axis=-1).reshape(T, PEER_HEADS * PEER_TOPK)
    nb = T // TOKEN_BLOCK
    HK = PEER_HEADS * PEER_TOPK

    def one_block(args):
        xb, ib, gb = args
        ub = jnp.take(peer_u, ib, axis=0).astype(jnp.float32)
        a = jnp.einsum('tkd,td->tk', ub, xb.astype(jnp.float32))
        a = jax.nn.gelu(a, approximate=False) * gb
        vb = jnp.take(peer_v, ib, axis=0).astype(jnp.float32)
        return jnp.einsum('tk,tkd->td', a, vb).astype(xb.dtype)

    out = lax.map(one_block, (hf.reshape(nb, TOKEN_BLOCK, D),
                              e_idx.reshape(nb, TOKEN_BLOCK, HK),
                              gate.reshape(nb, TOKEN_BLOCK, HK)))
    return out.reshape(B, S, D)

def trunk_layer(x, mod, lp, attend):
    (w_in, conv_w, w_conv_out, w_attn_out, w_four_out, w_o,
     g_mix, g_ffn, w_pq, sub_keys, peer_u, peer_v) = lp
    shift1, scale1, gate1, shift2, scale2, gate2 = mod
    B, S, _ = x.shape
    h = modulate(rmsnorm(x, g_mix), shift1, scale1)
    z = h @ w_in
    cb, cc, cx, q, k, v, f, gl = jnp.split(z, IN_SPLITS, axis=-1)
    y_conv = (cb * short_conv(cc * cx, conv_w)) @ w_conv_out
    q = q.reshape(B, S, NA_HEADS, NA_HEAD_DIM)
    k = k.reshape(B, S, NA_HEADS, NA_HEAD_DIM)
    v = v.reshape(B, S, NA_HEADS, NA_HEAD_DIM)
    y_att = attend(q, k, v) @ w_attn_out
    y_four = fourier_mix(f) @ w_four_out
    g = jax.nn.sigmoid(gl.astype(jnp.float32)).astype(x.dtype).reshape(B, S, N_BRANCH, D_MODEL)
    merged = g[:, :, 0] * y_conv + g[:, :, 1] * y_att + g[:, :, 2] * y_four
    x = x + gate1 * (merged @ w_o)
    h = modulate(rmsnorm(x, g_ffn), shift2, scale2)
    x = x + gate2 * peer_ffn(h, w_pq, sub_keys, peer_u, peer_v)
    return x, k, v

def setup_inputs(seed: int = 0) -> dict:
    key = jax.random.key(seed)
    ks = jax.random.split(key, 24)
    nrm = lambda k, shape, s: jax.random.normal(k, shape, jnp.float32) * s
    L = DEPTH
    return {
        'x_prompt': nrm(ks[0], (BATCH, SEQ, D_MODEL), 1.0),
        'x_sample': nrm(ks[1], (DEC_BATCH, DEC_SEQ, D_MODEL), 1.0),
        'cache_k': nrm(ks[2], (DEC_BATCH, DEPTH, PAST_LEN, NA_HEADS, NA_HEAD_DIM), 1.0),
        'cache_v': nrm(ks[3], (DEC_BATCH, DEPTH, PAST_LEN, NA_HEADS, NA_HEAD_DIM), 1.0),
        'c': nrm(ks[4], (DEC_BATCH, D_MODEL), 1.0),
        'c_ctx': nrm(ks[5], (D_MODEL,), 1.0),
        'w_in': nrm(ks[6], (L, D_MODEL, IN_COLS), D_MODEL ** -0.5),
        'conv_w': nrm(ks[7], (L, CONV_K, CONV_W), CONV_K ** -0.5),
        'w_conv_out': nrm(ks[8], (L, CONV_W, D_MODEL), CONV_W ** -0.5),
        'rpb': nrm(ks[9], (L, NA_HEADS, 2 * NA_MAX_ROWS - 1, 2 * NA_COLS - 1), 0.1),
        'w_attn_out': nrm(ks[10], (L, NA_WIDTH, D_MODEL), NA_WIDTH ** -0.5),
        'w_four_out': nrm(ks[11], (L, FNET_WIDTH, D_MODEL), FNET_WIDTH ** -0.5),
        'w_o': nrm(ks[12], (L, D_MODEL, D_MODEL), D_MODEL ** -0.5),
        'g_mix': 1.0 + nrm(ks[13], (L, D_MODEL), 0.02),
        'g_ffn': 1.0 + nrm(ks[14], (L, D_MODEL), 0.02),
        'w_mod': nrm(ks[15], (L, D_MODEL, N_MOD * D_MODEL), D_MODEL ** -0.5),
        'b_mod': nrm(ks[16], (L, N_MOD * D_MODEL), 0.02),
        'w_pq': nrm(ks[17], (L, D_MODEL, PEER_HEADS * 2 * PEER_KEY_DIM), D_MODEL ** -0.5),
        'sub_keys': nrm(ks[18], (L, PEER_HEADS, 2, PEER_KEYS, PEER_KEY_DIM), PEER_KEY_DIM ** -0.5),
        'peer_u': nrm(ks[19], (L, PEER_EXPERTS, D_MODEL), D_MODEL ** -0.5),
        'peer_v': nrm(ks[20], (L, PEER_EXPERTS, D_MODEL), (PEER_HEADS * PEER_TOPK) ** -0.5),
        'g_final': 1.0 + nrm(ks[21], (D_MODEL,), 0.02),
    }

def reference(x_prompt, x_sample, cache_k, cache_v, c, c_ctx, w_in, conv_w, w_conv_out, rpb,
              w_attn_out, w_four_out, w_o, g_mix, g_ffn, w_mod, b_mod, w_pq, sub_keys,
              peer_u, peer_v, g_final):
    xp = x_prompt
    xs = x_sample
    ctx_k, ctx_v = [], []
    for l in range(DEPTH):
        lp = (w_in[l], conv_w[l], w_conv_out[l], w_attn_out[l], w_four_out[l], w_o[l],
              g_mix[l], g_ffn[l], w_pq[l], sub_keys[l], peer_u[l], peer_v[l])
        mod_ctx = (jax.nn.silu(c_ctx) @ w_mod[l] + b_mod[l]).reshape(N_MOD, 1, 1, D_MODEL)
        mod_lat = (jax.nn.silu(c) @ w_mod[l] + b_mod[l]).reshape(-1, N_MOD, D_MODEL)
        mod_lat = mod_lat.transpose(1, 0, 2)[:, :, None, :]
        xp, k_l, v_l = trunk_layer(xp, mod_ctx, lp, context_attention)
        ctx_k.append(k_l)
        ctx_v.append(v_l)
        attend_lat = functools.partial(neighbourhood_attention, k_ctx=cache_k[:, l],
                                       v_ctx=cache_v[:, l], rpb=rpb[l])
        xs, _, _ = trunk_layer(xs, mod_lat, lp, attend_lat)
    y_prompt = rmsnorm(xp, g_final)
    y_sample = rmsnorm(xs, g_final)
    new_cache_k = jnp.stack(ctx_k, axis=1)
    new_cache_v = jnp.stack(ctx_v, axis=1)
    return (y_prompt, y_sample, new_cache_k, new_cache_v)


_drawn_inputs = setup_inputs


def setup_inputs(seed=0):
    import zlib

    import numpy as np

    out = dict(_drawn_inputs(seed))
    spreads = {}
    factors = {'rpb': 8.0, 'g_ffn': 8.0, 'g_final': 2.706}
    for name, (base, spread) in spreads.items():
        noise = np.random.default_rng([zlib.crc32(name.encode()), seed]).standard_normal(out[name].shape)
        drawn = base * np.exp(spread * noise) if base else spread * noise
        out[name] = __import__('jax').numpy.asarray(drawn.astype(out[name].dtype))
    for name, factor in factors.items():
        out[name] = (out[name] * factor).astype(out[name].dtype)
    return out
```

```python
import concourse.bass as bass
import concourse.mybir as mybir

F32 = mybir.dt.float32
F32R = mybir.dt.float32r
U32 = mybir.dt.uint32
ALU = mybir.AluOpType
ACT = mybir.ActivationFunctionType
AX = mybir.AxisListType

DEPTH = 2
P = 128
D = 1024
KT = D // P
TP, TS = 128, 256
T = TP + TS
TT = T // P
STREAMS = ((0, TP), (TP, T))
HEADS = 8
DH = 128
CTX = 128
GRID_W = 64
WIN = 16
SCALE = DH ** -0.5
KEYS = TS + CTX
SCORES = TP + 2 * KEYS
PH = 8
NK = 128
TOPK = 16
HK = PH * TOPK
EPS = 1e-6
LOWEST = -3.0e38
N_MOD = 6
SHIFT1, SCALE1, GATE1, SHIFT2, SCALE2, GATE2 = range(N_MOD)
FG, FD = 4, 256

SLOTS = 4
_groups = (("mod", N_MOD * KT), ("ccx", 2 * KT), ("cb", KT), ("qkvf", 4 * KT), ("gates", 3 * KT),
           ("conv_out", KT), ("attn_out", KT), ("four_out", KT), ("o", KT), ("pq", 2 * PH),
           ("peer", 2 * NK))
FIRST, COUNT, _at = {}, {}, 0
for _name, _panels in _groups:
    FIRST[_name], COUNT[_name] = _at, _panels // SLOTS
    _at += _panels // SLOTS
GROUPS = _at
PROJ = FIRST["peer"]

HALF = NK // 2
BATCH = 8
NB = T // BATCH

B_MOD, G_MIX, G_FFN, CONV_W = 0, N_MOD * KT, N_MOD * KT + KT, N_MOD * KT + 2 * KT
VEC = CONV_W + 3 * KT
PAD = T + 4
SEG = ((1, 1 + TP), (3 + TP, 3 + T))
DFT_CH, DFT_P, DFT_S = 0, 2 * 512, 2 * 512 + 2 * TP
DFT = DFT_S + 2 * 2 * TS


def build(nc, panels, x_in, c_in, vecs, g_final, k_cache, v_cache, bias_in, mask_in, dft_in,
          sub_keys, ident_in, iota_in, y_out, new_k, new_v):
    base = 1152

    def place(name, where, cols, dt=F32):
        return nc.alloc_sbuf_tensor_at(name, [P, cols], dt, offset=where), where + 4 * cols

    raw, o = place("raw", base, SLOTS * D)
    split_hi, o = place("split_hi", o, 2 * D, F32R)
    split_lo, o = place("split_lo", o, 2 * D, F32R)
    h_hi, o = place("h_hi", o, KT * T, F32R)
    h_lo, o = place("h_lo", o, KT * T, F32R)
    x, o = place("x", o, KT * T)
    ident, o = place("ident", o, P)
    iota, o = place("iota", o, P)
    ones, o = place("ones", o, P)
    mask, o = place("mask", o, GRID_W)
    vec, o = place("vec", o, VEC)
    modv, o = place("modv", o, N_MOD * KT * 2)
    gain, o = place("gain", o, 2 * KT * 2)
    c_t, o = place("c_t", o, KT * 2)
    c_hi, o = place("c_hi", o, KT * 2, F32R)
    c_lo, o = place("c_lo", o, KT * 2, F32R)
    gfin, o = place("gfin", o, KT)
    softm, o = place("softm", o, 2 * 16)
    arena = o

    qkvf, o = place("qkvf", arena, 4 * KT * T)
    q, k, v, f = (qkvf[:, i * KT * T:(i + 1) * KT * T] for i in range(4))
    gate01, o = place("gate01", o, 2 * KT * T)
    gate0, gate1 = gate01[:, 0:KT * T], gate01[:, KT * T:2 * KT * T]
    gate2, _ = place("gate2", o, KT * T)
    conv, o = place("conv", o, KT * PAD)
    u_hi, o = place("u_hi", o, KT * T, F32R)
    u_lo, o = place("u_lo", o, KT * T, F32R)
    bias, o = place("bias", o, 2 * 2 * TS)
    kc, o = place("kc", o, HEADS * CTX)
    vc, o = place("vc", o, HEADS * DH)
    prob_at = o
    prob, o = place("prob", o, 2 * SCORES)
    prob_t, o = place("prob_t", o, 2 * SCORES)
    dft, mixer_end = place("dft", o, DFT)
    cc_s, o = place("cc_s", prob_at, 2 * T)
    ccx, o = place("ccx", o, 2 * PAD)
    cb_s, o = place("cb_s", o, 2 * T)
    branch, _ = place("branch", prob_at, SLOTS * T)
    f_hi, o = place("f_hi", arena, KT * T, F32R)
    f_lo, o = place("f_lo", o, KT * T, F32R)
    fy, _ = place("fy", o, 2 * TT * 512)
    sq, o = place("sq", arena, KT * T)
    hf, o = place("hf", o, KT * T)
    ms, o = place("ms", o, T)
    rstd, _ = place("rstd", o, T)
    gates, o = place("gates", arena, HALF * T)
    gates_end = o
    gel, o = place("gel", o, 2 * T)
    act_f, o = place("act_f", o, 2 * T)
    a_hi, o = place("a_hi", o, 2 * T, F32R)
    a_lo, o = place("a_lo", o, 2 * T, F32R)
    hot2, o = place("hot2", o, 2 * BATCH * P)
    hot1, o = place("hot1", o, 2 * BATCH * HALF)
    route_t, o = place("route_t", o, 3 * T)
    cols, o = place("cols", o, 2 * 3 * BATCH)
    subk, peer_end = place("subk", o, 2 * PH * NK)
    y_nat, _ = place("y_nat", arena, TT * D)
    pq, o = place("pq", arena, SLOTS * T)
    sc, o = place("sc", o, SLOTS * TT * NK)
    sc2, o = place("sc2", o, TT * NK)
    val, o = place("val", o, SLOTS * TT * TOPK)
    idx, o = place("idx", o, SLOTS * TT * TOPK, U32)
    vals, o = place("vals", o, TT * 2 * PH * TOPK)
    idxs, o = place("idxs", o, TT * 2 * PH * TOPK)
    cand, o = place("cand", o, PH * TOPK * TOPK)
    cand2, o = place("cand2", o, PH * TOPK * TOPK)
    best, o = place("best", o, HK)
    pos, o = place("pos", o, HK, U32)
    pos_ab, o = place("pos_ab", o, 2 * HK, U32)
    pos_f, o = place("pos_f", o, 2 * HK)
    eq, o = place("eq", o, 2 * HK * TOPK)
    route, o = place("route", o, 3 * HK)
    gsum, o = place("gsum", o, 2 * PH)
    assert o <= gates_end and max(mixer_end, peer_end) <= 229344

    bank = [nc.alloc_psum_tensor(f"bank{i}", [P, 512], F32) for i in range(8)]

    sem = nc.alloc_semaphore
    consts_loaded = sem("consts_loaded")
    panel_loaded = [sem(f"panel_loaded{s}") for s in range(SLOTS)]
    hi_ready = [sem(f"hi_ready{s}") for s in range(SLOTS)]
    lo_ready = [sem(f"lo_ready{s}") for s in range(SLOTS)]
    panel_used = [sem(f"panel_used{b}") for b in range(2)]
    bank_free = [sem(f"bank_free{s}") for s in range(SLOTS)]
    layer_loaded = sem("layer_loaded")
    sub_loaded = sem("sub_loaded")
    bias_loaded = [sem("bias_loaded0"), sem("bias_loaded1")]
    bias_masked = sem("bias_masked")
    ones_ready = sem("ones_ready")
    c_ready = sem("c_ready")
    squares = sem("squares")
    sums = sem("sums")
    mean_sq = sem("mean_sq")
    root = sem("root")
    hf_ready = sem("hf_ready")
    hhi_ready = sem("hhi_ready")
    hlo_ready = sem("hlo_ready")
    uhi_ready = sem("uhi_ready")
    ulo_ready = sem("ulo_ready")
    vt_ready = sem("vt_ready")
    vt_act = sem("vt_act")
    vt_dve = sem("vt_dve")
    kv_out = sem("kv_out")
    s_ready = sem("s_ready")
    s_read = sem("s_read")
    max_ready = sem("max_ready")
    exp_ready = sem("exp_ready")
    prob_ready = sem("prob_ready")
    pt_ready = sem("pt_ready")
    pt_act = sem("pt_act")
    pt_dve = sem("pt_dve")
    o_ready = sem("o_ready")
    o_hi = sem("o_hi")
    o_lo = sem("o_lo")
    y1_ready = sem("y1_ready")
    y1_act = sem("y1_act")
    y1_dve = sem("y1_dve")
    y2_ready = sem("y2_ready")
    y2_hi = sem("y2_hi")
    y2_lo = sem("y2_lo")
    merged = sem("merged")
    mhi_ready = sem("mhi_ready")
    mlo_ready = sem("mlo_ready")
    keys_done = sem("keys_done")
    sc_ready = sem("sc_ready")
    sc_used = sem("sc_used")
    top_shifted = sem("top_shifted")
    top_exp = sem("top_exp")
    route_ready = sem("route_ready")
    route_tr = sem("route_tr")
    route_done = sem("route_done")
    hot_ready = sem("hot_ready")
    gate_mm = sem("gate_mm")
    gate_copied = sem("gate_copied")
    gelu_ready = sem("gelu_ready")
    act_ready = sem("act_ready")
    ahi_ready = sem("ahi_ready")
    alo_ready = sem("alo_ready")
    y_act = sem("y_act")
    y_dve = sem("y_dve")
    yt_ready = sem("yt_ready")
    x_updated = sem("x_updated")
    out_ready = sem("out_ready")
    out_done = sem("out_done")
    carried = sem("carried")
    dve_seq = sem("dve_seq")
    CONSTS = 7
    LOADS = 4

    class Order:

        def __init__(self):
            self.base, self.n = 0, 0

        def step(self, ins, wait=True, hold=False):
            ins.then_inc(dve_seq, 1)
            self.n += 1
            if wait:
                self.wait()
                if hold:
                    carry(nc.vector)

        def wait(self):
            nc.vector.wait_ge(dve_seq, self.base + self.n)

        def enter(self, i, start, steps):
            saved = self.base, self.n
            self.base, self.n = self.base + self.n + (i - start) * steps, 0
            return saved

        def leave(self, saved, turns, steps):
            assert self.n == steps, f"{self.n} steps in a loop's body, not {steps}"
            self.base, self.n = saved[0], saved[1] + turns * steps

    def col(t, n, width=T):
        return t[:, n * width:(n + 1) * width]

    def ahead(g, s):
        return (g, s + 2) if s < 2 else (g + 1, s - 2)

    def after_use(g, s):
        return 2 * g + s // 2 + 2

    def wait_split(eng, g, s):
        eng.wait_ge(panel_loaded[s], (g + 1) * 16)
        eng.wait_ge(panel_used[s % 2], after_use(g, s) - 1)

    def split_panel_hi(g, s):
        wait_split(nc.scalar, g, s)
        nc.scalar.activation(col(split_hi, s % 2, D), col(raw, s, D), ACT.Copy).then_inc(hi_ready[s], 1)

    def split_panel_lo(eng, g, s):
        wait_split(eng, g, s)
        eng.wait_ge(hi_ready[s], g + 1)
        eng.tensor_tensor(col(split_lo, s % 2, D), col(raw, s, D), col(split_hi, s % 2, D).bitcast(F32),
                          ALU.subtract).then_inc(lo_ready[s], 1)

    def carry(eng):
        eng.sem_inc(carried, 1)

    def wait_stored(eng, l, name):
        for s in range(SLOTS):
            eng.wait_ge(bank_free[s], l * PROJ + FIRST[name] + 1)

    block_cm = nc.Block()
    block = block_cm.__enter__()

    @block.sync
    def _(sp):
        for dst, src in ((x, x_in), (c_t, c_in), (ident, ident_in), (iota, iota_in), (mask, mask_in),
                         (gfin, g_final), (dft, dft_in)):
            sp.dma_start(dst[:, :], src).then_inc(consts_loaded, 16)
        for s in range(SLOTS):
            sp.dma_start(col(raw, s, D), panels[s, :, :]).then_inc(panel_loaded[s], 16)
        with sp.Fori(1, DEPTH * GROUPS) as g:
            for s in range(SLOTS):
                sp.wait_ge(hi_ready[s], g)
                sp.wait_ge(lo_ready[s], g)
                sp.dma_start(col(raw, s, D), panels[g * SLOTS + s, :, :]).then_inc(panel_loaded[s], 16)
        sp.wait_ge(out_ready, 1)
        sp.dma_start(y_out, hf[:, :]).then_inc(out_done, 16)
        sp.wait_ge(out_done, 16)
        sp.wait_ge(kv_out, DEPTH * 32)

    @block.tensor
    def _(pe):
        mm = nc.tensor.matmul
        transpose = lambda out, in_: nc.tensor.transpose(out, in_, ident[:, :])

        def panel(g, s, out, rhs_hi, rhs_lo, n):
            pe.wait_ge(hi_ready[s], g + 1)
            pe.wait_ge(lo_ready[s], g + 1)
            for kk in range(KT):
                w_hi, w_lo = col(col(split_hi, s % 2, D), kk, P), col(col(split_lo, s % 2, D), kk, P)
                mm(out, w_hi, col(rhs_hi, kk, n), start=(kk == 0), stop=False)
                mm(out, w_hi, col(rhs_lo, kk, n), start=False, stop=False)
                last = mm(out, w_lo, col(rhs_hi, kk, n), start=False, stop=(kk == KT - 1))
            last.then_inc(panel_used[s % 2], 1)

        def project(l, local, s, rhs_hi, rhs_lo, n=T):
            pe.wait_ge(bank_free[s], l * PROJ + local + 1)
            panel(l * GROUPS + local, s, bank[s][:, 0:n], rhs_hi, rhs_lo, n)

        def stage(l, name, rhs_hi, rhs_lo, n=T):
            carry(pe)
            with pe.Fori(0, COUNT[name]) as i:
                for s in range(SLOTS):
                    project(l, i + FIRST[name], s, rhs_hi, rhs_lo, n)

        def norm_sums(n):
            pe.wait_ge(squares, n)
            for kk in range(KT):
                last = mm(bank[4][:, 0:T], ones[:, :], col(sq, kk), start=(kk == 0), stop=(kk == KT - 1))
            last.then_inc(sums, 1)

        pe.sem_inc(panel_used[0], 1)
        pe.sem_inc(panel_used[1], 1)
        pe.sem_inc(keys_done, 4)
        pe.sem_inc(route_tr, 1)
        pe.sem_inc(gate_mm, 2)
        pe.wait_ge(ones_ready, 1)
        pe.wait_ge(consts_loaded, CONSTS * 16)
        with pe.Fori(0, DEPTH) as l:
            norm_sums(2 * l + 1)
            pe.wait_ge(c_ready, 3)
            stage(l, "mod", c_hi, c_lo, 2)
            pe.wait_ge(hlo_ready, l * 16 + 8)
            for name in ("ccx", "cb", "qkvf", "gates"):
                stage(l, name, h_hi, h_lo)

            wait_stored(pe, l, "conv_out")
            for h in range(HEADS):
                if h >= 4:
                    pe.wait_ge(vt_dve if h % 2 else vt_act, l * 4 + h // 2 - 1)
                for t in range(TT):
                    last = transpose(bank[4 + h % 4][:, t * P:(t + 1) * P], col(v, h)[:, t * P:(t + 1) * P])
                last.then_inc(vt_ready, 1)
            pe.wait_ge(vt_act, l * 4 + 4)
            pe.wait_ge(vt_dve, l * 4 + 4)
            pe.wait_ge(layer_loaded, (l + 1) * LOADS * 16)

            def scores(h):
                if h >= 1:
                    pe.wait_ge(s_read, l * HEADS + h)
                qh, kh = col(q, h), col(k, h)
                mm(bank[4][:, 0:TP], qh[:, 0:TP], kh[:, 0:TP], start=True, stop=True)
                for j in range(2):
                    qt = qh[:, TP + j * P:TP + (j + 1) * P]
                    c0 = TP if j == 0 else 0
                    mm(bank[4 + j][:, c0:c0 + TS], qt, kh[:, TP:T], start=True, stop=True)
                    last = mm(bank[4 + j][:, c0 + TS:c0 + KEYS], qt, col(kc, h, CTX), start=True, stop=True)
                last.then_inc(s_ready, 1)

            scores(0)
            for h in range(HEADS):
                if h + 1 < HEADS:
                    scores(h + 1)
                if h == 0:
                    pe.wait_ge(uhi_ready, (l + 1) * KT)
                    pe.wait_ge(ulo_ready, (l + 1) * KT + 2)
                project(l, FIRST["conv_out"] + h // SLOTS, h % SLOTS, u_hi, u_lo)
                pr, pt, vh = col(prob, h % 2, SCORES), col(prob_t, h % 2, SCORES), col(v, h)
                pe.wait_ge(prob_ready, l * HEADS + h + 1)
                if h >= 1:
                    pe.wait_ge(o_lo, l * HEADS + h)
                for kt in range(3):
                    for j in range(2):
                        c0 = kt * TS + j * P
                        transpose(bank[6 + c0 // 512][:, c0 % 512:c0 % 512 + P],
                                  pr[:, TP + j * KEYS + kt * P:TP + j * KEYS + (kt + 1) * P])
                transpose(bank[7][:, TS:TS + P], pr[:, 0:TP]).then_inc(pt_ready, 1)
                pe.wait_ge(pt_act, l * HEADS + h + 1)
                pe.wait_ge(pt_dve, l * HEADS + h + 1)
                mm(bank[6][:, 0:TP], vh[:, 0:P], pt[:, 3 * TS:3 * TS + TP], start=True, stop=True)
                mm(bank[6][:, TP:T], vh[:, P:2 * P], pt[:, 0:TS], start=True, stop=False)
                mm(bank[6][:, TP:T], vh[:, 2 * P:3 * P], pt[:, TS:2 * TS], start=False, stop=False)
                mm(bank[6][:, TP:T], col(vc, h, DH), pt[:, 2 * TS:3 * TS], start=False,
                   stop=True).then_inc(o_ready, 1)

            def fourier_channels(g):
                for t in range(TT):
                    u = g * TT + t
                    if u >= 2:
                        pe.wait_ge(y1_dve if u % 2 else y1_act, l * 6 + u // 2)
                    for c in range(2):
                        last = mm(bank[4 + u % 2][:, :], col(f, 2 * g + c)[:, t * P:(t + 1) * P],
                                  dft[:, DFT_CH + c * 512:DFT_CH + (c + 1) * 512], start=(c == 0), stop=(c == 1))
                    last.then_inc(y1_ready, 1)

            def fourier_tokens(g):
                pe.wait_ge(y1_act, l * 6 + (TT * (g + 1) + 1) // 2)
                pe.wait_ge(y1_dve, l * 6 + TT * (g + 1) // 2)
                yg = col(fy, g % 2, TT * 512)
                for dt in range(2):
                    u = 2 * g + dt
                    if u >= 2:
                        pe.wait_ge(y2_lo, l * 8 + u - 1)
                    out = bank[6 + u % 2]
                    for part in range(2):
                        w = yg[:, part * FD + dt * P:part * FD + (dt + 1) * P]
                        mm(out[:, 0:TP], w, dft[:, DFT_P + part * TP:DFT_P + (part + 1) * TP],
                           start=(part == 0), stop=(part == 1))
                    for t in range(2):
                        for part in range(2):
                            w0 = (1 + t) * 512 + part * FD + dt * P
                            r0 = DFT_S + (2 * t + part) * TS
                            last = mm(out[:, TP:T], yg[:, w0:w0 + P], dft[:, r0:r0 + TS],
                                      start=(t + part == 0), stop=(t + part == 2))
                    last.then_inc(y2_ready, 1)

            pe.wait_ge(o_lo, (l + 1) * HEADS)
            fourier_channels(0)
            for g in range(1, FG):
                fourier_channels(g)
                fourier_tokens(g - 1)
            fourier_tokens(FG - 1)

            stage(l, "attn_out", h_hi, h_lo)
            pe.wait_ge(y2_lo, (l + 1) * 8)
            stage(l, "four_out", f_hi, f_lo)
            pe.wait_ge(mhi_ready, (l + 1) * KT)
            pe.wait_ge(mlo_ready, (l + 1) * KT)
            stage(l, "o", u_hi, u_lo)

            norm_sums(2 * l + 2)
            pe.wait_ge(hlo_ready, l * 16 + 16)
            pe.wait_ge(sub_loaded, (l + 1) * 16)

            carry(pe)

            def keys(i, s):
                n = (l * COUNT["pq"] + i) * SLOTS + s
                pe.wait_ge(bank_free[s], l * PROJ + FIRST["pq"] + i + 2)
                pe.wait_ge(sc_ready, n + 1)
                for t in range(TT):
                    last = mm(col(bank[4 + s], t, NK), col(col(pq, s), t, P),
                              subk[:, bass.ds((i * SLOTS + s) * NK, NK)], start=True, stop=True)
                last.then_inc(keys_done, 1)

            with pe.Fori(0, COUNT["pq"]) as i:
                for s in range(SLOTS):
                    project(l, i + FIRST["pq"], s, h_hi, h_lo)
                    if s:
                        keys(i, s - 1)
                keys(i, SLOTS - 1)

            with pe.Fori(0, TT) as t:
                pe.wait_ge(route_ready, l * TT + t + 1)
                pe.wait_ge(route_done, l * TT + t + 1)
                for j in range(3):
                    last = transpose(col(bank[4], j, P), col(route, j, HK))
                last.then_inc(route_tr, 1)

            def build_gates(half):
                carry(pe)
                with pe.Fori(0, NB // 2) as i:
                    for b in range(2):
                        n = (l * 2 + half) * NB + i * 2 + b
                        pe.wait_ge(hot_ready, n + 1)
                        pe.wait_ge(gate_copied, n + 1)
                        for t in range(BATCH):
                            last = mm(col(bank[b], t, HALF), col(hot2, b * BATCH + t, P),
                                      col(hot1, b * BATCH + t, HALF), start=True, stop=True)
                        last.then_inc(gate_mm, 1)

            peer = l * GROUPS + FIRST["peer"]

            def outputs_v(g, s, b, j, first=False, last=False):
                pe.wait_ge(hi_ready[s], g + 1)
                pe.wait_ge(lo_ready[s], g + 1)
                pe.wait_ge(ahi_ready, l * NK + j + 3)
                pe.wait_ge(alo_ready, l * NK + j + 1)
                hi, lo = col(split_hi, s % 2, D), col(split_lo, s % 2, D)
                for t in range(TT):
                    w_hi, w_lo = col(col(a_hi, b), t, P), col(col(a_lo, b), t, P)
                    for w, rhs, start, stop in ((w_hi, hi, first, False), (w_hi, lo, False, False),
                                                (w_lo, hi, False, last)):
                        for c in range(2):
                            m = mm(bank[2 + 2 * t + c][:, :], w, col(rhs, c, 512), start=start, stop=stop)
                m.then_inc(panel_used[s % 2], 1)

            def pair(i, first=False):
                g, j = peer + i, 2 * i
                for b, (gu, su), (gv, sv) in ((1, (g, 1), (g, 2)), (0, (g, 3), (g + 1, 0))):
                    jj = j + 1 - b
                    if not (first and b):
                        pe.wait_ge(gelu_ready, l * NK + jj)
                    panel(gu, su, bank[b][:, 0:T], h_hi, h_lo, T)
                    outputs_v(gv, sv, 1 - b, jj, first=first and b == 1)

            build_gates(0)
            pe.wait_ge(gate_copied, (l * 2 + 1) * NB + 2)
            panel(peer, 0, bank[0][:, 0:T], h_hi, h_lo, T)
            pair(0, first=True)
            with pe.Fori(1, HALF // 2) as i:
                pair(i)
            pe.wait_ge(gelu_ready, l * NK + HALF + 1)
            build_gates(1)
            pe.wait_ge(gate_copied, (l * 2 + 2) * NB + 2)
            carry(pe)
            with pe.Fori(HALF // 2, HALF - 1) as i:
                pair(i)
            pe.wait_ge(gelu_ready, l * NK + NK - 2)
            panel(peer + HALF - 1, 1, bank[1][:, 0:T], h_hi, h_lo, T)
            outputs_v(peer + HALF - 1, 2, 0, NK - 2)
            outputs_v(peer + HALF - 1, 3, 1, NK - 1, last=True)

            pe.wait_ge(y_act, (l + 1) * TT)
            pe.wait_ge(y_dve, (l + 1) * TT)
            for kk in range(KT):
                if kk >= 2:
                    pe.wait_ge(x_updated, l * KT + kk)
                for t in range(TT):
                    last = transpose(col(bank[kk % 2], t, P), y_nat[:, t * D + kk * P:t * D + (kk + 1) * P])
                last.then_inc(yt_ready, 1)
        norm_sums(2 * DEPTH + 1)

    @block.scalar
    def _(act):
        copy = lambda out, in_: nc.scalar.activation(out, in_, ACT.Copy)

        def group(l, local, epilogue=None, after=None):
            for s in range(SLOTS):
                split_panel_hi(*ahead(l * GROUPS + local, s))
                if epilogue:
                    epilogue(s)
            if after:
                after()

        def product(g, s):
            act.wait_ge(panel_used[s % 2], after_use(g, s))
            return bank[s][:, 0:T]

        def norm(n):
            nc.scalar.activation(sq[:, :], x[:, :], ACT.Square).then_inc(squares, 1)
            act.wait_ge(mean_sq, n)
            nc.scalar.activation(ms[:, :], ms[:, :], ACT.Sqrt).then_inc(root, 1)

        def split_input(l, half):
            for kk in range(KT):
                act.wait_ge(hf_ready, l * 16 + half * 8 + kk + 1)
                copy(col(h_hi, kk), col(hf, kk)).then_inc(hhi_ready, 1)

        act.sem_inc(sc_ready, 4)
        act.sem_inc(gate_copied, 2)
        act.sem_inc(route_done, 1)
        act.sem_inc(ahi_ready, 2)
        act.wait_ge(consts_loaded, CONSTS * 16)
        nc.scalar.activation(c_t[:, :], c_t[:, :], ACT.Silu).then_inc(c_ready, 1)
        act.wait_ge(c_ready, 1)
        copy(c_hi[:, :], c_t[:, :]).then_inc(c_ready, 1)
        with act.Fori(0, DEPTH) as l:
            act.wait_ge(x_updated, l * KT + 1)
            for dst, src in ((vec, vecs[l, :, :]), (kc, k_cache[l, :, :]), (vc, v_cache[l, :, :]),
                             (dft, dft_in)):
                act.dma_start(dst[:, :], src).then_inc(layer_loaded, 16)
            for h in range(2):
                act.dma_start(col(bias, h, 2 * TS), bias_in[l * HEADS + h, :, :]).then_inc(bias_loaded[h], 16)
            split_panel_hi(l * GROUPS, 0)
            split_panel_hi(l * GROUPS, 1)
            norm(2 * l + 1)
            with act.Fori(0, COUNT["mod"]) as i:
                group(l, i + FIRST["mod"])
            split_input(l, 0)

            with act.Fori(0, COUNT["ccx"]) as i:
                local = i + FIRST["ccx"]

                def store_cc(s):
                    if s % 2 == 0:
                        out = product(l * GROUPS + local, s)
                        act.wait_ge(bank_free[s + 1], l * PROJ + local + 1)
                        copy(col(cc_s, s // 2), out).then_inc(bank_free[s], 1)
                group(l, local, store_cc)

            with act.Fori(0, COUNT["cb"]) as i:
                local = i + FIRST["cb"]

                def split_conv(s):
                    act.wait_ge(bank_free[s], l * PROJ + local + 2)
                    copy(u_hi[:, bass.ds((i * SLOTS + s) * T, T)], col(cb_s, s % 2)).then_inc(uhi_ready, 1)
                group(l, local, split_conv)

            with act.Fori(0, COUNT["qkvf"]) as i:
                local = i + FIRST["qkvf"]

                def store(s):
                    if s % 2 == 0:
                        out = product(l * GROUPS + local, s)
                        copy(qkvf[:, bass.ds((i * SLOTS + s) * T, T)], out).then_inc(bank_free[s], 1)
                group(l, local, store)

            for first, turns, dst in ((0, 4, gate01), (4, 2, gate2)):
                with act.Fori(0, turns) as i:
                    local = i + FIRST["gates"] + first

                    def store_gate(s):
                        out = product(l * GROUPS + local, s)
                        nc.scalar.activation(dst[:, bass.ds((i * SLOTS + s) * T, T)], out,
                                             ACT.Sigmoid).then_inc(bank_free[s], 1)
                    group(l, local, store_gate)

            for s in (1, 3):
                act.wait_ge(bank_free[s], l * PROJ + FIRST["gates"] + 1)
            wait_stored(act, l, "gates")
            act.dma_start(new_k[l, :, :, :], k.rearrange("p (h t) -> p h t", h=HEADS)[:, :, 0:TP]
                          ).then_inc(kv_out, 16)
            for h in range(0, HEADS, 2):
                act.wait_ge(vt_ready, l * HEADS + h + 1)
                copy(col(v, h), bank[4 + h % 4][:, 0:T]).then_inc(vt_act, 1)
            act.wait_ge(vt_act, l * 4 + 4)
            act.wait_ge(vt_dve, l * 4 + 4)
            act.dma_start(new_v[l, :, :, :], v.rearrange("p (h t) -> p h t", h=HEADS)[:, :, 0:DH]
                          ).then_inc(kv_out, 16)

            def exps(h):
                pr, sm = col(prob, h % 2, SCORES), col(softm, h % 2, 16)
                act.wait_ge(max_ready, l * HEADS + h + 1)
                for r, (beg, end) in enumerate(((0, TP), (TP, TP + KEYS), (TP + KEYS, SCORES))):
                    last = nc.scalar.activation(pr[:, beg:end], pr[:, beg:end], ACT.Exp, bias=sm[:, r:r + 1],
                                                scale=1.0, accum_out=sm[:, 4 + r:5 + r])
                last.then_inc(exp_ready, 1)

            exps(0)
            for h in range(HEADS):
                if h + 1 < HEADS:
                    exps(h + 1)
                if h + 2 < HEADS:
                    act.wait_ge(s_read, l * HEADS + h + 1)
                    act.dma_start(col(bias, h % 2, 2 * TS), bias_in[l * HEADS + h + 2, :, :]
                                  ).then_inc(bias_loaded[h % 2], 16)
                split_panel_hi(*ahead(l * GROUPS + FIRST["conv_out"] + h // SLOTS, h % SLOTS))
                act.wait_ge(pt_ready, l * HEADS + h + 1)
                if h >= 2:
                    act.wait_ge(o_ready, l * HEADS + h - 1)
                copy(col(prob_t, h % 2, SCORES)[:, 0:512], bank[6][:, :]).then_inc(pt_act, 1)
                act.wait_ge(o_ready, l * HEADS + h + 1)
                copy(col(h_hi, h), bank[6][:, 0:T]).then_inc(o_hi, 1)

            act.wait_ge(kv_out, (l + 1) * 32)

            def store_channels(g):
                for u in range(g * TT, (g + 1) * TT):
                    if u % 2 == 0:
                        act.wait_ge(y1_ready, l * 12 + u + 1)
                        if g >= 2:
                            act.wait_ge(y2_ready, l * 8 + 2 * (g - 1))
                        copy(col(col(fy, g % 2, TT * 512), u % TT, 512), bank[4][:, :]).then_inc(y1_act, 1)

            def split_tokens(g):
                for u in (2 * g, 2 * g + 1):
                    act.wait_ge(y2_ready, l * 8 + u + 1)
                    copy(col(f_hi, u), bank[6 + u % 2][:, 0:T]).then_inc(y2_hi, 1)

            store_channels(0)
            for g in range(1, FG):
                store_channels(g)
                split_tokens(g - 1)
            split_tokens(FG - 1)

            with act.Fori(0, COUNT["attn_out"]) as i:
                group(l, i + FIRST["attn_out"])
            with act.Fori(0, COUNT["four_out"]) as i:
                def split_merged(s):
                    act.wait_ge(merged, l * KT + i * SLOTS + s + 1)
                    n = bass.ds((i * SLOTS + s) * T, T)
                    copy(u_hi[:, n], gate01[:, n]).then_inc(mhi_ready, 1)
                group(l, i + FIRST["four_out"], split_merged)
            act.dma_start(subk[:, :], sub_keys[l, :, :]).then_inc(sub_loaded, 16)
            with act.Fori(0, COUNT["o"]) as i:
                group(l, i + FIRST["o"])

            wait_stored(act, l, "pq")
            norm(2 * l + 2)
            split_input(l, 1)

            with act.Fori(0, COUNT["pq"]) as i:
                local = i + FIRST["pq"]

                def store_scores(s):
                    n = (l * COUNT["pq"] + i) * SLOTS + s
                    act.wait_ge(keys_done, n + 1 + 4)
                    act.wait_ge(sc_used, n + 1)
                    copy(col(sc, s), bank[4 + s][:, 0:T]).then_inc(sc_ready, 1)

                def store_query(s):
                    out = product(l * GROUPS + local, s)
                    act.wait_ge(keys_done, (l * COUNT["pq"] + i) * SLOTS + s + 1)
                    copy(col(pq, s), out).then_inc(bank_free[s], 1)
                    if s:
                        store_scores(s - 1)
                group(l, local, store_query, lambda: store_scores(SLOTS - 1))

            with act.Fori(0, TT) as t:
                act.wait_ge(top_shifted, l * TT + t + 1)
                nc.scalar.activation(best[:, :], best[:, :], ACT.Exp).then_inc(top_exp, 1)
                act.wait_ge(route_tr, l * TT + t + 2)
                copy(route_t[:, :].rearrange("p (j t) -> p j t", j=3)[:, :, bass.ds(t * P, P)],
                     bank[4][:, 0:3 * P].rearrange("p (j t) -> p j t", j=3)).then_inc(route_done, 1)

            def store_gates(half):
                with act.Fori(0, NB // 2) as i:
                    for b in range(2):
                        act.wait_ge(gate_mm, (l * 2 + half) * NB + i * 2 + b + 1 + 2)
                        copy(gates[:, :].rearrange("p (j t) -> p j t", j=HALF)[:, :, bass.ds((i * 2 + b) * BATCH, BATCH)],
                             bank[b][:, :].rearrange("p (t j) -> p j t", j=HALF)).then_inc(gate_copied, 1)

            peer = l * GROUPS + FIRST["peer"]

            def gelu(i, b, g, s):
                j = l * NK + 2 * i + b
                act.wait_ge(panel_used[s % 2], after_use(g, s))
                act.wait_ge(act_ready, j + 1)
                nc.scalar.activation(col(gel, b), bank[b][:, 0:T], ACT.Gelu).then_inc(gelu_ready, 1)

            def split_act(i, b, first=False):
                j = l * NK + 2 * i + b
                act.wait_ge(act_ready, j + 1 + 2)
                if not first:
                    act.wait_ge(panel_used[0], after_use(*((peer + i - 1, 2) if b == 0 else (peer + i, 0))))
                copy(col(a_hi, b), col(act_f, b)).then_inc(ahi_ready, 1)

            def pair(i, first=False, last=False):
                g = peer + i
                gelu(i, 0, *((peer, 0) if first else (g - 1, 3)))
                split_act(i, 0, first)
                split_panel_hi(g, 2)
                split_panel_hi(g, 3)
                gelu(i, 1, g, 1)
                split_act(i, 1, first)
                if not last:
                    split_panel_hi(g + 1, 0)
                    split_panel_hi(g + 1, 1)

            store_gates(0)
            pair(0, first=True)
            with act.Fori(1, HALF // 2) as i:
                pair(i)
            gelu(HALF // 2, 0, peer + HALF // 2 - 1, 3)
            act.wait_ge(act_ready, l * NK + HALF + 2)
            store_gates(1)
            g = peer + HALF // 2
            split_act(HALF // 2, 0)
            split_panel_hi(g, 2)
            split_panel_hi(g, 3)
            gelu(HALF // 2, 1, g, 1)
            split_act(HALF // 2, 1)
            split_panel_hi(g + 1, 0)
            split_panel_hi(g + 1, 1)
            with act.Fori(HALF // 2 + 1, HALF - 1) as i:
                pair(i)
            pair(HALF - 1, last=True)

            act.wait_ge(panel_used[1], after_use(peer + HALF - 1, 3))
            for t in range(TT):
                copy(col(y_nat, 2 * t, 512), bank[2 + 2 * t][:, :]).then_inc(y_act, 1)
        act.wait_ge(x_updated, DEPTH * KT + 1)
        norm(2 * DEPTH + 1)

    @block.gpsimd
    def _(pool):
        def panels_lo(l, local):
            g = l * GROUPS + local
            for s in (0, 2):
                split_panel_lo(pool, *ahead(g, s))

        def lo(dst, src, hi):
            return pool.tensor_tensor(dst, src, hi.bitcast(F32), ALU.subtract)

        pool.memset(ones[:, :], 1.0).then_inc(ones_ready, 1)
        pool.sem_inc(ulo_ready, 2)
        with pool.Fori(0, DEPTH) as l:
            split_panel_lo(pool, l * GROUPS, 0)
            with pool.Fori(0, FIRST["cb"]) as i:
                panels_lo(l, i)
            with pool.Fori(0, COUNT["cb"]) as i:
                for s in range(SLOTS):
                    if s % 2 == 0:
                        split_panel_lo(pool, *ahead(l * GROUPS + FIRST["cb"] + i, s))
                    n = bass.ds((i * SLOTS + s) * T, T)
                    pool.wait_ge(uhi_ready, l * KT + i * SLOTS + s + 1)
                    lo(u_lo[:, n], col(cb_s, s % 2), u_hi[:, n]).then_inc(ulo_ready, 1)
            with pool.Fori(FIRST["qkvf"], FIRST["conv_out"]) as i:
                panels_lo(l, i)

            def add_mask(h):
                pool.wait_ge(bias_loaded[h % 2], (l * 4 + h // 2 + 1) * 16)
                bt = col(bias, h % 2, 2 * TS).rearrange("p (r c) -> p r c", c=GRID_W)
                pool.tensor_tensor(bt, bt, mask[:, :].unsqueeze(1).broadcast_to([P, 8, GRID_W]),
                                   ALU.add).then_inc(bias_masked, 1)

            add_mask(0)
            add_mask(1)
            for h in range(HEADS):
                if h % 2 == 0:
                    split_panel_lo(pool, *ahead(l * GROUPS + FIRST["conv_out"] + h // SLOTS, h % SLOTS))
                if h + 2 < HEADS:
                    add_mask(h + 2)
            with pool.Fori(FIRST["attn_out"], FIRST["four_out"]) as i:
                panels_lo(l, i)
            with pool.Fori(0, COUNT["four_out"]) as i:
                for s in range(SLOTS):
                    if s % 2 == 0:
                        split_panel_lo(pool, *ahead(l * GROUPS + FIRST["four_out"] + i, s))
                    n = bass.ds((i * SLOTS + s) * T, T)
                    pool.wait_ge(mhi_ready, l * KT + i * SLOTS + s + 1)
                    lo(u_lo[:, n], gate01[:, n], u_hi[:, n]).then_inc(mlo_ready, 1)
            with pool.Fori(FIRST["o"], GROUPS - 1) as i:
                panels_lo(l, i)
            split_panel_lo(pool, l * GROUPS + GROUPS - 1, 2)

    @block.vector
    def _(dve):
        V = nc.vector
        order = Order()

        def group(l, local, epilogue=None):
            for s in range(SLOTS):
                if s % 2:
                    split_panel_lo(dve, *ahead(l * GROUPS + local, s))
                if epilogue:
                    epilogue(s)

        def product(l, local, s):
            dve.wait_ge(panel_used[s % 2], after_use(l * GROUPS + local, s))
            return bank[s][:, 0:T]

        def norm(n):
            dve.wait_ge(sums, n)
            V.tensor_scalar(ms[:, :], bank[4][:, 0:T], 1.0 / D, EPS, ALU.mult, ALU.add).then_inc(mean_sq, 1)
            dve.wait_ge(root, n)
            order.step(V.reciprocal(rstd[:, :], ms[:, :]))
            order.step(V.tensor_tensor(hf[:, :].rearrange("p (k t) -> p k t", k=KT),
                                       x[:, :].rearrange("p (k t) -> p k t", k=KT),
                                       rstd[:, :].unsqueeze(1).broadcast_to([P, KT, T]), ALU.mult))

        def modulate(l, half):
            shift = SHIFT2 if half else SHIFT1
            for kk in range(KT):
                for m, (beg, end) in enumerate(STREAMS):
                    c = (shift * KT + kk) * 2 + m
                    gc = (half * KT + kk) * 2 + m
                    last = V.tensor_scalar(col(hf, kk)[:, beg:end], col(hf, kk)[:, beg:end], gain[:, gc:gc + 1],
                                           modv[:, c:c + 1], ALU.mult, ALU.add)
                last.then_inc(hf_ready, 1)
            for kk in range(KT):
                dve.wait_ge(hhi_ready, l * 16 + half * 8 + kk + 1)
                V.tensor_tensor(col(h_lo, kk), col(hf, kk), col(h_hi, kk).bitcast(F32),
                                ALU.subtract).then_inc(hlo_ready, 1)

        for s in range(SLOTS):
            dve.sem_inc(bank_free[s], 1)
        dve.sem_inc(sc_used, 4)
        dve.sem_inc(act_ready, 2)
        dve.sem_inc(x_updated, 1)
        dve.wait_ge(consts_loaded, CONSTS * 16)
        dve.wait_ge(c_ready, 2)
        V.tensor_tensor(c_lo[:, :], c_t[:, :], c_hi[:, :].bitcast(F32), ALU.subtract).then_inc(c_ready, 1)

        LAYER_STEPS = 413
        with dve.Fori(0, DEPTH) as l:
            layer = order.enter(l, 0, LAYER_STEPS)
            split_panel_lo(dve, l * GROUPS, 1)
            norm(2 * l + 1)
            dve.wait_ge(layer_loaded, (l + 1) * LOADS * 16)
            carry(dve)
            with dve.Fori(0, COUNT["mod"]) as i:
                def add_bias(s):
                    n = i * SLOTS + s
                    dve.wait_ge(panel_used[s % 2], after_use(l * GROUPS + i + FIRST["mod"], s))
                    V.tensor_scalar(modv[:, bass.ds(n * 2, 2)], bank[s][:, 0:2], vec[:, bass.ds(n, 1)], None,
                                    ALU.add).then_inc(bank_free[s], 1)
                group(l, i + FIRST["mod"], add_bias)
            wait_stored(dve, l, "ccx")
            for half, (scale, g0) in enumerate(((SCALE1, G_MIX), (SCALE2, G_FFN))):
                order.step(V.scalar_tensor_tensor(
                    gain[:, half * 16:half * 16 + 16].rearrange("p (k m) -> p k m", m=2),
                    modv[:, scale * 16:scale * 16 + 16].rearrange("p (k m) -> p k m", m=2), 1.0,
                    vec[:, g0:g0 + KT].unsqueeze(2).broadcast_to([P, KT, 2]), ALU.add, ALU.mult))
            modulate(l, 0)

            order.step(V.memset(ccx[:, :], 0.0))
            carry(dve)
            with dve.Fori(0, COUNT["ccx"]) as i:
                inner = order.enter(i, 0, 6)
                local = i + FIRST["ccx"]

                def convolve(s):
                    if s % 2 == 0:
                        return
                    cx, b = product(l, local, s), s // 2
                    dve.wait_ge(bank_free[s - 1], l * PROJ + local + 2)
                    pad = col(ccx, b, PAD)
                    for (beg, end), (p0, p1) in zip(STREAMS, SEG):
                        last = V.tensor_tensor(pad[:, p0:p1], col(cc_s, b)[:, beg:end], cx[:, beg:end], ALU.mult)
                    last.then_inc(bank_free[s], 1)
                    dve.wait_ge(bank_free[s], l * PROJ + local + 2)
                    n = i * 2 + b
                    u = conv[:, bass.ds(n * PAD + 1, PAD - 2)]
                    taps = [vec[:, bass.ds(n + (CONV_W + tap * KT), 1)] for tap in range(3)]
                    order.step(V.tensor_scalar(u, pad[:, 0:PAD - 2], taps[0], None, ALU.mult))
                    for tap in (1, 2):
                        order.step(V.scalar_tensor_tensor(u, pad[:, tap:tap + PAD - 2], taps[tap], u,
                                                          ALU.mult, ALU.add))
                group(l, local, convolve)
                order.leave(inner, COUNT["ccx"], 6)

            with dve.Fori(0, COUNT["cb"]) as i:
                local = i + FIRST["cb"]

                def times_cb(s):
                    cb = product(l, local, s)
                    dve.wait_ge(ulo_ready, l * KT + i * SLOTS + s + 1)
                    for (beg, end), (p0, p1) in zip(STREAMS, SEG):
                        last = V.tensor_tensor(col(cb_s, s % 2)[:, beg:end],
                                               conv[:, bass.ds((i * SLOTS + s) * PAD + p0, p1 - p0)],
                                               cb[:, beg:end], ALU.mult)
                    last.then_inc(bank_free[s], 1)
                group(l, local, times_cb)

            with dve.Fori(0, COUNT["qkvf"]) as i:
                local = i + FIRST["qkvf"]

                def store(s):
                    if s % 2:
                        V.tensor_copy(qkvf[:, bass.ds((i * SLOTS + s) * T, T)],
                                      product(l, local, s)).then_inc(bank_free[s], 1)
                group(l, local, store)
            with dve.Fori(0, COUNT["gates"]) as i:
                group(l, i + FIRST["gates"])

            for h in range(1, HEADS, 2):
                dve.wait_ge(vt_ready, l * HEADS + h + 1)
                V.tensor_copy(col(v, h), bank[4 + h % 4][:, 0:T]).then_inc(vt_dve, 1)

            def read_scores(h):
                pr, sm, bt = col(prob, h % 2, SCORES), col(softm, h % 2, 16), col(bias, h % 2, 2 * TS)
                dve.wait_ge(s_ready, l * HEADS + h + 1)
                dve.wait_ge(bias_masked, l * HEADS + h + 1)
                if h >= 2:
                    dve.wait_ge(pt_ready, l * HEADS + h - 1)
                V.tensor_scalar(pr[:, 0:TP], bank[4][:, 0:TP], SCALE, None, ALU.mult)
                for j in range(2):
                    c0, p0 = (TP if j == 0 else 0), TP + j * KEYS
                    V.scalar_tensor_tensor(pr[:, p0:p0 + TS], bank[4 + j][:, c0:c0 + TS], SCALE,
                                           col(bt, j, TS), ALU.mult, ALU.add)
                    last = V.tensor_scalar(pr[:, p0 + TS:p0 + KEYS], bank[4 + j][:, c0 + TS:c0 + KEYS], SCALE,
                                           None, ALU.mult)
                last.then_inc(s_read, 1)
                dve.wait_ge(s_read, l * HEADS + h + 1)
                V.tensor_reduce(sm[:, 0:1], pr[:, 0:TP], AX.X, ALU.max, negate=True)
                V.tensor_reduce(sm[:, 1:3], pr[:, TP:SCORES].rearrange("p (j k) -> p j k", j=2), AX.X, ALU.max,
                                negate=True).then_inc(max_ready, 1)

            read_scores(0)
            for h in range(HEADS):
                pr, sm = col(prob, h % 2, SCORES), col(softm, h % 2, 16)
                dve.wait_ge(exp_ready, l * HEADS + h + 1)
                order.step(V.reciprocal(sm[:, 8:11], sm[:, 4:7]))
                for r, (beg, end) in enumerate(((0, TP), (TP, TP + KEYS), (TP + KEYS, SCORES))):
                    last = V.tensor_scalar(pr[:, beg:end], pr[:, beg:end], sm[:, 8 + r:9 + r], None, ALU.mult)
                last.then_inc(prob_ready, 1)
                if h + 1 < HEADS:
                    read_scores(h + 1)
                local, s = FIRST["conv_out"] + h // SLOTS, h % SLOTS
                if s % 2:
                    split_panel_lo(dve, *ahead(l * GROUPS + local, s))
                V.tensor_tensor(col(gate0, h), col(gate0, h), product(l, local, s),
                                ALU.mult).then_inc(bank_free[s], 1)
                dve.wait_ge(pt_ready, l * HEADS + h + 1)
                if h >= 2:
                    dve.wait_ge(o_ready, l * HEADS + h - 1)
                V.tensor_copy(col(prob_t, h % 2, SCORES)[:, 512:SCORES], bank[7][:, 0:SCORES - 512]
                              ).then_inc(pt_dve, 1)
                dve.wait_ge(o_hi, l * HEADS + h + 1)
                V.tensor_tensor(col(h_lo, h), bank[6][:, 0:T], col(h_hi, h).bitcast(F32),
                                ALU.subtract).then_inc(o_lo, 1)

            dve.wait_ge(kv_out, (l + 1) * 32)

            def store_channels(g):
                for u in range(g * TT, (g + 1) * TT):
                    if u % 2:
                        dve.wait_ge(y1_ready, l * 12 + u + 1)
                        if g >= 2:
                            dve.wait_ge(y2_ready, l * 8 + 2 * (g - 1))
                        V.tensor_copy(col(col(fy, g % 2, TT * 512), u % TT, 512), bank[5][:, :]).then_inc(y1_dve, 1)

            def split_tokens(g):
                for u in (2 * g, 2 * g + 1):
                    dve.wait_ge(y2_hi, l * 8 + u + 1)
                    V.tensor_tensor(col(f_lo, u), bank[6 + u % 2][:, 0:T], col(f_hi, u).bitcast(F32),
                                    ALU.subtract).then_inc(y2_lo, 1)

            store_channels(0)
            for g in range(1, FG):
                store_channels(g)
                split_tokens(g - 1)
            split_tokens(FG - 1)

            for name, gate, done in (("attn_out", gate1, None), ("four_out", gate2, merged)):
                with dve.Fori(0, COUNT[name]) as i:
                    def add_branch(s):
                        n = bass.ds((i * SLOTS + s) * T, T)
                        local = i + FIRST[name]
                        V.tensor_tensor(col(branch, s), gate[:, n], product(l, local, s),
                                        ALU.mult).then_inc(bank_free[s], 1)
                        dve.wait_ge(bank_free[s], l * PROJ + local + 2)
                        last = V.tensor_tensor(gate01[:, n], gate01[:, n], col(branch, s), ALU.add)
                        if done is not None:
                            last.then_inc(done, 1)
                    group(l, i + FIRST[name], add_branch)

            def residual(xs, in_, n, which):
                for m, (beg, end) in enumerate(STREAMS):
                    g = modv[:, bass.ds(n * 2 + (which * 16 + m), 1)]
                    last = V.scalar_tensor_tensor(xs[m], in_[:, beg:end], g, xs[m], ALU.mult, ALU.add)
                return last

            with dve.Fori(0, COUNT["o"]) as i:
                def add_mixer(s):
                    n = i * SLOTS + s
                    xs = [x[:, bass.ds(n * T + beg, end - beg)] for beg, end in STREAMS]
                    residual(xs, product(l, i + FIRST["o"], s), n, GATE1).then_inc(bank_free[s], 1)
                group(l, i + FIRST["o"], add_mixer)

            norm(2 * l + 2)
            modulate(l, 1)

            with dve.Fori(0, COUNT["pq"]) as i:
                steps = SLOTS * TT * 3 + 2
                inner = order.enter(i, 0, steps)

                def rank(s):
                    n = (l * COUNT["pq"] + i) * SLOTS + s
                    dve.wait_ge(sc_ready, n + 1 + 4)
                    carry(dve)
                    vs = [col(val, s * TT + t, TOPK) for t in range(TT)]
                    ix = [col(idx, s * TT + t, TOPK) for t in range(TT)]
                    ss = [col(col(sc, s), t, NK) for t in range(TT)]
                    s2 = [col(sc2, t, NK) for t in range(TT)]
                    for t in range(TT):
                        order.step(V.max(vs[t][:, 0:8], ss[t]), wait=(t == TT - 1), hold=True)
                    for t in range(TT):
                        V.max_index(ix[t][:, 0:8], vs[t][:, 0:8], ss[t])
                        order.step(V.match_replace(s2[t], vs[t][:, 0:8], ss[t], LOWEST), wait=(t == TT - 1), hold=True)
                    for t in range(TT):
                        order.step(V.max(vs[t][:, 8:16], s2[t]), wait=(t == TT - 1), hold=True)
                    for t in range(TT):
                        last = V.max_index(ix[t][:, 8:16], vs[t][:, 8:16], s2[t])
                    last.then_inc(sc_used, 1)
                group(l, i + FIRST["pq"], rank)
                dve.wait_ge(sc_used, (l * COUNT["pq"] + i + 1) * SLOTS + 4)
                for dst, src in ((vals, val), (idxs, idx)):
                    out = dst[:, :].rearrange("p (t h r) -> p h t r", t=TT, r=TOPK)[:, bass.ds(i * SLOTS, SLOTS), :, :]
                    order.step(V.tensor_copy(out, src[:, :].rearrange("p (h t r) -> p h t r", h=SLOTS, r=TOPK)))
                order.leave(inner, COUNT["pq"], steps)

            with dve.Fori(0, TT) as t:
                steps = 42
                inner = order.enter(t, 0, steps)
                width = 2 * PH * TOPK
                vt = vals[:, bass.ds(t * width, width)].rearrange("p (h c r) -> p h c r", h=PH, c=2)
                it = idxs[:, bass.ds(t * width, width)].rearrange("p (h c r) -> p h c r", h=PH, c=2)
                grid = [P, PH, TOPK, TOPK]
                order.step(V.tensor_tensor(cand[:, :].rearrange("p (h a b) -> p h a b", h=PH, a=TOPK),
                                           vt[:, :, 0, :].unsqueeze(3).broadcast_to(grid),
                                           vt[:, :, 1, :].unsqueeze(2).broadcast_to(grid), ALU.add), hold=True)
                n2 = TOPK * TOPK
                for r in range(2):
                    src = cand if r == 0 else cand2
                    for h in range(PH):
                        order.step(V.max(col(best, h, TOPK)[:, 8 * r:8 * r + 8], col(src, h, n2)), wait=(h == PH - 1), hold=True)
                    for h in range(PH):
                        b8, c = col(best, h, TOPK)[:, 8 * r:8 * r + 8], col(src, h, n2)
                        ins = V.max_index(col(pos, h, TOPK)[:, 8 * r:8 * r + 8], b8, c)
                        if r == 0:
                            ins = V.match_replace(col(cand2, h, n2), b8, c, LOWEST)
                        order.step(ins, wait=(h == PH - 1), hold=True)
                b3 = best[:, :].rearrange("p (h r) -> p h r", h=PH)
                order.step(V.tensor_copy(gsum[:, 0:PH], b3[:, :, 0]))
                V.tensor_tensor(b3, b3, gsum[:, 0:PH].unsqueeze(2).broadcast_to([P, PH, TOPK]),
                                ALU.subtract).then_inc(top_shifted, 1)
                V.tensor_scalar(pos_ab[:, 0:HK], pos[:, :], 4, None, ALU.logical_shift_right)
                order.step(V.tensor_scalar(pos_ab[:, HK:2 * HK], pos[:, :], 15, None, ALU.bitwise_and))
                order.step(V.tensor_copy(pos_f[:, :], pos_ab[:, :]))
                eq3 = [col(eq, c, HK * TOPK).rearrange("p (n j) -> p n j", j=TOPK) for c in range(2)]
                for c in range(2):
                    order.step(V.tensor_tensor(eq3[c], col(pos_f, c, HK).unsqueeze(2).broadcast_to([P, HK, TOPK]),
                                               iota[:, 0:TOPK].unsqueeze(1).broadcast_to([P, HK, TOPK]),
                                               ALU.is_equal), wait=(c == 1))
                for c in range(2):
                    e4 = col(eq, c, HK * TOPK).rearrange("p (h k j) -> p h k j", h=PH, k=TOPK)
                    order.step(V.tensor_tensor(e4, e4, it[:, :, c, :].unsqueeze(2).broadcast_to(grid), ALU.mult),
                               wait=(c == 1))
                dve.wait_ge(route_tr, l * TT + t + 1)
                for c in range(2):
                    V.tensor_reduce(col(route, c, HK), eq3[c], AX.X, ALU.add)
                dve.wait_ge(top_exp, l * TT + t + 1)
                order.step(V.tensor_reduce(gsum[:, 0:PH], b3, AX.X, ALU.add))
                order.step(V.reciprocal(gsum[:, PH:2 * PH], gsum[:, 0:PH]))
                V.tensor_tensor(col(route, 2, HK).rearrange("p (h r) -> p h r", h=PH), b3,
                                gsum[:, PH:2 * PH].unsqueeze(2).broadcast_to([P, PH, TOPK]),
                                ALU.mult).then_inc(route_ready, 1)
                dve.wait_ge(route_ready, l * TT + t + 1)
                order.leave(inner, TT, steps)
            dve.wait_ge(route_done, (l + 1) * TT + 1)

            def one_hots(half):
                carry(dve)
                with dve.Fori(0, NB // 2) as i:
                    inner = order.enter(i, 0, 2)
                    for b in range(2):
                        dve.wait_ge(gate_mm, (l * 2 + half) * NB + i * 2 + b + 1)
                        cb = col(cols, b, 3 * BATCH)
                        src = route_t[:, :].rearrange("p (j t) -> p j t", j=3)[:, :, bass.ds((i * 2 + b) * BATCH, BATCH)]
                        order.step(V.tensor_copy(cb.rearrange("p (j t) -> p j t", j=3), src))
                        for t in range(BATCH):
                            i1, i2, gt = (cb[:, j * BATCH + t:j * BATCH + t + 1] for j in range(3))
                            V.tensor_scalar(col(hot2, b * BATCH + t, P), iota[:, :], i2, None, ALU.is_equal)
                            last = V.tensor_scalar(col(hot1, b * BATCH + t, HALF), col(iota, half, HALF), i1, gt,
                                                   ALU.is_equal, ALU.mult)
                        last.then_inc(hot_ready, 1)
                    order.leave(inner, NB // 2, 2)

            peer = l * GROUPS + FIRST["peer"]

            def gated(i, b, half, first=False):
                j = l * NK + 2 * i + b
                dve.wait_ge(gelu_ready, j + 1)
                dve.wait_ge(ahi_ready, j + 1)
                at = (2 * i + (b - half * HALF)) * T
                V.tensor_tensor(col(act_f, b), col(gel, b), gates[:, bass.ds(at, T)],
                                ALU.mult).then_inc(act_ready, 1)
                dve.wait_ge(ahi_ready, j + 1 + 2)
                V.tensor_tensor(col(a_lo, b), col(act_f, b), col(a_hi, b).bitcast(F32),
                                ALU.subtract).then_inc(alo_ready, 1)

            def pair(i, half, last=False):
                gated(i, 0, half)
                split_panel_lo(dve, peer + i, 3)
                gated(i, 1, half)
                if not last:
                    split_panel_lo(dve, peer + i + 1, 1)

            for half in range(2):
                one_hots(half)
                dve.wait_ge(gate_copied, (l * 2 + half + 1) * NB + 2)
                carry(dve)
                with dve.Fori(half * HALF // 2, (half + 1) * HALF // 2 - half) as i:
                    pair(i, half)
            pair(HALF - 1, 1, last=True)

            dve.wait_ge(panel_used[1], after_use(peer + HALF - 1, 3))
            for t in range(TT):
                V.tensor_copy(col(y_nat, 2 * t + 1, 512), bank[3 + 2 * t][:, :]).then_inc(y_dve, 1)
            for kk in range(KT):
                dve.wait_ge(yt_ready, l * KT + kk + 1)
                xs = [col(x, kk)[:, beg:end] for beg, end in STREAMS]
                for m, (beg, end) in enumerate(STREAMS):
                    c = (GATE2 * KT + kk) * 2 + m
                    last = V.scalar_tensor_tensor(xs[m], bank[kk % 2][:, beg:end], modv[:, c:c + 1], xs[m],
                                                  ALU.mult, ALU.add)
                last.then_inc(x_updated, 1)
            order.leave(layer, DEPTH, LAYER_STEPS)

        norm(2 * DEPTH + 1)
        V.tensor_tensor(hf[:, :].rearrange("p (k t) -> p k t", k=KT), hf[:, :].rearrange("p (k t) -> p k t", k=KT),
                        gfin[:, :].unsqueeze(2).broadcast_to([P, KT, T]), ALU.mult).then_inc(out_ready, 1)

    block_cm.__exit__(None, None, None)


def kernel(**inputs):
    import numpy as np
    import concourse.bacc as bacc
    from concourse import mybir as _mybir
    from concourse.bass_utils import run_bass_kernel_spmd

    a = {name: np.asarray(value) for name, value in inputs.items()}

    def features_first(t):
        n = t.shape[0]
        return t.reshape(n, KT, P).transpose(2, 1, 0).reshape(P, KT * n)

    def columns(w):
        n = w.shape[1]
        return w.reshape(KT, P, n // P, P).transpose(2, 1, 0, 3).reshape(n // P, P, D)

    panels = np.empty((DEPTH * GROUPS * SLOTS, P, D), np.float32)
    for l in range(DEPTH):
        w_in = columns(a["w_in"][l]).reshape(10, KT, P, D)
        cb, cc, cx, q, k, v, f, g0, g1, g2 = w_in
        u = a["peer_u"][l].reshape(NK, P, KT, P).transpose(0, 3, 2, 1).reshape(NK, P, D)
        vv = a["peer_v"][l].reshape(NK, P, D)
        uv = np.empty((2 * NK, P, D), np.float32)
        uv[0] = u[0]
        uv[1:2 * NK - 2:2] = u[1:]
        uv[2:2 * NK - 1:2] = vv[:-1]
        uv[2 * NK - 1] = vv[NK - 1]
        parts = (columns(a["w_mod"][l]), np.stack([cc, cx], 1).reshape(2 * KT, P, D), cb,
                 np.concatenate([q, k, v, f]), np.concatenate([g0, g1, g2]), columns(a["w_conv_out"][l]),
                 columns(a["w_attn_out"][l]), columns(a["w_four_out"][l]), columns(a["w_o"][l]),
                 columns(a["w_pq"][l]), uv)
        at = l * GROUPS * SLOTS
        for part in parts:
            panels[at:at + len(part)] = part
            at += len(part)

    def per_feature(t):
        return t.reshape(-1, KT, P).transpose(2, 0, 1).reshape(P, -1)

    vecs = np.stack([np.concatenate([per_feature(a["b_mod"][l].reshape(N_MOD, D)), per_feature(a["g_mix"][l][None]),
                                     per_feature(a["g_ffn"][l][None]), per_feature(a["conv_w"][l])], 1)
                     for l in range(DEPTH)])
    rows = TS // GRID_W
    dr = np.arange(rows)[None, :] - np.arange(rows)[:, None] + 7
    dc = np.arange(GRID_W)[None, :] - np.arange(GRID_W)[:, None] + WIN - 1
    padded = np.zeros(a["rpb"].shape[:3] + (2 * WIN,), np.float32)
    padded[..., :2 * WIN - 1] = a["rpb"]
    dc = np.where((dc < 0) | (dc > 2 * WIN - 2), 2 * WIN - 1, dc)
    table = padded[:, :, dr[:, None, :, None], dc[None, :, None, :]]
    table = table.reshape(DEPTH * HEADS, 2, P, TS).transpose(0, 2, 1, 3).reshape(DEPTH * HEADS, P, 2 * TS)
    c = np.arange(GRID_W)
    c0 = np.clip(c - WIN // 2, 0, GRID_W - WIN)
    window = np.where((c[None, :] >= c0[:, None]) & (c[None, :] < c0[:, None] + WIN), 0.0, -1e30)
    window = np.concatenate([window, window]).astype(np.float32)

    def transform(n):
        angle = 2 * np.pi * (np.outer(np.arange(n), np.arange(n)) % n) / n
        return np.cos(angle) / np.sqrt(n), np.sin(angle) / np.sqrt(n)

    cd, sd = transform(FD)
    cp, s_p = transform(TP)
    cs, ss = transform(TS)
    two = lambda m, w: m.reshape(2, P, w).transpose(1, 0, 2).reshape(P, 2 * w)
    tables = np.concatenate([two(np.concatenate([cd, sd], 1), 512), cp, -s_p,
                             two(np.concatenate([cs, -ss], 1), 2 * TS)], 1).astype(np.float32)

    ins = {
        "panels": panels,
        "x_in": features_first(np.concatenate([a["x_prompt"][0], a["x_sample"][0]])),
        "c_in": features_first(np.stack([a["c_ctx"], a["c"][0]])),
        "vecs": vecs,
        "g_final": per_feature(a["g_final"][None]),
        "k_cache": a["cache_k"][0].transpose(0, 3, 2, 1).reshape(DEPTH, DH, HEADS * CTX),
        "v_cache": a["cache_v"][0].reshape(DEPTH, CTX, HEADS * DH),
        "bias_in": table,
        "mask_in": window,
        "dft_in": tables,
        "sub_keys": a["sub_keys"].transpose(0, 4, 1, 2, 3).reshape(DEPTH, P, 2 * PH * NK),
        "ident_in": np.eye(P, dtype=np.float32),
        "iota_in": np.tile(np.arange(P, dtype=np.float32), (P, 1)),
    }
    outs = {"y_out": (P, KT * T), "new_k": (DEPTH, DH, HEADS, TP), "new_v": (DEPTH, TP, HEADS, DH)}
    nc = bacc.Bacc("TRN2", target_bir_lowering=False, num_devices=1, dynamic_dma_scratch_size=1024)
    ins = {name: np.ascontiguousarray(value) for name, value in ins.items()}
    aps = {name: nc.dram_tensor(name, value.shape, _mybir.dt.float32, kind="ExternalInput").ap()
           for name, value in ins.items()}
    aps |= {name: nc.dram_tensor(name, shape, _mybir.dt.float32, kind="ExternalOutput").ap()
            for name, shape in outs.items()}
    build(nc, **aps)
    got = run_bass_kernel_spmd(nc, [ins], core_ids=[0]).results[0]
    y = got["y_out"].reshape(P, KT, T).transpose(2, 1, 0).reshape(T, D)
    new_k = got["new_k"].transpose(0, 3, 2, 1)[None]
    return y[None, :TP], y[None, TP:], new_k, got["new_v"][None]
```

```python
import concourse.bass as bass
import concourse.mybir as mybir

F32 = mybir.dt.float32
F32R = mybir.dt.float32r
BF16 = mybir.dt.bfloat16
U32 = mybir.dt.uint32
ALU = mybir.AluOpType
ACT = mybir.ActivationFunctionType
AX = mybir.AxisListType

DEPTH = 2
P = 128
D = 1024
KT = D // P
TP, TS = 128, 256
T = TP + TS
TT = T // P
STREAMS = ((0, TP), (TP, T))
HEADS = 8
DH = 128
CTX = 128
GRID_W = 64
WIN = 16
SCALE = DH ** -0.5
KEYS = TS + CTX
SCORES = TP + 2 * KEYS
PH = 8
NK = 128
TOPK = 16
HK = PH * TOPK
EPS = 1e-6
LOWEST = -3.0e38
N_MOD = 6
SHIFT1, SCALE1, GATE1, SHIFT2, SCALE2, GATE2 = range(N_MOD)
FG, FD = 4, 256

SLOTS = 4
OWN_G, NEXT_G = 4 * KT // SLOTS, 2 * KT // SLOTS
MOD_G = OWN_G + NEXT_G
_groups = (("ccx", 2 * KT), ("cb", KT), ("qkvf", 4 * KT), ("gates", 3 * KT),
           ("conv_out", KT), ("attn_out", KT), ("four_out", KT), ("o", KT), ("pq", 2 * PH),
           ("peer", 2 * NK))
FIRST, COUNT, _at = {}, {}, 0
for _name, _panels in _groups:
    FIRST[_name], COUNT[_name] = _at, _panels // SLOTS
    _at += _panels // SLOTS
GROUPS = _at
PROJ = FIRST["peer"]

CHUNKS = 4
CHUNK = NK // CHUNKS
PAIRS = CHUNK // 2
BATCH = 8
PER_PAIR = 3
NB = T // BATCH
LAST_PAIR = NK // 2 - 1
PARTS = 3
assert NB == PAIRS * PER_PAIR

B_MOD, G_MIX, G_FFN, CONV_W = 0, N_MOD * KT, N_MOD * KT + KT, N_MOD * KT + 2 * KT
VEC = CONV_W + 3 * KT
PAD = T + 4
SEG = ((1, 1 + TP), (3 + TP, 3 + T))
DFT_CH, DFT_P, DFT_S = 0, 2 * 512, 2 * 512 + 2 * TP
DFT = DFT_S + 2 * 2 * TS


def build(nc, panels, mod_panels, x_in, c_in, vecs, g_final, k_cache, v_cache, bias_in, mask_in, dft_in,
          sub_keys, ident_in, iota_in, y_out, new_k, new_v):
    base = 1152

    def place(name, where, cols, dt=F32):
        size = 2 if dt == BF16 else 4
        return nc.alloc_sbuf_tensor_at(name, [P, cols], dt, offset=where), where + size * cols

    raw, o = place("raw", base, SLOTS * D)
    split_hi, o = place("split_hi", o, 2 * D, F32R)
    split_lo, o = place("split_lo", o, 2 * D, F32R)
    h_hi, o = place("h_hi", o, KT * T, F32R)
    h_lo, o = place("h_lo", o, KT * T, F32R)
    x, o = place("x", o, KT * T)
    ident, o = place("ident", o, P)
    iota, o = place("iota", o, P)
    ones, o = place("ones", o, P)
    mask, o = place("mask", o, GRID_W)
    vec, o = place("vec", o, VEC)
    modv, o = place("modv", o, N_MOD * KT * 2)
    gain, o = place("gain", o, 2 * KT * 2)
    gfin, o = place("gfin", o, KT)
    softm, o = place("softm", o, 2 * 16)
    arena = o

    qkvf, o = place("qkvf", arena, 4 * KT * T)
    q, k, v, f = (qkvf[:, i * KT * T:(i + 1) * KT * T] for i in range(4))
    gate01, o = place("gate01", o, 2 * KT * T)
    gate0, gate1 = gate01[:, 0:KT * T], gate01[:, KT * T:2 * KT * T]
    gate2_at = o
    gate2, _ = place("gate2", o, KT * T)
    conv, o = place("conv", o, KT * PAD)
    u_hi, o = place("u_hi", o, KT * T, F32R)
    u_lo, o = place("u_lo", o, KT * T, F32R)
    bias, o = place("bias", o, 2 * 2 * TS)
    kc_at = o
    kc, o = place("kc", o, HEADS * CTX)
    vc, o = place("vc", o, HEADS * DH)
    prob_at = o
    prob, o = place("prob", o, 2 * SCORES)
    prob_t, o = place("prob_t", o, 2 * SCORES)
    dft, o = place("dft", o, DFT)
    silu_c, mixer_end = place("silu_c", o, 2 * D)
    cc_s, o = place("cc_s", prob_at, 2 * T)
    ccx, o = place("ccx", o, 2 * PAD)
    cb_s, o = place("cb_s", o, 2 * T)
    waste, _ = place("waste", o, 2 * D, BF16)
    mod_raw, _ = place("mod_raw", kc_at, 2 * D)
    waste0, _ = place("waste0", gate2_at, SLOTS * D, BF16)
    branch, _ = place("branch", prob_at, SLOTS * T)
    f_hi, o = place("f_hi", arena, KT * T, F32R)
    f_lo, o = place("f_lo", o, KT * T, F32R)
    fy, _ = place("fy", o, 2 * TT * 512)
    sq, o = place("sq", arena, KT * T)
    hf, o = place("hf", o, KT * T)
    ms, o = place("ms", o, T)
    rstd, _ = place("rstd", o, T)
    gates, o = place("gates", arena, 2 * CHUNK * T)
    gates_end = o
    gel, o = place("gel", o, 2 * T)
    act_f, o = place("act_f", o, 2 * T)
    a_hi, o = place("a_hi", o, 2 * T, F32R)
    a_lo, o = place("a_lo", o, 2 * T, F32R)
    hot2, o = place("hot2", o, PER_PAIR * BATCH * P, BF16)
    hot1, o = place("hot1", o, PER_PAIR * BATCH * PARTS * CHUNK, BF16)
    eq1, o = place("eq1", o, PER_PAIR * BATCH * CHUNK)
    route_t, o = place("route_t", o, 2 * T)
    gate_t, o = place("gate_t", o, PARTS * T, BF16)
    subk, peer_end = place("subk", o, 2 * PH * NK)
    y_nat, _ = place("y_nat", arena, TT * D)
    pq, o = place("pq", arena, SLOTS * T)
    sc, o = place("sc", o, SLOTS * TT * NK)
    sc2, o = place("sc2", o, TT * NK)
    val, o = place("val", o, SLOTS * TT * TOPK)
    idx, o = place("idx", o, SLOTS * TT * TOPK, U32)
    vals, o = place("vals", o, TT * 2 * PH * TOPK)
    idxs, o = place("idxs", o, TT * 2 * PH * TOPK)
    cand, o = place("cand", o, PH * TOPK * TOPK)
    cand2, o = place("cand2", o, PH * TOPK * TOPK)
    best, o = place("best", o, HK)
    pos, o = place("pos", o, HK, U32)
    pos_ab, o = place("pos_ab", o, 2 * HK, U32)
    pos_f, o = place("pos_f", o, 2 * HK)
    eq, o = place("eq", o, 2 * HK * TOPK)
    route, o = place("route", o, 3 * HK)
    gsum, o = place("gsum", o, 2 * PH)
    rest, o = place("rest", o, P)
    assert o <= gates_end and max(mixer_end, peer_end) <= 229344

    bank = [nc.alloc_psum_tensor(f"bank{i}", [P, 512], F32) for i in range(8)]

    sem = nc.alloc_semaphore
    consts_loaded = sem("consts_loaded")
    first_loaded = [sem(f"first_loaded{s}") for s in range(SLOTS)]
    first_used = [sem(f"first_used{s}") for s in range(SLOTS)]
    mod_loaded = [sem(f"mod_loaded{b}") for b in range(2)]
    mod_used = [sem(f"mod_used{b}") for b in range(2)]
    kv_loaded = sem("kv_loaded")
    c_loaded = sem("c_loaded")
    panel_loaded = [sem(f"panel_loaded{s}") for s in range(SLOTS)]
    hi_ready = [sem(f"hi_ready{s}") for s in range(SLOTS)]
    lo_ready = [sem(f"lo_ready{s}") for s in range(SLOTS)]
    panel_used = [sem(f"panel_used{b}") for b in range(2)]
    bank_free = [sem(f"bank_free{s}") for s in range(SLOTS)]
    layer_loaded = sem("layer_loaded")
    sub_loaded = sem("sub_loaded")
    bias_loaded = [sem("bias_loaded0"), sem("bias_loaded1")]
    bias_masked = sem("bias_masked")
    ones_ready = sem("ones_ready")
    c_ready = sem("c_ready")
    squares = sem("squares")
    sums = sem("sums")
    mean_sq = sem("mean_sq")
    root = sem("root")
    hf_ready = sem("hf_ready")
    hhi_ready = sem("hhi_ready")
    hlo_ready = sem("hlo_ready")
    uhi_ready = sem("uhi_ready")
    ulo_ready = sem("ulo_ready")
    vt_ready = sem("vt_ready")
    vt_act = sem("vt_act")
    vt_dve = sem("vt_dve")
    kv_out = sem("kv_out")
    s_ready = sem("s_ready")
    s_read = sem("s_read")
    max_ready = sem("max_ready")
    exp_ready = sem("exp_ready")
    prob_ready = sem("prob_ready")
    pt_ready = sem("pt_ready")
    pt_act = sem("pt_act")
    pt_dve = sem("pt_dve")
    o_ready = sem("o_ready")
    o_hi = sem("o_hi")
    o_lo = sem("o_lo")
    y1_ready = sem("y1_ready")
    y1_act = sem("y1_act")
    y1_dve = sem("y1_dve")
    y2_ready = sem("y2_ready")
    y2_hi = sem("y2_hi")
    y2_lo = sem("y2_lo")
    merged = sem("merged")
    mhi_ready = sem("mhi_ready")
    mlo_ready = sem("mlo_ready")
    keys_done = sem("keys_done")
    sc_ready = sem("sc_ready")
    sc_used = sem("sc_used")
    top_shifted = sem("top_shifted")
    top_exp = sem("top_exp")
    route_ready = sem("route_ready")
    route_tr = sem("route_tr")
    route_done = sem("route_done")
    gate_hi = sem("gate_hi")
    eq_ready = sem("eq_ready")
    hot2_ready = sem("hot2_ready")
    hot1_ready = sem("hot1_ready")
    gate_mm = sem("gate_mm")
    gate_copied = sem("gate_copied")
    gelu_ready = sem("gelu_ready")
    act_ready = sem("act_ready")
    ahi_ready = sem("ahi_ready")
    alo_ready = sem("alo_ready")
    y_act = sem("y_act")
    y_dve = sem("y_dve")
    yt_ready = sem("yt_ready")
    x_updated = sem("x_updated")
    out_ready = sem("out_ready")
    out_done = sem("out_done")
    carried = sem("carried")
    dve_seq = sem("dve_seq")
    CONSTS = 6
    LOADS = 2

    class Order:

        def __init__(self):
            self.base, self.n = 0, 0

        def step(self, ins, wait=True, hold=False):
            ins.then_inc(dve_seq, 1)
            self.n += 1
            if wait:
                self.wait()
                if hold:
                    carry(nc.vector)

        def wait(self):
            nc.vector.wait_ge(dve_seq, self.base + self.n)

        def enter(self, i, start, steps):
            saved = self.base, self.n
            self.base, self.n = self.base + self.n + (i - start) * steps, 0
            return saved

        def leave(self, saved, turns, steps):
            assert self.n == steps, f"{self.n} steps in a loop's body, not {steps}"
            self.base, self.n = saved[0], saved[1] + turns * steps

    def col(t, n, width=T):
        return t[:, n * width:(n + 1) * width]

    def ahead(g, s):
        return (g, s + 2) if s < 2 else (g + 1, s - 2)

    def after_use(g, s):
        return 2 * g + s // 2 + 2

    def wait_split(eng, g, s):
        eng.wait_ge(panel_loaded[s], (g + 1) * 16)
        eng.wait_ge(panel_used[s % 2], after_use(g, s) - 1)

    def split_panel_hi(g, s):
        wait_split(nc.scalar, g, s)
        nc.scalar.activation(col(split_hi, s % 2, D), col(raw, s, D), ACT.Copy).then_inc(hi_ready[s], 1)

    def split_panel_lo(eng, g, s):
        wait_split(eng, g, s)
        eng.wait_ge(hi_ready[s], g + 2)
        eng.tensor_tensor(col(split_lo, s % 2, D), col(raw, s, D), col(split_hi, s % 2, D).bitcast(F32),
                          ALU.subtract).then_inc(lo_ready[s], 1)

    def carry(eng):
        eng.sem_inc(carried, 1)

    def wait_stored(eng, l, name):
        for s in range(SLOTS):
            eng.wait_ge(bank_free[s], l * PROJ + FIRST[name] + 1)

    block_cm = nc.Block()
    block = block_cm.__enter__()

    @block.sync
    def _(sp):
        sp.dma_start(silu_c[:, :], c_in.broadcast_to([P, 2 * D])).then_inc(c_loaded, 16)
        for s in range(SLOTS):
            sp.dma_start(col(raw, s, D), mod_panels[s, :, :]).then_inc(first_loaded[s], 16)
        for dst, src in ((x, x_in), (ident, ident_in), (iota, iota_in), (mask, mask_in), (gfin, g_final),
                         (dft, dft_in)):
            sp.dma_start(dst[:, :], src).then_inc(consts_loaded, 16)
        with sp.Fori(1, NEXT_G) as i:
            for s in range(SLOTS):
                sp.wait_ge(first_used[s], i)
                sp.dma_start(col(raw, s, D), mod_panels[i * SLOTS + s, :, :]).then_inc(first_loaded[s], 16)
        for s in range(SLOTS):
            sp.wait_ge(first_used[s], NEXT_G)

        def load_panel(g, s):
            sp.wait_ge(hi_ready[s], g + 1)
            sp.wait_ge(lo_ready[s], g + 1)
            sp.dma_start(col(raw, s, D), panels[g * SLOTS + s, :, :]).then_inc(panel_loaded[s], 16)

        with sp.Fori(0, DEPTH) as l:
            mod_from = FIRST["qkvf"] + 1
            with sp.Fori(0, mod_from) as i:
                for s in range(SLOTS):
                    load_panel(l * GROUPS + i, s)
            with sp.Fori(0, MOD_G) as i:
                for s in range(SLOTS):
                    load_panel(l * GROUPS + mod_from + i, s)
                    b, n = s % 2, l * MOD_G + i
                    sp.wait_ge(mod_used[b], n * 2 + s // 2 + 1)
                    sp.dma_start(col(mod_raw, b, D), mod_panels[(n + NEXT_G) * SLOTS + s, :, :]
                                 ).then_inc(mod_loaded[b], 16)
            with sp.Fori(mod_from + MOD_G, GROUPS) as i:
                for s in range(SLOTS):
                    load_panel(l * GROUPS + i, s)
        sp.wait_ge(out_ready, 1)
        sp.dma_start(y_out, hf[:, :]).then_inc(out_done, 16)
        sp.wait_ge(out_done, 16)
        sp.wait_ge(kv_out, DEPTH * 32)

    @block.tensor
    def _(pe):
        mm = nc.tensor.matmul
        transpose = lambda out, in_: nc.tensor.transpose(out, in_, ident[:, :])

        def panel(g, s, out, rhs_hi, rhs_lo, n):
            pe.wait_ge(hi_ready[s], g + 2)
            pe.wait_ge(lo_ready[s], g + 2)
            for kk in range(KT):
                w_hi, w_lo = col(col(split_hi, s % 2, D), kk, P), col(col(split_lo, s % 2, D), kk, P)
                mm(out, w_hi, col(rhs_hi, kk, n), start=(kk == 0), stop=False)
                mm(out, w_hi, col(rhs_lo, kk, n), start=False, stop=False)
                last = mm(out, w_lo, col(rhs_hi, kk, n), start=False, stop=(kk == KT - 1))
            last.then_inc(panel_used[s % 2], 1)

        def project(l, local, s, rhs_hi, rhs_lo, n=T):
            pe.wait_ge(bank_free[s], l * PROJ + local + 1)
            panel(l * GROUPS + local, s, bank[s][:, 0:n], rhs_hi, rhs_lo, n)

        def stage(l, name, rhs_hi, rhs_lo, n=T):
            carry(pe)
            with pe.Fori(0, COUNT[name]) as i:
                for s in range(SLOTS):
                    project(l, i + FIRST[name], s, rhs_hi, rhs_lo, n)

        def norm_sums(n):
            pe.wait_ge(squares, n)
            for kk in range(KT):
                last = mm(bank[4][:, 0:T], ones[:, :], col(sq, kk), start=(kk == 0), stop=(kk == KT - 1))
            last.then_inc(sums, 1)

        pe.sem_inc(panel_used[0], 1)
        pe.sem_inc(panel_used[1], 1)
        pe.sem_inc(keys_done, 4)
        pe.sem_inc(route_tr, 1)
        pe.sem_inc(gate_mm, PER_PAIR)
        pe.wait_ge(ones_ready, 1)
        pe.wait_ge(consts_loaded, CONSTS * 16)
        with pe.Fori(0, DEPTH) as l:
            norm_sums(2 * l + 1)
            pe.wait_ge(hlo_ready, l * 16 + 8)
            for name in ("ccx", "cb", "qkvf", "gates"):
                stage(l, name, h_hi, h_lo)

            wait_stored(pe, l, "conv_out")
            for h in range(HEADS):
                if h >= 4:
                    pe.wait_ge(vt_dve if h % 2 else vt_act, l * 4 + h // 2 - 1)
                for t in range(TT):
                    last = transpose(bank[4 + h % 4][:, t * P:(t + 1) * P], col(v, h)[:, t * P:(t + 1) * P])
                last.then_inc(vt_ready, 1)
            pe.wait_ge(vt_act, l * 4 + 4)
            pe.wait_ge(vt_dve, l * 4 + 4)
            pe.wait_ge(kv_loaded, (l + 1) * 2 * 16)

            def scores(h):
                if h >= 1:
                    pe.wait_ge(s_read, l * HEADS + h)
                qh, kh = col(q, h), col(k, h)
                mm(bank[4][:, 0:TP], qh[:, 0:TP], kh[:, 0:TP], start=True, stop=True)
                for j in range(2):
                    qt = qh[:, TP + j * P:TP + (j + 1) * P]
                    c0 = TP if j == 0 else 0
                    mm(bank[4 + j][:, c0:c0 + TS], qt, kh[:, TP:T], start=True, stop=True)
                    last = mm(bank[4 + j][:, c0 + TS:c0 + KEYS], qt, col(kc, h, CTX), start=True, stop=True)
                last.then_inc(s_ready, 1)

            scores(0)
            for h in range(HEADS):
                if h + 1 < HEADS:
                    scores(h + 1)
                if h == 0:
                    pe.wait_ge(uhi_ready, (l + 1) * KT)
                    pe.wait_ge(ulo_ready, (l + 1) * KT + 2)
                project(l, FIRST["conv_out"] + h // SLOTS, h % SLOTS, u_hi, u_lo)
                pr, pt, vh = col(prob, h % 2, SCORES), col(prob_t, h % 2, SCORES), col(v, h)
                pe.wait_ge(prob_ready, l * HEADS + h + 1)
                if h >= 1:
                    pe.wait_ge(o_lo, l * HEADS + h)
                for kt in range(3):
                    for j in range(2):
                        c0 = kt * TS + j * P
                        transpose(bank[6 + c0 // 512][:, c0 % 512:c0 % 512 + P],
                                  pr[:, TP + j * KEYS + kt * P:TP + j * KEYS + (kt + 1) * P])
                transpose(bank[7][:, TS:TS + P], pr[:, 0:TP]).then_inc(pt_ready, 1)
                pe.wait_ge(pt_act, l * HEADS + h + 1)
                pe.wait_ge(pt_dve, l * HEADS + h + 1)
                mm(bank[6][:, 0:TP], vh[:, 0:P], pt[:, 3 * TS:3 * TS + TP], start=True, stop=True)
                mm(bank[6][:, TP:T], vh[:, P:2 * P], pt[:, 0:TS], start=True, stop=False)
                mm(bank[6][:, TP:T], vh[:, 2 * P:3 * P], pt[:, TS:2 * TS], start=False, stop=False)
                mm(bank[6][:, TP:T], col(vc, h, DH), pt[:, 2 * TS:3 * TS], start=False,
                   stop=True).then_inc(o_ready, 1)

            def fourier_channels(g):
                for t in range(TT):
                    u = g * TT + t
                    if u >= 2:
                        pe.wait_ge(y1_dve if u % 2 else y1_act, l * 6 + u // 2)
                    for c in range(2):
                        last = mm(bank[4 + u % 2][:, :], col(f, 2 * g + c)[:, t * P:(t + 1) * P],
                                  dft[:, DFT_CH + c * 512:DFT_CH + (c + 1) * 512], start=(c == 0), stop=(c == 1))
                    last.then_inc(y1_ready, 1)

            def fourier_tokens(g):
                pe.wait_ge(y1_act, l * 6 + (TT * (g + 1) + 1) // 2)
                pe.wait_ge(y1_dve, l * 6 + TT * (g + 1) // 2)
                yg = col(fy, g % 2, TT * 512)
                for dt in range(2):
                    u = 2 * g + dt
                    if u >= 2:
                        pe.wait_ge(y2_lo, l * 8 + u - 1)
                    out = bank[6 + u % 2]
                    for part in range(2):
                        w = yg[:, part * FD + dt * P:part * FD + (dt + 1) * P]
                        mm(out[:, 0:TP], w, dft[:, DFT_P + part * TP:DFT_P + (part + 1) * TP],
                           start=(part == 0), stop=(part == 1))
                    for t in range(2):
                        for part in range(2):
                            w0 = (1 + t) * 512 + part * FD + dt * P
                            r0 = DFT_S + (2 * t + part) * TS
                            last = mm(out[:, TP:T], yg[:, w0:w0 + P], dft[:, r0:r0 + TS],
                                      start=(t + part == 0), stop=(t + part == 2))
                    last.then_inc(y2_ready, 1)

            pe.wait_ge(o_lo, (l + 1) * HEADS)
            fourier_channels(0)
            for g in range(1, FG):
                fourier_channels(g)
                fourier_tokens(g - 1)
            fourier_tokens(FG - 1)

            stage(l, "attn_out", h_hi, h_lo)
            pe.wait_ge(y2_lo, (l + 1) * 8)
            stage(l, "four_out", f_hi, f_lo)
            pe.wait_ge(mhi_ready, (l + 1) * KT)
            pe.wait_ge(mlo_ready, (l + 1) * KT)
            stage(l, "o", u_hi, u_lo)

            norm_sums(2 * l + 2)
            pe.wait_ge(hlo_ready, l * 16 + 16)
            pe.wait_ge(sub_loaded, (l + 1) * 16)

            carry(pe)

            def keys(i, s):
                n = (l * COUNT["pq"] + i) * SLOTS + s
                pe.wait_ge(bank_free[s], l * PROJ + FIRST["pq"] + i + 2)
                pe.wait_ge(sc_ready, n + 1)
                for t in range(TT):
                    last = mm(col(bank[4 + s], t, NK), col(col(pq, s), t, P),
                              subk[:, bass.ds((i * SLOTS + s) * NK, NK)], start=True, stop=True)
                last.then_inc(keys_done, 1)

            with pe.Fori(0, COUNT["pq"]) as i:
                for s in range(SLOTS):
                    project(l, i + FIRST["pq"], s, h_hi, h_lo)
                    if s:
                        keys(i, s - 1)
                keys(i, SLOTS - 1)

            with pe.Fori(0, TT) as t:
                pe.wait_ge(route_ready, l * TT + t + 1)
                pe.wait_ge(route_done, l * TT + t + 1)
                for j in range(3):
                    last = transpose(col(bank[4], j, P), col(route, j, HK))
                last.then_inc(route_tr, 1)

            def build_gates(chunk, t0, batches, out):
                n = (l * CHUNKS + chunk) * NB + t0
                pe.wait_ge(gate_copied, n + batches[0] + 1)
                for r in batches:
                    pe.wait_ge(hot2_ready, n + r + 1)
                    pe.wait_ge(hot1_ready, n + r + 1)
                    for t in range(BATCH):
                        w, parts = col(hot2, r * BATCH + t, P), col(hot1, r * BATCH + t, PARTS * CHUNK)
                        o = col(out, (r - batches[0]) * BATCH + t, CHUNK)
                        for c in range(PARTS):
                            last = mm(o, w, col(parts, c, CHUNK), start=(c == 0), stop=(c == PARTS - 1))
                    last.then_inc(gate_mm, 1)

            peer = l * GROUPS + FIRST["peer"]

            def outputs_v(g, s, b, j, first=False, last=False):
                pe.wait_ge(hi_ready[s], g + 2)
                pe.wait_ge(lo_ready[s], g + 2)
                pe.wait_ge(ahi_ready, l * NK + j + 3)
                pe.wait_ge(alo_ready, l * NK + j + 1)
                hi, lo = col(split_hi, s % 2, D), col(split_lo, s % 2, D)
                for t in range(TT):
                    w_hi, w_lo = col(col(a_hi, b), t, P), col(col(a_lo, b), t, P)
                    for w, rhs, start, stop in ((w_hi, hi, first, False), (w_hi, lo, False, False),
                                                (w_lo, hi, False, last)):
                        for c in range(2):
                            m = mm(bank[2 + 2 * t + c][:, :], w, col(rhs, c, 512), start=start, stop=stop)
                m.then_inc(panel_used[s % 2], 1)

            def scores_u(g, s, j):
                pe.wait_ge(gelu_ready, l * NK + j)
                panel(g, s, bank[0][:, 0:T], h_hi, h_lo, T)

            def pair(i, chunk, first=False):
                g, j, t0 = peer + i, 2 * i, (i - chunk * PAIRS) * PER_PAIR
                scores_u(g, 1, j + 1)
                outputs_v(g, 2, 0, j, first=first)
                if chunk + 1 < CHUNKS:
                    build_gates(chunk + 1, t0, (0, 1), bank[1])
                scores_u(g, 3, j + 2)
                if chunk + 1 < CHUNKS:
                    build_gates(chunk + 1, t0, (2,), bank[1])
                outputs_v(g + 1, 0, 1, j + 1)

            panel(peer, 0, bank[0][:, 0:T], h_hi, h_lo, T)
            carry(pe)
            with pe.Fori(0, PAIRS) as i:
                build_gates(0, i * PER_PAIR, (0, 1), bank[1])
                build_gates(0, i * PER_PAIR, (2,), bank[2])
            for chunk in range(CHUNKS):
                first, last = chunk == 0, chunk == CHUNKS - 1
                if first:
                    pair(0, 0, first=True)
                carry(pe)
                with pe.Fori(chunk * PAIRS + first, (chunk + 1) * PAIRS - last) as i:
                    pair(i, chunk)
            g = peer + CHUNKS * PAIRS - 1
            scores_u(g, 1, NK - 1)
            outputs_v(g, 2, 0, NK - 2)
            outputs_v(g, 3, 1, NK - 1, last=True)

            pe.wait_ge(y_act, (l + 1) * TT)
            pe.wait_ge(y_dve, (l + 1) * TT)
            for kk in range(KT):
                if kk >= 2:
                    pe.wait_ge(x_updated, l * KT + kk)
                for t in range(TT):
                    last = transpose(col(bank[kk % 2], t, P), y_nat[:, t * D + kk * P:t * D + (kk + 1) * P])
                last.then_inc(yt_ready, 1)
        norm_sums(2 * DEPTH + 1)

    @block.scalar
    def _(act):
        copy = lambda out, in_: nc.scalar.activation(out, in_, ACT.Copy)

        def group(l, local, epilogue=None, after=None):
            for s in range(SLOTS):
                split_panel_hi(*ahead(l * GROUPS + local, s))
                if epilogue:
                    epilogue(s)
            if after:
                after()

        def product(g, s):
            act.wait_ge(panel_used[s % 2], after_use(g, s))
            return bank[s][:, 0:T]

        def norm(n):
            nc.scalar.activation(sq[:, :], x[:, :], ACT.Square).then_inc(squares, 1)
            act.wait_ge(mean_sq, n)
            nc.scalar.activation(ms[:, :], ms[:, :], ACT.Sqrt).then_inc(root, 1)

        def split_input(l, half):
            for kk in range(KT):
                act.wait_ge(hf_ready, l * 16 + half * 8 + kk + 1)
                copy(col(h_hi, kk), col(hf, kk)).then_inc(hhi_ready, 1)

        act.sem_inc(sc_ready, 4)
        act.sem_inc(gate_copied, 1)
        for s in range(SLOTS):
            act.sem_inc(hi_ready[s], 1)
        act.sem_inc(route_done, 1)
        act.sem_inc(ahi_ready, 2)
        act.wait_ge(c_loaded, 16)
        nc.scalar.activation(silu_c[:, :], silu_c[:, :], ACT.Silu).then_inc(c_ready, 1)
        act.wait_ge(consts_loaded, CONSTS * 16)
        with act.Fori(0, DEPTH) as l:
            act.wait_ge(x_updated, l * KT + 1)
            for dst, src in ((vec, vecs[l, :, :]), (dft, dft_in)):
                act.dma_start(dst[:, :], src).then_inc(layer_loaded, 16)
            for h in range(2):
                act.dma_start(col(bias, h, 2 * TS), bias_in[l * HEADS + h, :, :]).then_inc(bias_loaded[h], 16)
            norm(2 * l + 1)
            split_panel_hi(l * GROUPS, 0)
            split_panel_hi(l * GROUPS, 1)
            split_input(l, 0)

            with act.Fori(0, COUNT["ccx"]) as i:
                local = i + FIRST["ccx"]

                def store_cc(s):
                    if s % 2 == 0:
                        out = product(l * GROUPS + local, s)
                        act.wait_ge(bank_free[s + 1], l * PROJ + local + 1)
                        copy(col(cc_s, s // 2), out).then_inc(bank_free[s], 1)
                group(l, local, store_cc)

            with act.Fori(0, COUNT["cb"]) as i:
                local = i + FIRST["cb"]

                def split_conv(s):
                    act.wait_ge(bank_free[s], l * PROJ + local + 2)
                    copy(u_hi[:, bass.ds((i * SLOTS + s) * T, T)], col(cb_s, s % 2)).then_inc(uhi_ready, 1)
                group(l, local, split_conv)

            with act.Fori(0, COUNT["qkvf"]) as i:
                local = i + FIRST["qkvf"]

                def store(s):
                    if s % 2 == 0:
                        out = product(l * GROUPS + local, s)
                        copy(qkvf[:, bass.ds((i * SLOTS + s) * T, T)], out).then_inc(bank_free[s], 1)
                group(l, local, store)

            for first, turns, dst in ((0, 4, gate01), (4, 2, gate2)):
                if first:
                    for b in range(2):
                        act.wait_ge(mod_used[b], (l + 1) * MOD_G * 2 + 1)
                    for dst_, src in ((kc, k_cache[l, :, :]), (vc, v_cache[l, :, :])):
                        act.dma_start(dst_[:, :], src).then_inc(kv_loaded, 16)
                with act.Fori(0, turns) as i:
                    local = i + FIRST["gates"] + first

                    def store_gate(s):
                        out = product(l * GROUPS + local, s)
                        nc.scalar.activation(dst[:, bass.ds((i * SLOTS + s) * T, T)], out,
                                             ACT.Sigmoid).then_inc(bank_free[s], 1)
                    group(l, local, store_gate)

            for s in (1, 3):
                act.wait_ge(bank_free[s], l * PROJ + FIRST["gates"] + 1)
            wait_stored(act, l, "gates")
            act.dma_start(new_k[l, :, :, :], k.rearrange("p (h t) -> p h t", h=HEADS)[:, :, 0:TP]
                          ).then_inc(kv_out, 16)
            for h in range(0, HEADS, 2):
                act.wait_ge(vt_ready, l * HEADS + h + 1)
                copy(col(v, h), bank[4 + h % 4][:, 0:T]).then_inc(vt_act, 1)
            act.wait_ge(vt_act, l * 4 + 4)
            act.wait_ge(vt_dve, l * 4 + 4)
            act.dma_start(new_v[l, :, :, :], v.rearrange("p (h t) -> p h t", h=HEADS)[:, :, 0:DH]
                          ).then_inc(kv_out, 16)

            def exps(h):
                pr, sm = col(prob, h % 2, SCORES), col(softm, h % 2, 16)
                act.wait_ge(max_ready, l * HEADS + h + 1)
                for r, (beg, end) in enumerate(((0, TP), (TP, TP + KEYS), (TP + KEYS, SCORES))):
                    last = nc.scalar.activation(pr[:, beg:end], pr[:, beg:end], ACT.Exp, bias=sm[:, r:r + 1],
                                                scale=1.0, accum_out=sm[:, 4 + r:5 + r])
                last.then_inc(exp_ready, 1)

            exps(0)
            for h in range(HEADS):
                if h + 1 < HEADS:
                    exps(h + 1)
                if h + 2 < HEADS:
                    act.wait_ge(s_read, l * HEADS + h + 1)
                    act.dma_start(col(bias, h % 2, 2 * TS), bias_in[l * HEADS + h + 2, :, :]
                                  ).then_inc(bias_loaded[h % 2], 16)
                split_panel_hi(*ahead(l * GROUPS + FIRST["conv_out"] + h // SLOTS, h % SLOTS))
                act.wait_ge(pt_ready, l * HEADS + h + 1)
                if h >= 2:
                    act.wait_ge(o_ready, l * HEADS + h - 1)
                copy(col(prob_t, h % 2, SCORES)[:, 0:512], bank[6][:, :]).then_inc(pt_act, 1)
                act.wait_ge(o_ready, l * HEADS + h + 1)
                copy(col(h_hi, h), bank[6][:, 0:T]).then_inc(o_hi, 1)

            act.wait_ge(kv_out, (l + 1) * 32)

            def store_channels(g):
                for u in range(g * TT, (g + 1) * TT):
                    if u % 2 == 0:
                        act.wait_ge(y1_ready, l * 12 + u + 1)
                        if g >= 2:
                            act.wait_ge(y2_ready, l * 8 + 2 * (g - 1))
                        copy(col(col(fy, g % 2, TT * 512), u % TT, 512), bank[4][:, :]).then_inc(y1_act, 1)

            def split_tokens(g):
                for u in (2 * g, 2 * g + 1):
                    act.wait_ge(y2_ready, l * 8 + u + 1)
                    copy(col(f_hi, u), bank[6 + u % 2][:, 0:T]).then_inc(y2_hi, 1)

            store_channels(0)
            for g in range(1, FG):
                store_channels(g)
                split_tokens(g - 1)
            split_tokens(FG - 1)

            with act.Fori(0, COUNT["attn_out"]) as i:
                group(l, i + FIRST["attn_out"])
            with act.Fori(0, COUNT["four_out"]) as i:
                def split_merged(s):
                    act.wait_ge(merged, l * KT + i * SLOTS + s + 1)
                    n = bass.ds((i * SLOTS + s) * T, T)
                    copy(u_hi[:, n], gate01[:, n]).then_inc(mhi_ready, 1)
                group(l, i + FIRST["four_out"], split_merged)
            act.dma_start(subk[:, :], sub_keys[l, :, :]).then_inc(sub_loaded, 16)
            with act.Fori(0, COUNT["o"]) as i:
                group(l, i + FIRST["o"])

            wait_stored(act, l, "pq")
            norm(2 * l + 2)
            split_input(l, 1)

            with act.Fori(0, COUNT["pq"]) as i:
                local = i + FIRST["pq"]

                def store_scores(s):
                    n = (l * COUNT["pq"] + i) * SLOTS + s
                    act.wait_ge(keys_done, n + 1 + 4)
                    act.wait_ge(sc_used, n + 1)
                    copy(col(sc, s), bank[4 + s][:, 0:T]).then_inc(sc_ready, 1)

                def store_query(s):
                    out = product(l * GROUPS + local, s)
                    act.wait_ge(keys_done, (l * COUNT["pq"] + i) * SLOTS + s + 1)
                    copy(col(pq, s), out).then_inc(bank_free[s], 1)
                    if s:
                        store_scores(s - 1)
                group(l, local, store_query, lambda: store_scores(SLOTS - 1))

            with act.Fori(0, TT) as t:
                act.wait_ge(top_shifted, l * TT + t + 1)
                nc.scalar.activation(best[:, :], best[:, :], ACT.Exp).then_inc(top_exp, 1)
                act.wait_ge(route_tr, l * TT + t + 2)
                copy(route_t[:, 0:2 * T].rearrange("p (j t) -> p j t", j=2)[:, :, bass.ds(t * P, P)],
                     bank[4][:, 0:2 * P].rearrange("p (j t) -> p j t", j=2))
                copy(gate_t[:, bass.ds(t * P, P)], col(bank[4], 2, P)).then_inc(gate_hi, 1)

            def store_gates(chunk, t0, batches, src):
                act.wait_ge(gate_mm, (l * CHUNKS + chunk) * NB + t0 + batches[-1] + 1 + PER_PAIR)
                n = len(batches) * BATCH
                dst = col(gates, chunk % 2, CHUNK * T).rearrange("p (j t) -> p j t", j=CHUNK)
                copy(dst[:, :, bass.ds((t0 + batches[0]) * BATCH, n)],
                     src[:, 0:n * CHUNK].rearrange("p (t j) -> p j t", j=CHUNK)).then_inc(gate_copied, len(batches))

            peer = l * GROUPS + FIRST["peer"]

            def gelu(i, b, g, s):
                j = l * NK + 2 * i + b
                act.wait_ge(panel_used[s % 2], after_use(g, s))
                act.wait_ge(act_ready, j + 1)
                nc.scalar.activation(col(gel, b), bank[0][:, 0:T], ACT.Gelu).then_inc(gelu_ready, 1)

            def split_act(i, b, first=False):
                j = l * NK + 2 * i + b
                act.wait_ge(act_ready, j + 1 + 2)
                if not first:
                    act.wait_ge(panel_used[0], after_use(*((peer + i - 1, 2) if b == 0 else (peer + i, 0))))
                copy(col(a_hi, b), col(act_f, b)).then_inc(ahi_ready, 1)

            def pair(i, chunk, first=False, last=False):
                g, t0 = peer + i, (i - chunk * PAIRS) * PER_PAIR
                build = chunk + 1 < CHUNKS
                gelu(i, 0, *((peer, 0) if first else (g - 1, 3)))
                split_act(i, 0, first)
                split_panel_hi(g, 2)
                split_panel_hi(g, 3)
                gelu(i, 1, g, 1)
                split_act(i, 1, first)
                if not last:
                    split_panel_hi(g + 1, 0)
                if build:
                    store_gates(chunk + 1, t0, (0, 1), bank[1])
                if not last:
                    split_panel_hi(g + 1, 1)
                if build:
                    store_gates(chunk + 1, t0, (2,), bank[1])

            with act.Fori(0, PAIRS) as i:
                store_gates(0, i * PER_PAIR, (0, 1), bank[1])
                store_gates(0, i * PER_PAIR, (2,), bank[2])
            for chunk in range(CHUNKS):
                first, last = chunk == 0, chunk == CHUNKS - 1
                if first:
                    pair(0, 0, first=True)
                else:
                    act.wait_ge(act_ready, l * NK + chunk * CHUNK + 2)
                with act.Fori(chunk * PAIRS + first, (chunk + 1) * PAIRS - last) as i:
                    pair(i, chunk)
            pair(LAST_PAIR, CHUNKS - 1, last=True)

            act.wait_ge(panel_used[1], after_use(peer + LAST_PAIR, 3))
            for t in range(TT):
                copy(col(y_nat, 2 * t, 512), bank[2 + 2 * t][:, :]).then_inc(y_act, 1)
        act.wait_ge(x_updated, DEPTH * KT + 1)
        norm(2 * DEPTH + 1)

    @block.gpsimd
    def _(pool):
        def panels_lo(l, local):
            g = l * GROUPS + local
            for s in (0, 2):
                split_panel_lo(pool, *ahead(g, s))

        def lo(dst, src, hi):
            return pool.tensor_tensor(dst, src, hi.bitcast(F32), ALU.subtract)

        pool.memset(ones[:, :], 1.0).then_inc(ones_ready, 1)
        pool.sem_inc(ulo_ready, 2)
        pool.sem_inc(lo_ready[0], 1)
        pool.sem_inc(lo_ready[2], 1)
        with pool.Fori(0, DEPTH) as l:
            split_panel_lo(pool, l * GROUPS, 0)
            with pool.Fori(FIRST["ccx"], FIRST["cb"]) as i:
                panels_lo(l, i)
            with pool.Fori(0, COUNT["cb"]) as i:
                for s in range(SLOTS):
                    if s % 2 == 0:
                        split_panel_lo(pool, *ahead(l * GROUPS + FIRST["cb"] + i, s))
                    n = bass.ds((i * SLOTS + s) * T, T)
                    pool.wait_ge(uhi_ready, l * KT + i * SLOTS + s + 1)
                    lo(u_lo[:, n], col(cb_s, s % 2), u_hi[:, n]).then_inc(ulo_ready, 1)
            with pool.Fori(FIRST["qkvf"], FIRST["conv_out"]) as i:
                panels_lo(l, i)

            def add_mask(h):
                pool.wait_ge(bias_loaded[h % 2], (l * 4 + h // 2 + 1) * 16)
                bt = col(bias, h % 2, 2 * TS).rearrange("p (r c) -> p r c", c=GRID_W)
                pool.tensor_tensor(bt, bt, mask[:, :].unsqueeze(1).broadcast_to([P, 8, GRID_W]),
                                   ALU.add).then_inc(bias_masked, 1)

            add_mask(0)
            add_mask(1)
            for h in range(HEADS):
                if h % 2 == 0:
                    split_panel_lo(pool, *ahead(l * GROUPS + FIRST["conv_out"] + h // SLOTS, h % SLOTS))
                if h + 2 < HEADS:
                    add_mask(h + 2)
            with pool.Fori(FIRST["attn_out"], FIRST["four_out"]) as i:
                panels_lo(l, i)
            with pool.Fori(0, COUNT["four_out"]) as i:
                for s in range(SLOTS):
                    if s % 2 == 0:
                        split_panel_lo(pool, *ahead(l * GROUPS + FIRST["four_out"] + i, s))
                    n = bass.ds((i * SLOTS + s) * T, T)
                    pool.wait_ge(mhi_ready, l * KT + i * SLOTS + s + 1)
                    lo(u_lo[:, n], gate01[:, n], u_hi[:, n]).then_inc(mlo_ready, 1)
            with pool.Fori(FIRST["o"], FIRST["peer"]) as i:
                panels_lo(l, i)

            def hot1_of(chunk, t0, batches):
                for r in batches:
                    n = (l * CHUNKS + chunk) * NB + t0 + r
                    pool.wait_ge(eq_ready, n + 1)
                    pool.wait_ge(gate_mm, n + 1)
                    gt = gate_t[:, :].rearrange("p (c t) -> p t c", c=PARTS)[:, bass.ds((t0 + r) * BATCH, BATCH), :]
                    shape = [P, BATCH, PARTS, CHUNK]
                    pool.tensor_tensor(col(hot1, r, BATCH * PARTS * CHUNK).rearrange("p (t c j) -> p t c j", c=PARTS, j=CHUNK),
                                       col(eq1, r, BATCH * CHUNK).rearrange("p (t j) -> p t j", j=CHUNK)
                                       .unsqueeze(2).broadcast_to(shape),
                                       gt.unsqueeze(3).broadcast_to(shape), ALU.mult).then_inc(hot1_ready, 1)

            peer = l * GROUPS + FIRST["peer"]
            with pool.Fori(0, PAIRS) as i:
                hot1_of(0, i * PER_PAIR, (0, 1, 2))
            for chunk in range(CHUNKS):
                with pool.Fori(chunk * PAIRS, (chunk + 1) * PAIRS - (chunk == CHUNKS - 1)) as i:
                    split_panel_lo(pool, peer + i, 2)
                    if chunk + 1 < CHUNKS:
                        hot1_of(chunk + 1, (i - chunk * PAIRS) * PER_PAIR, (0, 1))
                    split_panel_lo(pool, peer + i + 1, 0)
                    if chunk + 1 < CHUNKS:
                        hot1_of(chunk + 1, (i - chunk * PAIRS) * PER_PAIR, (2,))
            split_panel_lo(pool, peer + LAST_PAIR, 2)

    @block.vector
    def _(dve):
        V = nc.vector
        order = Order()

        def group(l, local, epilogue=None):
            for s in range(SLOTS):
                if s % 2:
                    split_panel_lo(dve, *ahead(l * GROUPS + local, s))
                if epilogue:
                    epilogue(s)

        def product(l, local, s):
            dve.wait_ge(panel_used[s % 2], after_use(l * GROUPS + local, s))
            return bank[s][:, 0:T]

        def norm(n):
            dve.wait_ge(sums, n)
            V.tensor_scalar(ms[:, :], bank[4][:, 0:T], 1.0 / D, EPS, ALU.mult, ALU.add).then_inc(mean_sq, 1)
            dve.wait_ge(root, n)
            order.step(V.reciprocal(rstd[:, :], ms[:, :]))
            order.step(V.tensor_tensor(hf[:, :].rearrange("p (k t) -> p k t", k=KT),
                                       x[:, :].rearrange("p (k t) -> p k t", k=KT),
                                       rstd[:, :].unsqueeze(1).broadcast_to([P, KT, T]), ALU.mult))

        def modulate(l, half):
            shift = SHIFT2 if half else SHIFT1
            for kk in range(KT):
                for m, (beg, end) in enumerate(STREAMS):
                    c = (shift * KT + kk) * 2 + m
                    gc = (half * KT + kk) * 2 + m
                    last = V.tensor_scalar(col(hf, kk)[:, beg:end], col(hf, kk)[:, beg:end], gain[:, gc:gc + 1],
                                           modv[:, c:c + 1], ALU.mult, ALU.add)
                last.then_inc(hf_ready, 1)
            for kk in range(KT):
                dve.wait_ge(hhi_ready, l * 16 + half * 8 + kk + 1)
                V.tensor_tensor(col(h_lo, kk), col(hf, kk), col(h_hi, kk).bitcast(F32),
                                ALU.subtract).then_inc(hlo_ready, 1)

        for s in range(SLOTS):
            dve.sem_inc(bank_free[s], 1)
        dve.sem_inc(sc_used, 4)
        dve.sem_inc(act_ready, 2)
        dve.sem_inc(x_updated, 1)
        for b in range(2):
            dve.sem_inc(mod_used[b], 1)
        dve.sem_inc(lo_ready[1], 1)
        dve.sem_inc(lo_ready[3], 1)

        def modulation(panel, waste, n, used):
            for m in range(2):
                last = V.scalar_tensor_tensor(waste if m == 0 else panel, panel, 1.0, col(silu_c, m, D), ALU.mult,
                                              ALU.mult, accum_out=modv[:, bass.ds(n * 2 + m, 1)])
            last.then_inc(used, 1)

        def add_bias(first, blocks):
            mods = modv[:, first * 2:(first + blocks) * 2].rearrange("p (n m) -> p n m", m=2)
            order.step(V.tensor_tensor(mods, mods, vec[:, B_MOD + first:B_MOD + first + blocks].unsqueeze(2)
                                       .broadcast_to([P, blocks, 2]), ALU.add))

        def make_gain(half):
            scale, g0 = ((SCALE1, G_MIX), (SCALE2, G_FFN))[half]
            order.step(V.scalar_tensor_tensor(
                gain[:, half * 16:half * 16 + 16].rearrange("p (k m) -> p k m", m=2),
                modv[:, scale * 16:scale * 16 + 16].rearrange("p (k m) -> p k m", m=2), 1.0,
                vec[:, g0:g0 + KT].unsqueeze(2).broadcast_to([P, KT, 2]), ALU.add, ALU.mult))

        dve.wait_ge(c_ready, 1)
        with dve.Fori(0, NEXT_G) as i:
            for s in range(SLOTS):
                dve.wait_ge(first_loaded[s], (i + 1) * 16)
                modulation(col(raw, s, D), col(waste0, s, D), i * SLOTS + s, first_used[s])
        for s in range(SLOTS):
            dve.wait_ge(first_used[s], NEXT_G)
        dve.wait_ge(consts_loaded, CONSTS * 16)
        carry(dve)

        def mod_panel(l, i, s, block):
            n = (l * MOD_G + i) * 2 + s // 2
            dve.wait_ge(mod_loaded[s % 2], (n + 1) * 16)
            modulation(col(mod_raw, s % 2, D), col(waste, s % 2, D), block, mod_used[s % 2])

        LAYER_STEPS = 325
        with dve.Fori(0, DEPTH) as l:
            layer = order.enter(l, 0, LAYER_STEPS)
            norm(2 * l + 1)
            dve.wait_ge(layer_loaded, (l + 1) * LOADS * 16)
            split_panel_lo(dve, l * GROUPS, 1)
            add_bias(SHIFT1 * KT, 2 * KT)
            make_gain(0)
            modulate(l, 0)

            order.step(V.memset(ccx[:, :], 0.0))
            carry(dve)
            with dve.Fori(0, COUNT["ccx"]) as i:
                inner = order.enter(i, 0, 6)
                local = i + FIRST["ccx"]

                def convolve(s):
                    if s % 2 == 0:
                        return
                    cx, b = product(l, local, s), s // 2
                    dve.wait_ge(bank_free[s - 1], l * PROJ + local + 2)
                    pad = col(ccx, b, PAD)
                    for (beg, end), (p0, p1) in zip(STREAMS, SEG):
                        last = V.tensor_tensor(pad[:, p0:p1], col(cc_s, b)[:, beg:end], cx[:, beg:end], ALU.mult)
                    last.then_inc(bank_free[s], 1)
                    dve.wait_ge(bank_free[s], l * PROJ + local + 2)
                    n = i * 2 + b
                    u = conv[:, bass.ds(n * PAD + 1, PAD - 2)]
                    taps = [vec[:, bass.ds(n + (CONV_W + tap * KT), 1)] for tap in range(3)]
                    order.step(V.tensor_scalar(u, pad[:, 0:PAD - 2], taps[0], None, ALU.mult))
                    for tap in (1, 2):
                        order.step(V.scalar_tensor_tensor(u, pad[:, tap:tap + PAD - 2], taps[tap], u,
                                                          ALU.mult, ALU.add))
                group(l, local, convolve)
                order.leave(inner, COUNT["ccx"], 6)

            with dve.Fori(0, COUNT["cb"]) as i:
                local = i + FIRST["cb"]

                def times_cb(s):
                    cb = product(l, local, s)
                    dve.wait_ge(ulo_ready, l * KT + i * SLOTS + s + 1)
                    for (beg, end), (p0, p1) in zip(STREAMS, SEG):
                        last = V.tensor_tensor(col(cb_s, s % 2)[:, beg:end],
                                               conv[:, bass.ds((i * SLOTS + s) * PAD + p0, p1 - p0)],
                                               cb[:, beg:end], ALU.mult)
                    last.then_inc(bank_free[s], 1)
                group(l, local, times_cb)

            with dve.Fori(0, COUNT["qkvf"]) as i:
                local = i + FIRST["qkvf"]

                def store(s):
                    if s % 2:
                        V.tensor_copy(qkvf[:, bass.ds((i * SLOTS + s) * T, T)],
                                      product(l, local, s)).then_inc(bank_free[s], 1)
                    mod_panel(l, i, s, GATE1 * KT + i * SLOTS + s)
                group(l, local, store)
            with dve.Fori(0, NEXT_G) as i:
                group(l, i + FIRST["gates"], lambda s: mod_panel(l, i + OWN_G, s, SHIFT1 * KT + i * SLOTS + s))
            for b in range(2):
                dve.wait_ge(mod_used[b], (l + 1) * MOD_G * 2 + 1)
            add_bias(GATE1 * KT, 4 * KT)
            make_gain(1)
            carry(dve)
            with dve.Fori(NEXT_G, COUNT["gates"]) as i:
                group(l, i + FIRST["gates"])

            for h in range(1, HEADS, 2):
                dve.wait_ge(vt_ready, l * HEADS + h + 1)
                V.tensor_copy(col(v, h), bank[4 + h % 4][:, 0:T]).then_inc(vt_dve, 1)

            def read_scores(h):
                pr, sm, bt = col(prob, h % 2, SCORES), col(softm, h % 2, 16), col(bias, h % 2, 2 * TS)
                dve.wait_ge(s_ready, l * HEADS + h + 1)
                dve.wait_ge(bias_masked, l * HEADS + h + 1)
                if h >= 2:
                    dve.wait_ge(pt_ready, l * HEADS + h - 1)
                V.tensor_scalar(pr[:, 0:TP], bank[4][:, 0:TP], SCALE, None, ALU.mult)
                for j in range(2):
                    c0, p0 = (TP if j == 0 else 0), TP + j * KEYS
                    V.scalar_tensor_tensor(pr[:, p0:p0 + TS], bank[4 + j][:, c0:c0 + TS], SCALE,
                                           col(bt, j, TS), ALU.mult, ALU.add)
                    last = V.tensor_scalar(pr[:, p0 + TS:p0 + KEYS], bank[4 + j][:, c0 + TS:c0 + KEYS], SCALE,
                                           None, ALU.mult)
                last.then_inc(s_read, 1)
                dve.wait_ge(s_read, l * HEADS + h + 1)
                V.tensor_reduce(sm[:, 0:1], pr[:, 0:TP], AX.X, ALU.max, negate=True)
                V.tensor_reduce(sm[:, 1:3], pr[:, TP:SCORES].rearrange("p (j k) -> p j k", j=2), AX.X, ALU.max,
                                negate=True).then_inc(max_ready, 1)

            read_scores(0)
            for h in range(HEADS):
                pr, sm = col(prob, h % 2, SCORES), col(softm, h % 2, 16)
                dve.wait_ge(exp_ready, l * HEADS + h + 1)
                order.step(V.reciprocal(sm[:, 8:11], sm[:, 4:7]))
                for r, (beg, end) in enumerate(((0, TP), (TP, TP + KEYS), (TP + KEYS, SCORES))):
                    last = V.tensor_scalar(pr[:, beg:end], pr[:, beg:end], sm[:, 8 + r:9 + r], None, ALU.mult)
                last.then_inc(prob_ready, 1)
                if h + 1 < HEADS:
                    read_scores(h + 1)
                local, s = FIRST["conv_out"] + h // SLOTS, h % SLOTS
                if s % 2:
                    split_panel_lo(dve, *ahead(l * GROUPS + local, s))
                V.tensor_tensor(col(gate0, h), col(gate0, h), product(l, local, s),
                                ALU.mult).then_inc(bank_free[s], 1)
                dve.wait_ge(pt_ready, l * HEADS + h + 1)
                if h >= 2:
                    dve.wait_ge(o_ready, l * HEADS + h - 1)
                V.tensor_copy(col(prob_t, h % 2, SCORES)[:, 512:SCORES], bank[7][:, 0:SCORES - 512]
                              ).then_inc(pt_dve, 1)
                dve.wait_ge(o_hi, l * HEADS + h + 1)
                V.tensor_tensor(col(h_lo, h), bank[6][:, 0:T], col(h_hi, h).bitcast(F32),
                                ALU.subtract).then_inc(o_lo, 1)

            dve.wait_ge(kv_out, (l + 1) * 32)

            def store_channels(g):
                for u in range(g * TT, (g + 1) * TT):
                    if u % 2:
                        dve.wait_ge(y1_ready, l * 12 + u + 1)
                        if g >= 2:
                            dve.wait_ge(y2_ready, l * 8 + 2 * (g - 1))
                        V.tensor_copy(col(col(fy, g % 2, TT * 512), u % TT, 512), bank[5][:, :]).then_inc(y1_dve, 1)

            def split_tokens(g):
                for u in (2 * g, 2 * g + 1):
                    dve.wait_ge(y2_hi, l * 8 + u + 1)
                    V.tensor_tensor(col(f_lo, u), bank[6 + u % 2][:, 0:T], col(f_hi, u).bitcast(F32),
                                    ALU.subtract).then_inc(y2_lo, 1)

            store_channels(0)
            for g in range(1, FG):
                store_channels(g)
                split_tokens(g - 1)
            split_tokens(FG - 1)

            for name, gate, done in (("attn_out", gate1, None), ("four_out", gate2, merged)):
                with dve.Fori(0, COUNT[name]) as i:
                    def add_branch(s):
                        n = bass.ds((i * SLOTS + s) * T, T)
                        local = i + FIRST[name]
                        V.tensor_tensor(col(branch, s), gate[:, n], product(l, local, s),
                                        ALU.mult).then_inc(bank_free[s], 1)
                        dve.wait_ge(bank_free[s], l * PROJ + local + 2)
                        last = V.tensor_tensor(gate01[:, n], gate01[:, n], col(branch, s), ALU.add)
                        if done is not None:
                            last.then_inc(done, 1)
                    group(l, i + FIRST[name], add_branch)

            def residual(xs, in_, n, which):
                for m, (beg, end) in enumerate(STREAMS):
                    g = modv[:, bass.ds(n * 2 + (which * 16 + m), 1)]
                    last = V.scalar_tensor_tensor(xs[m], in_[:, beg:end], g, xs[m], ALU.mult, ALU.add)
                return last

            with dve.Fori(0, COUNT["o"]) as i:
                def add_mixer(s):
                    n = i * SLOTS + s
                    xs = [x[:, bass.ds(n * T + beg, end - beg)] for beg, end in STREAMS]
                    residual(xs, product(l, i + FIRST["o"], s), n, GATE1).then_inc(bank_free[s], 1)
                group(l, i + FIRST["o"], add_mixer)

            norm(2 * l + 2)
            modulate(l, 1)

            with dve.Fori(0, COUNT["pq"]) as i:
                steps = SLOTS * TT * 3 + 2
                inner = order.enter(i, 0, steps)

                def rank(s):
                    n = (l * COUNT["pq"] + i) * SLOTS + s
                    dve.wait_ge(sc_ready, n + 1 + 4)
                    carry(dve)
                    vs = [col(val, s * TT + t, TOPK) for t in range(TT)]
                    ix = [col(idx, s * TT + t, TOPK) for t in range(TT)]
                    ss = [col(col(sc, s), t, NK) for t in range(TT)]
                    s2 = [col(sc2, t, NK) for t in range(TT)]
                    for t in range(TT):
                        order.step(V.max(vs[t][:, 0:8], ss[t]), wait=(t == TT - 1), hold=True)
                    for t in range(TT):
                        V.max_index(ix[t][:, 0:8], vs[t][:, 0:8], ss[t])
                        order.step(V.match_replace(s2[t], vs[t][:, 0:8], ss[t], LOWEST), wait=(t == TT - 1), hold=True)
                    for t in range(TT):
                        order.step(V.max(vs[t][:, 8:16], s2[t]), wait=(t == TT - 1), hold=True)
                    for t in range(TT):
                        last = V.max_index(ix[t][:, 8:16], vs[t][:, 8:16], s2[t])
                    last.then_inc(sc_used, 1)
                group(l, i + FIRST["pq"], rank)
                dve.wait_ge(sc_used, (l * COUNT["pq"] + i + 1) * SLOTS + 4)
                for dst, src in ((vals, val), (idxs, idx)):
                    out = dst[:, :].rearrange("p (t h r) -> p h t r", t=TT, r=TOPK)[:, bass.ds(i * SLOTS, SLOTS), :, :]
                    order.step(V.tensor_copy(out, src[:, :].rearrange("p (h t r) -> p h t r", h=SLOTS, r=TOPK)))
                order.leave(inner, COUNT["pq"], steps)

            with dve.Fori(0, TT) as t:
                steps = 44
                inner = order.enter(t, 0, steps)
                width = 2 * PH * TOPK
                vt = vals[:, bass.ds(t * width, width)].rearrange("p (h c r) -> p h c r", h=PH, c=2)
                it = idxs[:, bass.ds(t * width, width)].rearrange("p (h c r) -> p h c r", h=PH, c=2)
                grid = [P, PH, TOPK, TOPK]
                order.step(V.tensor_tensor(cand[:, :].rearrange("p (h a b) -> p h a b", h=PH, a=TOPK),
                                           vt[:, :, 0, :].unsqueeze(3).broadcast_to(grid),
                                           vt[:, :, 1, :].unsqueeze(2).broadcast_to(grid), ALU.add), hold=True)
                n2 = TOPK * TOPK
                for r in range(2):
                    src = cand if r == 0 else cand2
                    for h in range(PH):
                        order.step(V.max(col(best, h, TOPK)[:, 8 * r:8 * r + 8], col(src, h, n2)), wait=(h == PH - 1), hold=True)
                    for h in range(PH):
                        b8, c = col(best, h, TOPK)[:, 8 * r:8 * r + 8], col(src, h, n2)
                        ins = V.max_index(col(pos, h, TOPK)[:, 8 * r:8 * r + 8], b8, c)
                        if r == 0:
                            ins = V.match_replace(col(cand2, h, n2), b8, c, LOWEST)
                        order.step(ins, wait=(h == PH - 1), hold=True)
                b3 = best[:, :].rearrange("p (h r) -> p h r", h=PH)
                order.step(V.tensor_copy(gsum[:, 0:PH], b3[:, :, 0]))
                V.tensor_tensor(b3, b3, gsum[:, 0:PH].unsqueeze(2).broadcast_to([P, PH, TOPK]),
                                ALU.subtract).then_inc(top_shifted, 1)
                V.tensor_scalar(pos_ab[:, 0:HK], pos[:, :], 4, None, ALU.logical_shift_right)
                order.step(V.tensor_scalar(pos_ab[:, HK:2 * HK], pos[:, :], 15, None, ALU.bitwise_and))
                order.step(V.tensor_copy(pos_f[:, :], pos_ab[:, :]))
                eq3 = [col(eq, c, HK * TOPK).rearrange("p (n j) -> p n j", j=TOPK) for c in range(2)]
                for c in range(2):
                    order.step(V.tensor_tensor(eq3[c], col(pos_f, c, HK).unsqueeze(2).broadcast_to([P, HK, TOPK]),
                                               iota[:, 0:TOPK].unsqueeze(1).broadcast_to([P, HK, TOPK]),
                                               ALU.is_equal), wait=(c == 1))
                for c in range(2):
                    e4 = col(eq, c, HK * TOPK).rearrange("p (h k j) -> p h k j", h=PH, k=TOPK)
                    order.step(V.tensor_tensor(e4, e4, it[:, :, c, :].unsqueeze(2).broadcast_to(grid), ALU.mult),
                               wait=(c == 1))
                dve.wait_ge(route_tr, l * TT + t + 1)
                for c in range(2):
                    V.tensor_reduce(col(route, c, HK), eq3[c], AX.X, ALU.add)
                dve.wait_ge(top_exp, l * TT + t + 1)
                order.step(V.tensor_reduce(gsum[:, 0:PH], b3, AX.X, ALU.add))
                order.step(V.reciprocal(gsum[:, PH:2 * PH], gsum[:, 0:PH]))
                V.tensor_tensor(col(route, 2, HK).rearrange("p (h r) -> p h r", h=PH), b3,
                                gsum[:, PH:2 * PH].unsqueeze(2).broadcast_to([P, PH, TOPK]),
                                ALU.mult).then_inc(route_ready, 1)
                dve.wait_ge(gate_hi, l * TT + t + 1)
                g1, g2, g3 = [gate_t[:, bass.ds(t * P + c * T, P)] for c in range(PARTS)]
                order.step(V.tensor_tensor(rest[:, :], col(bank[4], 2, P), g1, ALU.subtract))
                order.step(V.tensor_copy(g2, rest[:, :]))
                V.tensor_tensor(g3, rest[:, :], g2, ALU.subtract).then_inc(route_done, 1)
                order.leave(inner, TT, steps)

            dve.wait_ge(route_done, (l + 1) * TT + 1)

            def one_hots(chunk, t0, batches):
                for r in batches:
                    n = (l * CHUNKS + chunk) * NB + t0 + r
                    dve.wait_ge(gate_mm, n + 1)
                    at = (t0 + r) * BATCH
                    for out, w, row, c0, done in ((eq1, CHUNK, 0, chunk * CHUNK, eq_ready),
                                                  (hot2, P, 1, 0, hot2_ready)):
                        shape = [P, BATCH, w]
                        V.tensor_tensor(col(out, r, BATCH * w).rearrange("p (t j) -> p t j", j=w),
                                        iota[:, c0:c0 + w].unsqueeze(1).broadcast_to(shape),
                                        route_t[:, bass.ds(at + row * T, BATCH)].unsqueeze(2).broadcast_to(shape),
                                        ALU.is_equal).then_inc(done, 1)

            peer = l * GROUPS + FIRST["peer"]

            def gated(i, b, chunk):
                j = l * NK + 2 * i + b
                dve.wait_ge(gelu_ready, j + 1)
                dve.wait_ge(ahi_ready, j + 1)
                at = (2 * i + (b + (chunk % 2 - chunk) * CHUNK)) * T
                V.tensor_tensor(col(act_f, b), col(gel, b), gates[:, bass.ds(at, T)],
                                ALU.mult).then_inc(act_ready, 1)
                dve.wait_ge(ahi_ready, j + 1 + 2)
                V.tensor_tensor(col(a_lo, b), col(act_f, b), col(a_hi, b).bitcast(F32),
                                ALU.subtract).then_inc(alo_ready, 1)

            def pair(i, chunk, last=False):
                t0 = (i - chunk * PAIRS) * PER_PAIR
                build = chunk + 1 < CHUNKS
                gated(i, 0, chunk)
                if build:
                    one_hots(chunk + 1, t0, (0, 1))
                split_panel_lo(dve, peer + i, 3)
                gated(i, 1, chunk)
                if build:
                    one_hots(chunk + 1, t0, (2,))
                if not last:
                    split_panel_lo(dve, peer + i + 1, 1)

            carry(dve)
            with dve.Fori(0, PAIRS) as i:
                one_hots(0, i * PER_PAIR, (0, 1, 2))
            for chunk in range(CHUNKS):
                dve.wait_ge(gate_copied, (l * CHUNKS + chunk + 1) * NB + 1)
                carry(dve)
                with dve.Fori(chunk * PAIRS, (chunk + 1) * PAIRS - (chunk == CHUNKS - 1)) as i:
                    pair(i, chunk)
            pair(LAST_PAIR, CHUNKS - 1, last=True)

            dve.wait_ge(panel_used[1], after_use(peer + LAST_PAIR, 3))
            for t in range(TT):
                V.tensor_copy(col(y_nat, 2 * t + 1, 512), bank[3 + 2 * t][:, :]).then_inc(y_dve, 1)
            for kk in range(KT):
                dve.wait_ge(yt_ready, l * KT + kk + 1)
                xs = [col(x, kk)[:, beg:end] for beg, end in STREAMS]
                for m, (beg, end) in enumerate(STREAMS):
                    c = (GATE2 * KT + kk) * 2 + m
                    last = V.scalar_tensor_tensor(xs[m], bank[kk % 2][:, beg:end], modv[:, c:c + 1], xs[m],
                                                  ALU.mult, ALU.add)
                last.then_inc(x_updated, 1)
            order.leave(layer, DEPTH, LAYER_STEPS)

        norm(2 * DEPTH + 1)
        V.tensor_tensor(hf[:, :].rearrange("p (k t) -> p k t", k=KT), hf[:, :].rearrange("p (k t) -> p k t", k=KT),
                        gfin[:, :].unsqueeze(2).broadcast_to([P, KT, T]), ALU.mult).then_inc(out_ready, 1)

    block_cm.__exit__(None, None, None)


def kernel(**inputs):
    import numpy as np
    import concourse.bacc as bacc
    from concourse import mybir as _mybir
    from concourse.bass_utils import run_bass_kernel_spmd

    a = {name: np.asarray(value) for name, value in inputs.items()}

    def features_first(t):
        n = t.shape[0]
        return t.reshape(n, KT, P).transpose(2, 1, 0).reshape(P, KT * n)

    def columns(w):
        n = w.shape[1]
        return w.reshape(KT, P, n // P, P).transpose(2, 1, 0, 3).reshape(n // P, P, D)

    panels = np.empty((DEPTH * GROUPS * SLOTS, P, D), np.float32)
    w_mod = a["w_mod"].reshape(DEPTH, D, N_MOD * KT, P).transpose(0, 2, 3, 1)
    blocks = [w_mod[0, :2 * KT]]
    for l in range(DEPTH):
        blocks += [w_mod[l, 2 * KT:], w_mod[(l + 1) % DEPTH, :2 * KT]]
    mod_panels = np.concatenate(blocks)
    for l in range(DEPTH):
        w_in = columns(a["w_in"][l]).reshape(10, KT, P, D)
        cb, cc, cx, q, k, v, f, g0, g1, g2 = w_in
        u = a["peer_u"][l].reshape(NK, P, KT, P).transpose(0, 3, 2, 1).reshape(NK, P, D)
        vv = a["peer_v"][l].reshape(NK, P, D)
        uv = np.empty((2 * NK, P, D), np.float32)
        uv[0] = u[0]
        uv[1:2 * NK - 2:2] = u[1:]
        uv[2:2 * NK - 1:2] = vv[:-1]
        uv[2 * NK - 1] = vv[NK - 1]
        parts = (np.stack([cc, cx], 1).reshape(2 * KT, P, D), cb,
                 np.concatenate([q, k, v, f]), np.concatenate([g0, g1, g2]), columns(a["w_conv_out"][l]),
                 columns(a["w_attn_out"][l]), columns(a["w_four_out"][l]), columns(a["w_o"][l]),
                 columns(a["w_pq"][l]), uv)
        at = l * GROUPS * SLOTS
        for part in parts:
            panels[at:at + len(part)] = part
            at += len(part)

    def per_feature(t):
        return t.reshape(-1, KT, P).transpose(2, 0, 1).reshape(P, -1)

    vecs = np.stack([np.concatenate([per_feature(a["b_mod"][l].reshape(N_MOD, D)), per_feature(a["g_mix"][l][None]),
                                     per_feature(a["g_ffn"][l][None]), per_feature(a["conv_w"][l])], 1)
                     for l in range(DEPTH)])
    rows = TS // GRID_W
    dr = np.arange(rows)[None, :] - np.arange(rows)[:, None] + 7
    dc = np.arange(GRID_W)[None, :] - np.arange(GRID_W)[:, None] + WIN - 1
    padded = np.zeros(a["rpb"].shape[:3] + (2 * WIN,), np.float32)
    padded[..., :2 * WIN - 1] = a["rpb"]
    dc = np.where((dc < 0) | (dc > 2 * WIN - 2), 2 * WIN - 1, dc)
    table = padded[:, :, dr[:, None, :, None], dc[None, :, None, :]]
    table = table.reshape(DEPTH * HEADS, 2, P, TS).transpose(0, 2, 1, 3).reshape(DEPTH * HEADS, P, 2 * TS)
    c = np.arange(GRID_W)
    c0 = np.clip(c - WIN // 2, 0, GRID_W - WIN)
    window = np.where((c[None, :] >= c0[:, None]) & (c[None, :] < c0[:, None] + WIN), 0.0, -1e30)
    window = np.concatenate([window, window]).astype(np.float32)

    def transform(n):
        angle = 2 * np.pi * (np.outer(np.arange(n), np.arange(n)) % n) / n
        return np.cos(angle) / np.sqrt(n), np.sin(angle) / np.sqrt(n)

    cd, sd = transform(FD)
    cp, s_p = transform(TP)
    cs, ss = transform(TS)
    two = lambda m, w: m.reshape(2, P, w).transpose(1, 0, 2).reshape(P, 2 * w)
    tables = np.concatenate([two(np.concatenate([cd, sd], 1), 512), cp, -s_p,
                             two(np.concatenate([cs, -ss], 1), 2 * TS)], 1).astype(np.float32)

    ins = {
        "panels": panels,
        "mod_panels": mod_panels,
        "x_in": features_first(np.concatenate([a["x_prompt"][0], a["x_sample"][0]])),
        "c_in": np.concatenate([a["c_ctx"], a["c"][0]])[None],
        "vecs": vecs,
        "g_final": per_feature(a["g_final"][None]),
        "k_cache": a["cache_k"][0].transpose(0, 3, 2, 1).reshape(DEPTH, DH, HEADS * CTX),
        "v_cache": a["cache_v"][0].reshape(DEPTH, CTX, HEADS * DH),
        "bias_in": table,
        "mask_in": window,
        "dft_in": tables,
        "sub_keys": a["sub_keys"].transpose(0, 4, 1, 2, 3).reshape(DEPTH, P, 2 * PH * NK),
        "ident_in": np.eye(P, dtype=np.float32),
        "iota_in": np.tile(np.arange(P, dtype=np.float32), (P, 1)),
    }
    outs = {"y_out": (P, KT * T), "new_k": (DEPTH, DH, HEADS, TP), "new_v": (DEPTH, TP, HEADS, DH)}
    nc = bacc.Bacc("TRN2", target_bir_lowering=False, num_devices=1, dynamic_dma_scratch_size=1024)
    ins = {name: np.ascontiguousarray(value) for name, value in ins.items()}
    aps = {name: nc.dram_tensor(name, value.shape, _mybir.dt.float32, kind="ExternalInput").ap()
           for name, value in ins.items()}
    aps |= {name: nc.dram_tensor(name, shape, _mybir.dt.float32, kind="ExternalOutput").ap()
            for name, shape in outs.items()}
    build(nc, **aps)
    got = run_bass_kernel_spmd(nc, [ins], core_ids=[0]).results[0]
    y = got["y_out"].reshape(P, KT, T).transpose(2, 1, 0).reshape(T, D)
    new_k = got["new_k"].transpose(0, 3, 2, 1)[None]
    return y[None, :TP], y[None, TP:], new_k, got["new_v"][None]
```

```python
import concourse.bass as bass
import concourse.mybir as mybir

F32 = mybir.dt.float32
F32R = mybir.dt.float32r
BF16 = mybir.dt.bfloat16
U32 = mybir.dt.uint32
ALU = mybir.AluOpType
ACT = mybir.ActivationFunctionType
AX = mybir.AxisListType

DEPTH = 2
P = 128
D = 1024
KT = D // P
TP, TS = 128, 256
T = TP + TS
TT = T // P
STREAMS = ((0, TP), (TP, T))
HEADS = 8
DH = 128
CTX = 128
GRID_W = 64
WIN = 16
SCALE = DH ** -0.5
KEYS = TS + CTX
SCORES = TP + 2 * KEYS
PH = 8
NK = 128
TOPK = 16
HK = PH * TOPK
EPS = 1e-6
LOWEST = -3.0e38
N_MOD = 6
SHIFT1, SCALE1, GATE1, SHIFT2, SCALE2, GATE2 = range(N_MOD)
FG, FD = 4, 256

SLOTS = 4
OWN_G, NEXT_G = 4 * KT // SLOTS, 2 * KT // SLOTS
MOD_G = OWN_G + NEXT_G
_groups = (("ccx", 2 * KT), ("cb", KT), ("qkvf", 4 * KT), ("gates", 3 * KT),
           ("conv_out", KT), ("attn_out", KT), ("four_out", KT), ("o", KT), ("pq", 2 * PH),
           ("peer", 2 * NK))
FIRST, COUNT, _at = {}, {}, 0
for _name, _panels in _groups:
    FIRST[_name], COUNT[_name] = _at, _panels // SLOTS
    _at += _panels // SLOTS
GROUPS = _at
PROJ = FIRST["peer"]

CHUNKS = 4
CHUNK = NK // CHUNKS
PAIRS = CHUNK // 2
BATCH = 8
PER_PAIR = 3
NB = T // BATCH
LAST_PAIR = NK // 2 - 1
EARLY_G = 1 + TT
EARLY = EARLY_G * SLOTS
PARTS = 3
assert NB == PAIRS * PER_PAIR and EARLY == CHUNK // 2

B_MOD, G_MIX, G_FFN, CONV_W = 0, N_MOD * KT, N_MOD * KT + KT, N_MOD * KT + 2 * KT
VEC = CONV_W + 3 * KT
PAD = T + 4
SEG = ((1, 1 + TP), (3 + TP, 3 + T))
DFT_CH, DFT_P, DFT_S = 0, 2 * 512, 2 * 512 + 2 * TP
DFT = DFT_S + 2 * 2 * TS


def build(nc, panels, mod_panels, x_in, c_in, vecs, g_final, k_cache, v_cache, bias_in, mask_in, dft_in,
          sub_keys, ident_in, iota_in, y_out, new_k, new_v):
    base = 1152

    def place(name, where, cols, dt=F32):
        size = 2 if dt == BF16 else 4
        return nc.alloc_sbuf_tensor_at(name, [P, cols], dt, offset=where), where + size * cols

    raw, o = place("raw", base, SLOTS * D)
    split_hi, o = place("split_hi", o, 2 * D, F32R)
    split_lo, o = place("split_lo", o, 2 * D, F32R)
    h_hi, o = place("h_hi", o, KT * T, F32R)
    h_lo, o = place("h_lo", o, KT * T, F32R)
    x, o = place("x", o, KT * T)
    ident, o = place("ident", o, P)
    iota, o = place("iota", o, P)
    ones, o = place("ones", o, P)
    mask, o = place("mask", o, GRID_W)
    vec, o = place("vec", o, DEPTH * VEC)
    modv, o = place("modv", o, N_MOD * KT * 2)
    gain, o = place("gain", o, 2 * KT * 2)
    gfin, o = place("gfin", o, KT)
    softm, o = place("softm", o, 2 * 16)
    arena = o

    qkvf, o = place("qkvf", arena, 4 * KT * T)
    q, k, v, f = (qkvf[:, i * KT * T:(i + 1) * KT * T] for i in range(4))
    gate01, o = place("gate01", o, 2 * KT * T)
    gate0, gate1 = gate01[:, 0:KT * T], gate01[:, KT * T:2 * KT * T]
    gate2_at = o
    gate2, _ = place("gate2", o, KT * T)
    conv, o = place("conv", o, KT * PAD)
    u_hi, o = place("u_hi", o, KT * T, F32R)
    u_lo, o = place("u_lo", o, KT * T, F32R)
    bias, o = place("bias", o, 2 * 2 * TS)
    kc_at = o
    kc, o = place("kc", o, HEADS * CTX)
    vc, o = place("vc", o, HEADS * DH)
    prob_at = o
    prob, o = place("prob", o, 2 * SCORES)
    prob_t, o = place("prob_t", o, 2 * SCORES)
    dft, o = place("dft", o, DFT)
    silu_c, mixer_end = place("silu_c", o, 2 * D)
    cc_s, o = place("cc_s", prob_at, 2 * T)
    ccx, o = place("ccx", o, 2 * PAD)
    cb_s, o = place("cb_s", o, 2 * T)
    waste, _ = place("waste", o, 2 * D, BF16)
    mod_raw, _ = place("mod_raw", kc_at, 2 * D)
    waste0, _ = place("waste0", gate2_at, SLOTS * D, BF16)
    branch, _ = place("branch", prob_at, SLOTS * T)
    f_hi, o = place("f_hi", arena, KT * T, F32R)
    f_lo, o = place("f_lo", o, KT * T, F32R)
    fy, _ = place("fy", o, 2 * TT * 512)
    sq, o = place("sq", arena + 4 * TT * D, KT * T)
    hf, o = place("hf", o, KT * T)
    ms, o = place("ms", o, T)
    rstd, _ = place("rstd", o, T)
    gates, o = place("gates", arena, 2 * CHUNK * T)
    gates_end = o
    gel, o = place("gel", o, 2 * T)
    act_f, o = place("act_f", o, 2 * T)
    a_hi, o = place("a_hi", o, 2 * T, F32R)
    a_lo, o = place("a_lo", o, 2 * T, F32R)
    hot2, o = place("hot2", o, PER_PAIR * BATCH * P, BF16)
    eq1, o = place("eq1", o, PER_PAIR * BATCH * CHUNK, BF16)
    hot1, o = place("hot1", o, PER_PAIR * BATCH * PARTS * CHUNK, BF16)
    index, o = place("index", o, BATCH * P, BF16)
    route_t, o = place("route_t", o, 2 * T, BF16)
    gate_t, o = place("gate_t", o, PARTS * T, BF16)
    subk, peer_end = place("subk", o, 2 * PH * NK)
    y_nat, _ = place("y_nat", arena, TT * D)
    pq, o = place("pq", arena, SLOTS * T)
    sc, o = place("sc", o, SLOTS * TT * NK)
    sc2, o = place("sc2", o, TT * NK)
    val, o = place("val", o, SLOTS * TT * TOPK)
    idx, o = place("idx", o, SLOTS * TT * TOPK, U32)
    vals, o = place("vals", o, TT * 2 * PH * TOPK)
    idxs, o = place("idxs", o, TT * 2 * PH * TOPK)
    cand, o = place("cand", o, PH * TOPK * TOPK)
    cand2, o = place("cand2", o, PH * TOPK * TOPK)
    best, o = place("best", o, HK)
    pos, o = place("pos", o, HK, U32)
    pos_ab, o = place("pos_ab", o, 2 * HK, U32)
    pos_f, o = place("pos_f", o, 2 * HK)
    eq, o = place("eq", o, 2 * HK * TOPK)
    route, o = place("route", o, 3 * HK)
    gsum, o = place("gsum", o, 2 * PH)
    rest, o = place("rest", o, P)
    gel_early, o = place("gel_early", o, EARLY * T)
    assert o <= gates_end and max(mixer_end, peer_end) <= 229344

    bank = [nc.alloc_psum_tensor(f"bank{i}", [P, 512], F32) for i in range(8)]

    sem = nc.alloc_semaphore
    consts_loaded = sem("consts_loaded")
    first_loaded = [sem(f"first_loaded{s}") for s in range(SLOTS)]
    first_used = [sem(f"first_used{s}") for s in range(SLOTS)]
    mod_loaded = [sem(f"mod_loaded{b}") for b in range(2)]
    mod_used = [sem(f"mod_used{b}") for b in range(2)]
    kv_loaded = sem("kv_loaded")
    c_loaded = sem("c_loaded")
    panel_loaded = [sem(f"panel_loaded{s}") for s in range(SLOTS)]
    hi_ready = [sem(f"hi_ready{s}") for s in range(SLOTS)]
    lo_ready = [sem(f"lo_ready{s}") for s in range(SLOTS)]
    panel_used = [sem(f"panel_used{b}") for b in range(2)]
    bank_free = [sem(f"bank_free{s}") for s in range(SLOTS)]
    dft_loaded = sem("dft_loaded")
    sub_loaded = sem("sub_loaded")
    bias_loaded = [sem("bias_loaded0"), sem("bias_loaded1")]
    bias_masked = sem("bias_masked")
    ones_ready = sem("ones_ready")
    c_ready = sem("c_ready")
    squares = sem("squares")
    sums = sem("sums")
    mean_sq = sem("mean_sq")
    root = sem("root")
    hf_ready = sem("hf_ready")
    hhi_ready = sem("hhi_ready")
    hlo_ready = sem("hlo_ready")
    uhi_ready = sem("uhi_ready")
    ulo_ready = sem("ulo_ready")
    vt_ready = sem("vt_ready")
    vt_act = sem("vt_act")
    vt_dve = sem("vt_dve")
    kv_out = sem("kv_out")
    s_ready = sem("s_ready")
    s_read = sem("s_read")
    max_ready = sem("max_ready")
    exp_ready = sem("exp_ready")
    prob_ready = sem("prob_ready")
    pt_ready = sem("pt_ready")
    pt_act = sem("pt_act")
    pt_dve = sem("pt_dve")
    o_ready = sem("o_ready")
    o_hi = sem("o_hi")
    o_lo = sem("o_lo")
    y1_ready = sem("y1_ready")
    y1_act = sem("y1_act")
    y1_dve = sem("y1_dve")
    y2_ready = sem("y2_ready")
    y2_hi = sem("y2_hi")
    y2_lo = sem("y2_lo")
    merged = sem("merged")
    mhi_ready = sem("mhi_ready")
    mlo_ready = sem("mlo_ready")
    keys_done = sem("keys_done")
    sc_ready = sem("sc_ready")
    sc_used = sem("sc_used")
    top_shifted = sem("top_shifted")
    top_exp = sem("top_exp")
    route_ready = sem("route_ready")
    route_tr = sem("route_tr")
    route_done = sem("route_done")
    gate_hi = sem("gate_hi")
    eq_ready = sem("eq_ready")
    hot2_ready = sem("hot2_ready")
    hot1_ready = [sem(f"hot1_ready{r}") for r in range(PER_PAIR)]
    gate_mm = sem("gate_mm")
    gate_copied = sem("gate_copied")
    gelu_ready = sem("gelu_ready")
    act_ready = sem("act_ready")
    ahi_ready = sem("ahi_ready")
    alo_ready = sem("alo_ready")
    y_act = sem("y_act")
    y_dve = sem("y_dve")
    yt_ready = sem("yt_ready")
    x_updated = sem("x_updated")
    out_ready = sem("out_ready")
    out_done = sem("out_done")
    carried = sem("carried")
    dve_seq = sem("dve_seq")
    CONSTS = 6

    class Order:

        def __init__(self):
            self.base, self.n = 0, 0

        def step(self, ins, wait=True, hold=False):
            ins.then_inc(dve_seq, 1)
            self.n += 1
            if wait:
                self.wait()
                if hold:
                    carry(nc.vector)

        def wait(self):
            nc.vector.wait_ge(dve_seq, self.base + self.n)

        def enter(self, i, start, steps):
            saved = self.base, self.n
            self.base, self.n = self.base + self.n + (i - start) * steps, 0
            return saved

        def leave(self, saved, turns, steps):
            assert self.n == steps, f"{self.n} steps in a loop's body, not {steps}"
            self.base, self.n = saved[0], saved[1] + turns * steps

    def col(t, n, width=T):
        return t[:, n * width:(n + 1) * width]

    def ahead(g, s):
        return (g, s + 2) if s < 2 else (g + 1, s - 2)

    def after_use(g, s):
        return 2 * g + s // 2 + 2

    def wait_split(eng, g, s):
        eng.wait_ge(panel_loaded[s], (g + 1) * 16)
        eng.wait_ge(panel_used[s % 2], after_use(g, s) - 1)

    def split_panel_hi(g, s):
        wait_split(nc.scalar, g, s)
        nc.scalar.activation(col(split_hi, s % 2, D), col(raw, s, D), ACT.Copy).then_inc(hi_ready[s], 1)

    def split_panel_lo(eng, g, s):
        wait_split(eng, g, s)
        eng.wait_ge(hi_ready[s], g + 2)
        eng.tensor_tensor(col(split_lo, s % 2, D), col(raw, s, D), col(split_hi, s % 2, D).bitcast(F32),
                          ALU.subtract).then_inc(lo_ready[s], 1)

    def carry(eng):
        eng.sem_inc(carried, 1)

    def wait_stored(eng, l, name):
        for s in range(SLOTS):
            eng.wait_ge(bank_free[s], l * PROJ + FIRST[name] + 1)

    def pairs_of(chunk):
        return (EARLY // 2 if chunk == 0 else chunk * PAIRS,
                LAST_PAIR if chunk == CHUNKS - 1 else (chunk + 1) * PAIRS)

    def plan(i, chunk):
        if chunk == CHUNKS - 1:
            return (None,) * 4
        turn = i - chunk * PAIRS
        if chunk == 0:
            turn = (i - EARLY // 2) * 2
            return (turn, (0, 1)), (turn, (2,)), (turn + 1, (0, 1)), (turn + 1, (2,))
        return None, (turn, (0, 1)), (turn, (2,)), None

    def by_vector(chunk, r):
        return r <= chunk < 2

    def gate_products(eng, l, chunk, turn, r):
        n = (l * CHUNKS + chunk) * NB + turn * PER_PAIR + r
        eng.wait_ge(eq_ready, n + 1)
        eng.wait_ge(gate_mm, n + 1)
        shape = [P, PARTS, CHUNK, BATCH]
        tokens = bass.ds(turn * (PER_PAIR * BATCH) + r * BATCH, BATCH)
        eng.tensor_tensor(col(hot1, r, BATCH * PARTS * CHUNK).rearrange("p (c j t) -> p c j t", c=PARTS, t=BATCH),
                          col(eq1, r, BATCH * CHUNK).rearrange("p (j t) -> p j t", t=BATCH)
                          .unsqueeze(1).broadcast_to(shape),
                          gate_t[:, :].rearrange("p (c t) -> p c t", c=PARTS)[:, :, tokens]
                          .unsqueeze(2).broadcast_to(shape), ALU.mult).then_inc(hot1_ready[r], 1)

    block_cm = nc.Block()
    block = block_cm.__enter__()

    @block.sync
    def _(sp):
        sp.dma_start(silu_c[:, :], c_in.broadcast_to([P, 2 * D])).then_inc(c_loaded, 16)
        for s in range(SLOTS):
            sp.dma_start(col(raw, s, D), mod_panels[s, :, :]).then_inc(first_loaded[s], 16)
        for dst, src in ((x, x_in), (ident, ident_in), (iota, iota_in), (mask, mask_in), (gfin, g_final),
                         (vec, vecs)):
            sp.dma_start(dst[:, :], src).then_inc(consts_loaded, 16)
        with sp.Fori(1, NEXT_G) as i:
            for s in range(SLOTS):
                sp.wait_ge(first_used[s], i)
                sp.dma_start(col(raw, s, D), mod_panels[i * SLOTS + s, :, :]).then_inc(first_loaded[s], 16)
        for s in range(SLOTS):
            sp.wait_ge(first_used[s], NEXT_G)

        def load_panel(g, s):
            sp.wait_ge(hi_ready[s], g + 1)
            sp.wait_ge(lo_ready[s], g + 1)
            sp.dma_start(col(raw, s, D), panels[g * SLOTS + s, :, :]).then_inc(panel_loaded[s], 16)

        with sp.Fori(0, DEPTH) as l:
            mod_from = FIRST["qkvf"] + 1
            with sp.Fori(0, mod_from) as i:
                for s in range(SLOTS):
                    load_panel(l * GROUPS + i, s)
            with sp.Fori(0, MOD_G) as i:
                for s in range(SLOTS):
                    load_panel(l * GROUPS + mod_from + i, s)
                    b, n = s % 2, l * MOD_G + i
                    sp.wait_ge(mod_used[b], n * 2 + s // 2 + 1)
                    sp.dma_start(col(mod_raw, b, D), mod_panels[(n + NEXT_G) * SLOTS + s, :, :]
                                 ).then_inc(mod_loaded[b], 16)
            with sp.Fori(mod_from + MOD_G, GROUPS) as i:
                for s in range(SLOTS):
                    load_panel(l * GROUPS + i, s)
        for part in range(2):
            sp.wait_ge(out_ready, (part + 1) * KT // 2)
            half = slice(part * KT // 2 * T, (part + 1) * KT // 2 * T)
            sp.dma_start(y_out[:, half], hf[:, half]).then_inc(out_done, 16)
        sp.wait_ge(out_done, 2 * 16)
        sp.wait_ge(kv_out, DEPTH * 32)

    @block.tensor
    def _(pe):
        mm = nc.tensor.matmul
        transpose = lambda out, in_: nc.tensor.transpose(out, in_, ident[:, :])

        def panel(g, s, out, rhs_hi, rhs_lo, n, arriving=None):
            pe.wait_ge(hi_ready[s], g + 2)
            pe.wait_ge(lo_ready[s], g + 2)
            for kk in range(KT):
                if arriving:
                    pe.wait_ge(arriving[0], arriving[1] + kk + 1)
                w_hi, w_lo = col(col(split_hi, s % 2, D), kk, P), col(col(split_lo, s % 2, D), kk, P)
                mm(out, w_hi, col(rhs_hi, kk, n), start=(kk == 0), stop=False)
                mm(out, w_hi, col(rhs_lo, kk, n), start=False, stop=False)
                last = mm(out, w_lo, col(rhs_hi, kk, n), start=False, stop=(kk == KT - 1))
            last.then_inc(panel_used[s % 2], 1)

        def project(l, local, s, rhs_hi, rhs_lo, n=T, arriving=None):
            pe.wait_ge(bank_free[s], l * PROJ + local + 1)
            panel(l * GROUPS + local, s, bank[s][:, 0:n], rhs_hi, rhs_lo, n, arriving)

        def stage(l, name, rhs_hi, rhs_lo, n=T, arriving=None):
            carry(pe)
            with pe.Fori(0, COUNT[name]) as i:
                for s in range(SLOTS):
                    project(l, i + FIRST[name], s, rhs_hi, rhs_lo, n, arriving if s == 0 else None)

        def add_squares(n, kk):
            pe.wait_ge(squares, (n - 1) * KT + kk + 1)
            last = mm(bank[4][:, 0:T], ones[:, :], col(sq, kk), start=(kk == 0), stop=(kk == KT - 1))
            if kk == KT - 1:
                last.then_inc(sums, 1)

        pe.sem_inc(panel_used[0], 1)
        pe.sem_inc(panel_used[1], 1)
        pe.sem_inc(keys_done, 4)
        pe.sem_inc(route_tr, 1)
        pe.sem_inc(gate_mm, PER_PAIR)
        pe.wait_ge(ones_ready, 1)
        pe.wait_ge(consts_loaded, CONSTS * 16)
        for kk in range(KT):
            add_squares(1, kk)
        with pe.Fori(0, DEPTH) as l:
            for name in ("ccx", "cb", "qkvf", "gates"):
                stage(l, name, h_hi, h_lo, arriving=(hlo_ready, l * 16) if name == "ccx" else None)

            wait_stored(pe, l, "conv_out")
            for h in range(HEADS):
                if h >= 4:
                    pe.wait_ge(vt_dve if h % 2 else vt_act, l * 4 + h // 2 - 1)
                for t in range(TT):
                    last = transpose(bank[4 + h % 4][:, t * P:(t + 1) * P], col(v, h)[:, t * P:(t + 1) * P])
                last.then_inc(vt_ready, 1)
            pe.wait_ge(vt_act, l * 4 + 4)
            pe.wait_ge(vt_dve, l * 4 + 4)
            pe.wait_ge(kv_loaded, (l + 1) * 2 * 16)

            def scores(h):
                if h >= 1:
                    pe.wait_ge(s_read, l * HEADS + h)
                qh, kh = col(q, h), col(k, h)
                mm(bank[4][:, 0:TP], qh[:, 0:TP], kh[:, 0:TP], start=True, stop=True)
                for j in range(2):
                    qt = qh[:, TP + j * P:TP + (j + 1) * P]
                    c0 = TP if j == 0 else 0
                    mm(bank[4 + j][:, c0:c0 + TS], qt, kh[:, TP:T], start=True, stop=True)
                    last = mm(bank[4 + j][:, c0 + TS:c0 + KEYS], qt, col(kc, h, CTX), start=True, stop=True)
                last.then_inc(s_ready, 1)

            scores(0)
            for h in range(HEADS):
                if h + 1 < HEADS:
                    scores(h + 1)
                if h == 0:
                    pe.wait_ge(uhi_ready, (l + 1) * KT)
                    pe.wait_ge(ulo_ready, (l + 1) * KT + 2)
                project(l, FIRST["conv_out"] + h // SLOTS, h % SLOTS, u_hi, u_lo)
                pr, pt, vh = col(prob, h % 2, SCORES), col(prob_t, h % 2, SCORES), col(v, h)
                pe.wait_ge(prob_ready, l * HEADS + h + 1)
                if h >= 1:
                    pe.wait_ge(o_lo, l * HEADS + h)
                for kt in range(3):
                    for j in range(2):
                        c0 = kt * TS + j * P
                        transpose(bank[6 + c0 // 512][:, c0 % 512:c0 % 512 + P],
                                  pr[:, TP + j * KEYS + kt * P:TP + j * KEYS + (kt + 1) * P])
                transpose(bank[7][:, TS:TS + P], pr[:, 0:TP]).then_inc(pt_ready, 1)
                pe.wait_ge(pt_act, l * HEADS + h + 1)
                pe.wait_ge(pt_dve, l * HEADS + h + 1)
                mm(bank[6][:, 0:TP], vh[:, 0:P], pt[:, 3 * TS:3 * TS + TP], start=True, stop=True)
                mm(bank[6][:, TP:T], vh[:, P:2 * P], pt[:, 0:TS], start=True, stop=False)
                mm(bank[6][:, TP:T], vh[:, 2 * P:3 * P], pt[:, TS:2 * TS], start=False, stop=False)
                mm(bank[6][:, TP:T], col(vc, h, DH), pt[:, 2 * TS:3 * TS], start=False,
                   stop=True).then_inc(o_ready, 1)

            def fourier_channels(g):
                for t in range(TT):
                    u = g * TT + t
                    if u >= 2:
                        pe.wait_ge(y1_dve if u % 2 else y1_act, l * 6 + u // 2)
                    for c in range(2):
                        last = mm(bank[4 + u % 2][:, :], col(f, 2 * g + c)[:, t * P:(t + 1) * P],
                                  dft[:, DFT_CH + c * 512:DFT_CH + (c + 1) * 512], start=(c == 0), stop=(c == 1))
                    last.then_inc(y1_ready, 1)

            def fourier_tokens(g):
                pe.wait_ge(y1_act, l * 6 + (TT * (g + 1) + 1) // 2)
                pe.wait_ge(y1_dve, l * 6 + TT * (g + 1) // 2)
                yg = col(fy, g % 2, TT * 512)
                for dt in range(2):
                    u = 2 * g + dt
                    if u >= 2:
                        pe.wait_ge(y2_lo, l * 8 + u - 1)
                    out = bank[6 + u % 2]
                    for part in range(2):
                        w = yg[:, part * FD + dt * P:part * FD + (dt + 1) * P]
                        mm(out[:, 0:TP], w, dft[:, DFT_P + part * TP:DFT_P + (part + 1) * TP],
                           start=(part == 0), stop=(part == 1))
                    for t in range(2):
                        for part in range(2):
                            w0 = (1 + t) * 512 + part * FD + dt * P
                            r0 = DFT_S + (2 * t + part) * TS
                            last = mm(out[:, TP:T], yg[:, w0:w0 + P], dft[:, r0:r0 + TS],
                                      start=(t + part == 0), stop=(t + part == 2))
                    last.then_inc(y2_ready, 1)

            pe.wait_ge(dft_loaded, (l + 1) * 16)
            pe.wait_ge(o_lo, (l + 1) * HEADS)
            fourier_channels(0)
            for g in range(1, FG):
                fourier_channels(g)
                fourier_tokens(g - 1)
            fourier_tokens(FG - 1)

            stage(l, "attn_out", h_hi, h_lo)
            pe.wait_ge(y2_lo, (l + 1) * 8)
            stage(l, "four_out", f_hi, f_lo)
            for n in range(KT):
                project(l, FIRST["o"] + n // SLOTS, n % SLOTS, u_hi, u_lo,
                        arriving=(mlo_ready, l * KT) if n == 0 else None)
                if n >= 2:
                    add_squares(2 * l + 2, n - 2)
            for n in (KT - 2, KT - 1):
                add_squares(2 * l + 2, n)
            pe.wait_ge(sub_loaded, (l + 1) * 16)

            carry(pe)

            def keys(i, s):
                n = (l * COUNT["pq"] + i) * SLOTS + s
                pe.wait_ge(bank_free[s], l * PROJ + FIRST["pq"] + i + 2)
                pe.wait_ge(sc_ready, n + 1)
                for t in range(TT):
                    last = mm(col(bank[4 + s], t, NK), col(col(pq, s), t, P),
                              subk[:, bass.ds((i * SLOTS + s) * NK, NK)], start=True, stop=True)
                last.then_inc(keys_done, 1)

            with pe.Fori(0, COUNT["pq"]) as i:
                for s in range(SLOTS):
                    project(l, i + FIRST["pq"], s, h_hi, h_lo,
                            arriving=(hlo_ready, l * 16 + 8) if s == 0 else None)
                    if s:
                        keys(i, s - 1)
                keys(i, SLOTS - 1)

            peer = l * GROUPS + FIRST["peer"]

            def early(i, first=False):
                for s in range(SLOTS):
                    if s >= 2 or not first:
                        pe.wait_ge(gelu_ready, l * NK + i * SLOTS + s - 1)
                    panel(peer + i, s, bank[s % 2][:, 0:T], h_hi, h_lo, T)

            early(0, first=True)
            carry(pe)
            with pe.Fori(0, TT) as t:
                early(t + 1)
                pe.wait_ge(route_ready, l * TT + t + 1)
                pe.wait_ge(route_done, l * TT + t + 1)
                for j in range(3):
                    last = transpose(col(bank[4], j, P), col(route, j, HK))
                last.then_inc(route_tr, 1)

            def build_gates(chunk, turn, batches, out):
                n = (l * CHUNKS + chunk) * NB + turn * PER_PAIR
                pe.wait_ge(gate_copied, n + batches[0] + 1)
                for r in batches:
                    pe.wait_ge(hot2_ready, n + r + 1)
                    pe.wait_ge(hot1_ready[r], (l * CHUNKS + chunk) * PAIRS + turn + 1)
                    for t in range(BATCH):
                        w = col(hot2, r, BATCH * P).rearrange("p (j t) -> p t j", t=BATCH)[:, t, :]
                        parts = col(hot1, r, BATCH * PARTS * CHUNK).rearrange("p (j t) -> p t j", t=BATCH)[:, t, :]
                        o = col(out, (r - batches[0]) * BATCH + t, CHUNK)
                        for c in range(PARTS):
                            last = mm(o, w, col(parts, c, CHUNK), start=(c == 0), stop=(c == PARTS - 1))
                    last.then_inc(gate_mm, 1)

            def outputs_v(g, s, b, j, first=False, last=False):
                pe.wait_ge(hi_ready[s], g + 2)
                pe.wait_ge(lo_ready[s], g + 2)
                pe.wait_ge(ahi_ready, l * NK + j + 3)
                pe.wait_ge(alo_ready, l * NK + j + 1)
                hi, lo = col(split_hi, s % 2, D), col(split_lo, s % 2, D)
                for t in range(TT):
                    w_hi, w_lo = col(col(a_hi, b), t, P), col(col(a_lo, b), t, P)
                    for w, rhs, start, stop in ((w_hi, hi, first, False), (w_hi, lo, False, False),
                                                (w_lo, hi, False, last)):
                        for c in range(2):
                            m = mm(bank[2 + 2 * t + c][:, :], w, col(rhs, c, 512), start=start, stop=stop)
                m.then_inc(panel_used[s % 2], 1)

            def scores_u(g, s, j):
                pe.wait_ge(gelu_ready, l * NK + j)
                panel(g, s, bank[0][:, 0:T], h_hi, h_lo, T)

            def pair(i, chunk):
                g, j = peer + i, 2 * i
                work = plan(i, chunk)
                steps = (lambda: scores_u(g, 1, j + 1), lambda: outputs_v(g, 2, 0, j),
                         lambda: scores_u(g, 3, j + 2), lambda: outputs_v(g + 1, 0, 1, j + 1))
                for step, batches in zip(steps, work):
                    step()
                    if batches:
                        build_gates(chunk + 1, *batches, bank[1])

            pe.wait_ge(gelu_ready, l * NK + EARLY)
            carry(pe)
            with pe.Fori(0, PAIRS) as i:
                build_gates(0, i, (0, 1), bank[1])
                build_gates(0, i, (2,), bank[2])

            def early_outputs(i, slots=range(SLOTS), first=False):
                for s in slots:
                    outputs_v(peer + EARLY_G + i, s, s % 2, i * SLOTS + s, first=first and s == 0)

            early_outputs(0, first=True)
            carry(pe)
            with pe.Fori(1, EARLY_G - 1) as i:
                early_outputs(i)
            early_outputs(EARLY_G - 1, slots=range(3))
            g = peer + 2 * EARLY_G - 1
            scores_u(g, 3, EARLY)
            outputs_v(g + 1, 0, 1, EARLY - 1)
            for chunk in range(CHUNKS):
                carry(pe)
                with pe.Fori(*pairs_of(chunk)) as i:
                    pair(i, chunk)
            g = peer + LAST_PAIR
            scores_u(g, 1, NK - 1)
            outputs_v(g, 2, 0, NK - 2)
            outputs_v(g, 3, 1, NK - 1, last=True)

            pe.wait_ge(y_act, (l + 1) * TT)
            pe.wait_ge(y_dve, (l + 1) * TT)
            for kk in range(KT):
                if kk >= 2:
                    pe.wait_ge(x_updated, l * KT + kk)
                for t in range(TT):
                    last = transpose(col(bank[kk % 2], t, P), y_nat[:, t * D + kk * P:t * D + (kk + 1) * P])
                last.then_inc(yt_ready, 1)
                if kk >= 2:
                    add_squares(2 * l + 3, kk - 2)
            for kk in (KT - 2, KT - 1):
                add_squares(2 * l + 3, kk)

    @block.scalar
    def _(act):
        copy = lambda out, in_: nc.scalar.activation(out, in_, ACT.Copy)

        def group(l, local, epilogue=None, after=None):
            for s in range(SLOTS):
                split_panel_hi(*ahead(l * GROUPS + local, s))
                if epilogue:
                    epilogue(s)
            if after:
                after()

        def product(g, s):
            act.wait_ge(panel_used[s % 2], after_use(g, s))
            return bank[s][:, 0:T]

        def square(kk):
            nc.scalar.activation(col(sq, kk), col(x, kk), ACT.Square).then_inc(squares, 1)

        def root_of(n):
            act.wait_ge(mean_sq, n)
            nc.scalar.activation(ms[:, :], ms[:, :], ACT.Sqrt).then_inc(root, 1)

        def shift_input(l, half):
            for kk in range(KT):
                act.wait_ge(hf_ready, l * 16 + half * 8 + kk + 1)
                for m, (beg, end) in enumerate(STREAMS):
                    c = ((SHIFT2 if half else SHIFT1) * KT + kk) * 2 + m
                    last = nc.scalar.activation(col(h_hi, kk)[:, beg:end], col(hf, kk)[:, beg:end], ACT.Identity,
                                                bias=modv[:, c:c + 1])
                last.then_inc(hhi_ready, 1)

        act.sem_inc(sc_ready, 4)
        act.sem_inc(gate_copied, 1)
        for s in range(SLOTS):
            act.sem_inc(hi_ready[s], 1)
        act.sem_inc(route_done, 1)
        act.sem_inc(ahi_ready, 2)
        act.wait_ge(c_loaded, 16)
        nc.scalar.activation(silu_c[:, :], silu_c[:, :], ACT.Silu).then_inc(c_ready, 1)
        act.wait_ge(consts_loaded, CONSTS * 16)
        for kk in range(KT):
            square(kk)
        with act.Fori(0, DEPTH) as l:
            act.dma_start(dft[:, :], dft_in).then_inc(dft_loaded, 16)
            for h in range(2):
                act.dma_start(col(bias, h, 2 * TS), bias_in[l * HEADS + h, :, :]).then_inc(bias_loaded[h], 16)
            split_panel_hi(l * GROUPS, 0)
            split_panel_hi(l * GROUPS, 1)
            root_of(2 * l + 1)
            shift_input(l, 0)

            with act.Fori(0, COUNT["ccx"]) as i:
                local = i + FIRST["ccx"]

                def store_cc(s):
                    if s % 2 == 0:
                        out = product(l * GROUPS + local, s)
                        act.wait_ge(bank_free[s + 1], l * PROJ + local + 1)
                        copy(col(cc_s, s // 2), out).then_inc(bank_free[s], 1)
                group(l, local, store_cc)

            with act.Fori(0, COUNT["cb"]) as i:
                local = i + FIRST["cb"]

                def split_conv(s):
                    act.wait_ge(bank_free[s], l * PROJ + local + 2)
                    copy(u_hi[:, bass.ds((i * SLOTS + s) * T, T)], col(cb_s, s % 2)).then_inc(uhi_ready, 1)
                group(l, local, split_conv)

            with act.Fori(0, COUNT["qkvf"]) as i:
                local = i + FIRST["qkvf"]

                def store(s):
                    if s % 2 == 0:
                        out = product(l * GROUPS + local, s)
                        copy(qkvf[:, bass.ds((i * SLOTS + s) * T, T)], out).then_inc(bank_free[s], 1)
                group(l, local, store)

            for first, turns, dst in ((0, 4, gate01), (4, 2, gate2)):
                if first:
                    for b in range(2):
                        act.wait_ge(mod_used[b], (l + 1) * MOD_G * 2 + 1)
                    for dst_, src in ((kc, k_cache[l, :, :]), (vc, v_cache[l, :, :])):
                        act.dma_start(dst_[:, :], src).then_inc(kv_loaded, 16)
                with act.Fori(0, turns) as i:
                    local = i + FIRST["gates"] + first

                    def store_gate(s):
                        out = product(l * GROUPS + local, s)
                        nc.scalar.activation(dst[:, bass.ds((i * SLOTS + s) * T, T)], out,
                                             ACT.Sigmoid).then_inc(bank_free[s], 1)
                    group(l, local, store_gate)

            for s in (1, 3):
                act.wait_ge(bank_free[s], l * PROJ + FIRST["gates"] + 1)
            wait_stored(act, l, "gates")
            act.dma_start(new_k[l, :, :, :], k.rearrange("p (h t) -> p h t", h=HEADS)[:, :, 0:TP]
                          ).then_inc(kv_out, 16)
            for h in range(0, HEADS, 2):
                act.wait_ge(vt_ready, l * HEADS + h + 1)
                copy(col(v, h), bank[4 + h % 4][:, 0:T]).then_inc(vt_act, 1)
            act.wait_ge(vt_act, l * 4 + 4)
            act.wait_ge(vt_dve, l * 4 + 4)
            act.dma_start(new_v[l, :, :, :], v.rearrange("p (h t) -> p h t", h=HEADS)[:, :, 0:DH]
                          ).then_inc(kv_out, 16)

            def exps(h):
                pr, sm = col(prob, h % 2, SCORES), col(softm, h % 2, 16)
                act.wait_ge(max_ready, l * HEADS + h + 1)
                for r, (beg, end) in enumerate(((0, TP), (TP, TP + KEYS), (TP + KEYS, SCORES))):
                    last = nc.scalar.activation(pr[:, beg:end], pr[:, beg:end], ACT.Exp, bias=sm[:, r:r + 1],
                                                scale=1.0, accum_out=sm[:, 4 + r:5 + r])
                last.then_inc(exp_ready, 1)

            exps(0)
            for h in range(HEADS):
                if h + 1 < HEADS:
                    exps(h + 1)
                if h + 2 < HEADS:
                    act.wait_ge(s_read, l * HEADS + h + 1)
                    act.dma_start(col(bias, h % 2, 2 * TS), bias_in[l * HEADS + h + 2, :, :]
                                  ).then_inc(bias_loaded[h % 2], 16)
                split_panel_hi(*ahead(l * GROUPS + FIRST["conv_out"] + h // SLOTS, h % SLOTS))
                act.wait_ge(pt_ready, l * HEADS + h + 1)
                if h >= 2:
                    act.wait_ge(o_ready, l * HEADS + h - 1)
                copy(col(prob_t, h % 2, SCORES)[:, 0:512], bank[6][:, :]).then_inc(pt_act, 1)
                act.wait_ge(o_ready, l * HEADS + h + 1)
                copy(col(h_hi, h), bank[6][:, 0:T]).then_inc(o_hi, 1)

            act.wait_ge(kv_out, (l + 1) * 32)

            def store_channels(g):
                for u in range(g * TT, (g + 1) * TT):
                    if u % 2 == 0:
                        act.wait_ge(y1_ready, l * 12 + u + 1)
                        if g >= 2:
                            act.wait_ge(y2_ready, l * 8 + 2 * (g - 1))
                        copy(col(col(fy, g % 2, TT * 512), u % TT, 512), bank[4][:, :]).then_inc(y1_act, 1)

            def split_tokens(g):
                for u in (2 * g, 2 * g + 1):
                    act.wait_ge(y2_ready, l * 8 + u + 1)
                    copy(col(f_hi, u), bank[6 + u % 2][:, 0:T]).then_inc(y2_hi, 1)

            store_channels(0)
            for g in range(1, FG):
                store_channels(g)
                split_tokens(g - 1)
            split_tokens(FG - 1)

            with act.Fori(0, COUNT["attn_out"]) as i:
                group(l, i + FIRST["attn_out"])
            with act.Fori(0, COUNT["four_out"]) as i:
                def split_merged(s):
                    act.wait_ge(merged, l * KT + i * SLOTS + s + 1)
                    n = bass.ds((i * SLOTS + s) * T, T)
                    copy(u_hi[:, n], gate01[:, n]).then_inc(mhi_ready, 1)
                group(l, i + FIRST["four_out"], split_merged)
            act.dma_start(subk[:, :], sub_keys[l, :, :]).then_inc(sub_loaded, 16)
            for n in range(KT):
                local, s = FIRST["o"] + n // SLOTS, n % SLOTS
                split_panel_hi(*ahead(l * GROUPS + local, s))
                act.wait_ge(bank_free[s], l * PROJ + local + 2)
                square(n)
            root_of(2 * l + 2)
            shift_input(l, 1)

            with act.Fori(0, COUNT["pq"]) as i:
                local = i + FIRST["pq"]

                def store_scores(s):
                    n = (l * COUNT["pq"] + i) * SLOTS + s
                    act.wait_ge(keys_done, n + 1 + 4)
                    act.wait_ge(sc_used, n + 1)
                    copy(col(sc, s), bank[4 + s][:, 0:T]).then_inc(sc_ready, 1)

                def store_query(s):
                    out = product(l * GROUPS + local, s)
                    act.wait_ge(keys_done, (l * COUNT["pq"] + i) * SLOTS + s + 1)
                    copy(col(pq, s), out).then_inc(bank_free[s], 1)
                    if s:
                        store_scores(s - 1)
                group(l, local, store_query, lambda: store_scores(SLOTS - 1))

            peer = l * GROUPS + FIRST["peer"]

            def early(i):
                for s in range(SLOTS):
                    act.wait_ge(panel_used[s % 2], after_use(peer + i, s))
                    nc.scalar.activation(gel_early[:, bass.ds((i * SLOTS + s) * T, T)], bank[s % 2][:, 0:T],
                                         ACT.Gelu).then_inc(gelu_ready, 1)
                    split_panel_hi(*ahead(peer + i, s))

            early(0)
            with act.Fori(0, TT) as t:
                early(t + 1)
                act.wait_ge(top_shifted, l * TT + t + 1)
                nc.scalar.activation(best[:, :], best[:, :], ACT.Exp).then_inc(top_exp, 1)
                act.wait_ge(route_tr, l * TT + t + 2)
                copy(route_t[:, 0:2 * T].rearrange("p (j t) -> p j t", j=2)[:, :, bass.ds(t * P, P)],
                     bank[4][:, 0:2 * P].rearrange("p (j t) -> p j t", j=2))
                copy(gate_t[:, bass.ds(t * P, P)], col(bank[4], 2, P)).then_inc(gate_hi, 1)

            def store_gates(chunk, turn, batches, src):
                act.wait_ge(gate_mm, (l * CHUNKS + chunk) * NB + turn * PER_PAIR + batches[-1] + 1 + PER_PAIR)
                n = len(batches) * BATCH
                dst = col(gates, chunk % 2, CHUNK * T).rearrange("p (j t) -> p j t", j=CHUNK)
                copy(dst[:, :, bass.ds(turn * (PER_PAIR * BATCH) + batches[0] * BATCH, n)],
                     src[:, 0:n * CHUNK].rearrange("p (t j) -> p j t", j=CHUNK)).then_inc(gate_copied, len(batches))

            def gelu(i, b, g, s):
                j = l * NK + 2 * i + b
                act.wait_ge(panel_used[s % 2], after_use(g, s))
                act.wait_ge(act_ready, j + 1)
                nc.scalar.activation(col(gel, b), bank[0][:, 0:T], ACT.Gelu).then_inc(gelu_ready, 1)

            def split_act(j, b, before):
                act.wait_ge(act_ready, l * NK + j + 1 + 2)
                if before:
                    act.wait_ge(panel_used[before[1] % 2], after_use(*before))
                copy(col(a_hi, b), col(act_f, b)).then_inc(ahi_ready, 1)

            def pair(i, chunk, first=False, last=False):
                g = peer + i
                work = plan(i, chunk)

                def store(n):
                    if work[n]:
                        store_gates(chunk + 1, *work[n], bank[1])
                gelu(i, 0, g - 1, 3)
                if not first:
                    store_behind(i - 1, chunk)
                split_act(2 * i, 0, (g - 1, 2))
                split_panel_hi(g, 2)
                split_panel_hi(g, 3)
                gelu(i, 1, g, 1)
                store(0)
                split_act(2 * i + 1, 1, (g, 0))
                if not last:
                    split_panel_hi(g + 1, 0)
                store(1)
                if not last:
                    split_panel_hi(g + 1, 1)
                store(2)

            def store_behind(i, chunk):
                if plan(i, chunk)[3]:
                    store_gates(chunk + 1, *plan(i, chunk)[3], bank[1])

            with act.Fori(0, PAIRS) as i:
                store_gates(0, i, (0, 1), bank[1])
                store_gates(0, i, (2,), bank[2])

            def early_outputs(i, slots=range(SLOTS), first=False):
                for s in slots:
                    g = peer + EARLY_G + i
                    split_act(i * SLOTS + s, s % 2, (g, s - 2) if s >= 2 else None if first else (g - 1, s + 2))
                    if not (first and s == 0):
                        split_panel_hi(*((g, s + 1) if s + 1 < SLOTS else (g + 1, 0)))

            early_outputs(0, first=True)
            with act.Fori(1, EARLY_G - 1) as i:
                early_outputs(i)
            early_outputs(EARLY_G - 1, slots=range(3))
            g = peer + 2 * EARLY_G - 1
            split_act(EARLY - 1, 1, (g, 1))
            split_panel_hi(g + 1, 0)
            split_panel_hi(g + 1, 1)
            act.wait_ge(act_ready, l * NK + EARLY + 2)
            for chunk in range(CHUNKS):
                if chunk:
                    act.wait_ge(act_ready, l * NK + chunk * CHUNK + 2)
                first, end = pairs_of(chunk)
                if chunk == 0:
                    pair(first, 0, first=True)
                    first += 1
                with act.Fori(first, end) as i:
                    pair(i, chunk)
                store_behind(end - 1, chunk)
            pair(LAST_PAIR, CHUNKS - 1, last=True)

            act.wait_ge(panel_used[1], after_use(peer + LAST_PAIR, 3))
            for t in range(TT):
                copy(col(y_nat, 2 * t, 512), bank[2 + 2 * t][:, :]).then_inc(y_act, 1)
            for kk in range(KT):
                act.wait_ge(x_updated, l * KT + kk + 2)
                square(kk)
        root_of(2 * DEPTH + 1)

    @block.gpsimd
    def _(pool):
        def panels_lo(l, local):
            g = l * GROUPS + local
            for s in (0, 2):
                split_panel_lo(pool, *ahead(g, s))

        def lo(dst, src, hi):
            return pool.tensor_tensor(dst, src, hi.bitcast(F32), ALU.subtract)

        pool.memset(ones[:, :], 1.0).then_inc(ones_ready, 1)
        pool.sem_inc(ulo_ready, 2)
        pool.sem_inc(lo_ready[0], 1)
        pool.sem_inc(lo_ready[2], 1)
        with pool.Fori(0, DEPTH) as l:
            split_panel_lo(pool, l * GROUPS, 0)
            with pool.Fori(FIRST["ccx"], FIRST["cb"]) as i:
                panels_lo(l, i)
            with pool.Fori(0, COUNT["cb"]) as i:
                for s in range(SLOTS):
                    if s % 2 == 0:
                        split_panel_lo(pool, *ahead(l * GROUPS + FIRST["cb"] + i, s))
                    n = bass.ds((i * SLOTS + s) * T, T)
                    pool.wait_ge(uhi_ready, l * KT + i * SLOTS + s + 1)
                    lo(u_lo[:, n], col(cb_s, s % 2), u_hi[:, n]).then_inc(ulo_ready, 1)
            with pool.Fori(FIRST["qkvf"], FIRST["conv_out"]) as i:
                panels_lo(l, i)

            def add_mask(h):
                pool.wait_ge(bias_loaded[h % 2], (l * 4 + h // 2 + 1) * 16)
                bt = col(bias, h % 2, 2 * TS).rearrange("p (r c) -> p r c", c=GRID_W)
                pool.tensor_tensor(bt, bt, mask[:, :].unsqueeze(1).broadcast_to([P, 8, GRID_W]),
                                   ALU.add).then_inc(bias_masked, 1)

            add_mask(0)
            add_mask(1)
            for h in range(HEADS):
                if h % 2 == 0:
                    split_panel_lo(pool, *ahead(l * GROUPS + FIRST["conv_out"] + h // SLOTS, h % SLOTS))
                if h + 2 < HEADS:
                    add_mask(h + 2)
            with pool.Fori(FIRST["attn_out"], FIRST["four_out"]) as i:
                panels_lo(l, i)
            with pool.Fori(0, COUNT["four_out"]) as i:
                for s in range(SLOTS):
                    if s % 2 == 0:
                        split_panel_lo(pool, *ahead(l * GROUPS + FIRST["four_out"] + i, s))
                    n = bass.ds((i * SLOTS + s) * T, T)
                    pool.wait_ge(mhi_ready, l * KT + i * SLOTS + s + 1)
                    lo(u_lo[:, n], gate01[:, n], u_hi[:, n]).then_inc(mlo_ready, 1)
            with pool.Fori(FIRST["o"], FIRST["peer"]) as i:
                panels_lo(l, i)

            def hot1_of(chunk, turn, batches):
                for r in batches:
                    if not by_vector(chunk, r):
                        gate_products(pool, l, chunk, turn, r)

            peer = l * GROUPS + FIRST["peer"]
            with pool.Fori(0, EARLY_G) as i:
                for s in range(SLOTS):
                    split_panel_lo(pool, *ahead(peer + i, s))
            with pool.Fori(0, PAIRS) as i:
                hot1_of(0, i, (0, 1, 2))
            with pool.Fori(peer + EARLY_G, peer + 2 * EARLY_G) as g:
                split_panel_lo(pool, g, 2)
                split_panel_lo(pool, g + 1, 0)
            for chunk in range(CHUNKS):
                with pool.Fori(*pairs_of(chunk)) as i:
                    work = plan(i, chunk)

                    def products(n):
                        if work[n]:
                            hot1_of(chunk + 1, *work[n])
                    split_panel_lo(pool, peer + i, 2)
                    products(0)
                    products(1)
                    split_panel_lo(pool, peer + i + 1, 0)
                    products(2)
                    products(3)
            split_panel_lo(pool, peer + LAST_PAIR, 2)

    @block.vector
    def _(dve):
        V = nc.vector
        order = Order()

        def group(l, local, epilogue=None):
            for s in range(SLOTS):
                if s % 2:
                    split_panel_lo(dve, *ahead(l * GROUPS + local, s))
                if epilogue:
                    epilogue(s)

        def product(l, local, s):
            dve.wait_ge(panel_used[s % 2], after_use(l * GROUPS + local, s))
            return bank[s][:, 0:T]

        def norm(n):
            dve.wait_ge(sums, n)
            V.tensor_scalar(ms[:, :], bank[4][:, 0:T], 1.0 / D, EPS, ALU.mult, ALU.add).then_inc(mean_sq, 1)
            dve.wait_ge(root, n)
            order.step(V.reciprocal(rstd[:, :], ms[:, :]))

        def modulate(l, half):
            def scaled(kk):
                for m, (beg, end) in enumerate(STREAMS):
                    c = (half * KT + kk) * 2 + m
                    last = V.scalar_tensor_tensor(col(hf, kk)[:, beg:end], col(x, kk)[:, beg:end], gain[:, c:c + 1],
                                                  rstd[:, beg:end], ALU.mult, ALU.mult)
                last.then_inc(hf_ready, 1)

            scaled(0)
            scaled(1)
            for kk in range(KT):
                dve.wait_ge(hhi_ready, l * 16 + half * 8 + kk + 1)
                for m, (beg, end) in enumerate(STREAMS):
                    c = ((SHIFT2 if half else SHIFT1) * KT + kk) * 2 + m
                    last = V.scalar_tensor_tensor(col(h_lo, kk)[:, beg:end], col(hf, kk)[:, beg:end],
                                                  modv[:, c:c + 1], col(h_hi, kk)[:, beg:end].bitcast(F32),
                                                  ALU.add, ALU.subtract)
                last.then_inc(hlo_ready, 1)
                if kk + 2 < KT:
                    scaled(kk + 2)

        for s in range(SLOTS):
            dve.sem_inc(bank_free[s], 1)
        dve.sem_inc(sc_used, 4)
        dve.sem_inc(act_ready, 2)
        dve.sem_inc(x_updated, 1)
        for b in range(2):
            dve.sem_inc(mod_used[b], 1)
        dve.sem_inc(lo_ready[1], 1)
        dve.sem_inc(lo_ready[3], 1)

        def modulation(panel, waste, n, used):
            for m in range(2):
                last = V.scalar_tensor_tensor(waste if m == 0 else panel, panel, 1.0, col(silu_c, m, D), ALU.mult,
                                              ALU.mult, accum_out=modv[:, bass.ds(n * 2 + m, 1)])
            last.then_inc(used, 1)

        def add_bias(l, first, blocks):
            mods = modv[:, first * 2:(first + blocks) * 2].rearrange("p (n m) -> p n m", m=2)
            order.step(V.tensor_tensor(mods, mods, vec[:, bass.ds(l * VEC + (B_MOD + first), blocks)].unsqueeze(2)
                                       .broadcast_to([P, blocks, 2]), ALU.add))

        def make_gain(l, half):
            scale, g0 = ((SCALE1, G_MIX), (SCALE2, G_FFN))[half]
            order.step(V.scalar_tensor_tensor(
                gain[:, half * 16:half * 16 + 16].rearrange("p (k m) -> p k m", m=2),
                modv[:, scale * 16:scale * 16 + 16].rearrange("p (k m) -> p k m", m=2), 1.0,
                vec[:, bass.ds(l * VEC + g0, KT)].unsqueeze(2).broadcast_to([P, KT, 2]), ALU.add, ALU.mult))

        dve.wait_ge(c_ready, 1)
        with dve.Fori(0, NEXT_G) as i:
            for s in range(SLOTS):
                dve.wait_ge(first_loaded[s], (i + 1) * 16)
                modulation(col(raw, s, D), col(waste0, s, D), i * SLOTS + s, first_used[s])
        for s in range(SLOTS):
            dve.wait_ge(first_used[s], NEXT_G)
        dve.wait_ge(consts_loaded, CONSTS * 16)
        carry(dve)

        def mod_panel(l, i, s, block):
            n = (l * MOD_G + i) * 2 + s // 2
            dve.wait_ge(mod_loaded[s % 2], (n + 1) * 16)
            modulation(col(mod_raw, s % 2, D), col(waste, s % 2, D), block, mod_used[s % 2])

        LAYER_STEPS = 324
        with dve.Fori(0, DEPTH) as l:
            layer = order.enter(l, 0, LAYER_STEPS)
            split_panel_lo(dve, l * GROUPS, 1)
            add_bias(l, SHIFT1 * KT, 2 * KT)
            make_gain(l, 0)
            norm(2 * l + 1)
            modulate(l, 0)

            order.step(V.memset(ccx[:, :], 0.0))
            carry(dve)
            with dve.Fori(0, COUNT["ccx"]) as i:
                inner = order.enter(i, 0, 6)
                local = i + FIRST["ccx"]

                def convolve(s):
                    if s % 2 == 0:
                        return
                    cx, b = product(l, local, s), s // 2
                    dve.wait_ge(bank_free[s - 1], l * PROJ + local + 2)
                    pad = col(ccx, b, PAD)
                    for (beg, end), (p0, p1) in zip(STREAMS, SEG):
                        last = V.tensor_tensor(pad[:, p0:p1], col(cc_s, b)[:, beg:end], cx[:, beg:end], ALU.mult)
                    last.then_inc(bank_free[s], 1)
                    dve.wait_ge(bank_free[s], l * PROJ + local + 2)
                    n = i * 2 + b
                    u = conv[:, bass.ds(n * PAD + 1, PAD - 2)]
                    taps = [vec[:, bass.ds(l * VEC + n + (CONV_W + tap * KT), 1)] for tap in range(3)]
                    order.step(V.tensor_scalar(u, pad[:, 0:PAD - 2], taps[0], None, ALU.mult))
                    for tap in (1, 2):
                        order.step(V.scalar_tensor_tensor(u, pad[:, tap:tap + PAD - 2], taps[tap], u,
                                                          ALU.mult, ALU.add))
                group(l, local, convolve)
                order.leave(inner, COUNT["ccx"], 6)

            with dve.Fori(0, COUNT["cb"]) as i:
                local = i + FIRST["cb"]

                def times_cb(s):
                    cb = product(l, local, s)
                    dve.wait_ge(ulo_ready, l * KT + i * SLOTS + s + 1)
                    for (beg, end), (p0, p1) in zip(STREAMS, SEG):
                        last = V.tensor_tensor(col(cb_s, s % 2)[:, beg:end],
                                               conv[:, bass.ds((i * SLOTS + s) * PAD + p0, p1 - p0)],
                                               cb[:, beg:end], ALU.mult)
                    last.then_inc(bank_free[s], 1)
                group(l, local, times_cb)

            with dve.Fori(0, COUNT["qkvf"]) as i:
                local = i + FIRST["qkvf"]

                def store(s):
                    if s % 2:
                        V.tensor_copy(qkvf[:, bass.ds((i * SLOTS + s) * T, T)],
                                      product(l, local, s)).then_inc(bank_free[s], 1)
                    mod_panel(l, i, s, GATE1 * KT + i * SLOTS + s)
                group(l, local, store)
            with dve.Fori(0, NEXT_G) as i:
                group(l, i + FIRST["gates"], lambda s: mod_panel(l, i + OWN_G, s, SHIFT1 * KT + i * SLOTS + s))
            for b in range(2):
                dve.wait_ge(mod_used[b], (l + 1) * MOD_G * 2 + 1)
            add_bias(l, GATE1 * KT, 4 * KT)
            make_gain(l, 1)
            carry(dve)
            with dve.Fori(NEXT_G, COUNT["gates"]) as i:
                group(l, i + FIRST["gates"])

            for h in range(1, HEADS, 2):
                dve.wait_ge(vt_ready, l * HEADS + h + 1)
                V.tensor_copy(col(v, h), bank[4 + h % 4][:, 0:T]).then_inc(vt_dve, 1)

            def read_scores(h):
                pr, sm, bt = col(prob, h % 2, SCORES), col(softm, h % 2, 16), col(bias, h % 2, 2 * TS)
                dve.wait_ge(s_ready, l * HEADS + h + 1)
                dve.wait_ge(bias_masked, l * HEADS + h + 1)
                if h >= 2:
                    dve.wait_ge(pt_ready, l * HEADS + h - 1)
                V.tensor_scalar(pr[:, 0:TP], bank[4][:, 0:TP], SCALE, None, ALU.mult)
                for j in range(2):
                    c0, p0 = (TP if j == 0 else 0), TP + j * KEYS
                    V.scalar_tensor_tensor(pr[:, p0:p0 + TS], bank[4 + j][:, c0:c0 + TS], SCALE,
                                           col(bt, j, TS), ALU.mult, ALU.add)
                    last = V.tensor_scalar(pr[:, p0 + TS:p0 + KEYS], bank[4 + j][:, c0 + TS:c0 + KEYS], SCALE,
                                           None, ALU.mult)
                last.then_inc(s_read, 1)
                dve.wait_ge(s_read, l * HEADS + h + 1)
                V.tensor_reduce(sm[:, 0:1], pr[:, 0:TP], AX.X, ALU.max, negate=True)
                V.tensor_reduce(sm[:, 1:3], pr[:, TP:SCORES].rearrange("p (j k) -> p j k", j=2), AX.X, ALU.max,
                                negate=True).then_inc(max_ready, 1)

            read_scores(0)
            for h in range(HEADS):
                pr, sm = col(prob, h % 2, SCORES), col(softm, h % 2, 16)
                dve.wait_ge(exp_ready, l * HEADS + h + 1)
                order.step(V.reciprocal(sm[:, 8:11], sm[:, 4:7]))
                for r, (beg, end) in enumerate(((0, TP), (TP, TP + KEYS), (TP + KEYS, SCORES))):
                    last = V.tensor_scalar(pr[:, beg:end], pr[:, beg:end], sm[:, 8 + r:9 + r], None, ALU.mult)
                last.then_inc(prob_ready, 1)
                if h + 1 < HEADS:
                    read_scores(h + 1)
                local, s = FIRST["conv_out"] + h // SLOTS, h % SLOTS
                if s % 2:
                    split_panel_lo(dve, *ahead(l * GROUPS + local, s))
                V.tensor_tensor(col(gate0, h), col(gate0, h), product(l, local, s),
                                ALU.mult).then_inc(bank_free[s], 1)
                dve.wait_ge(pt_ready, l * HEADS + h + 1)
                if h >= 2:
                    dve.wait_ge(o_ready, l * HEADS + h - 1)
                V.tensor_copy(col(prob_t, h % 2, SCORES)[:, 512:SCORES], bank[7][:, 0:SCORES - 512]
                              ).then_inc(pt_dve, 1)
                dve.wait_ge(o_hi, l * HEADS + h + 1)
                V.tensor_tensor(col(h_lo, h), bank[6][:, 0:T], col(h_hi, h).bitcast(F32),
                                ALU.subtract).then_inc(o_lo, 1)

            dve.wait_ge(kv_out, (l + 1) * 32)

            def store_channels(g):
                for u in range(g * TT, (g + 1) * TT):
                    if u % 2:
                        dve.wait_ge(y1_ready, l * 12 + u + 1)
                        if g >= 2:
                            dve.wait_ge(y2_ready, l * 8 + 2 * (g - 1))
                        V.tensor_copy(col(col(fy, g % 2, TT * 512), u % TT, 512), bank[5][:, :]).then_inc(y1_dve, 1)

            def split_tokens(g):
                for u in (2 * g, 2 * g + 1):
                    dve.wait_ge(y2_hi, l * 8 + u + 1)
                    V.tensor_tensor(col(f_lo, u), bank[6 + u % 2][:, 0:T], col(f_hi, u).bitcast(F32),
                                    ALU.subtract).then_inc(y2_lo, 1)

            store_channels(0)
            for g in range(1, FG):
                store_channels(g)
                split_tokens(g - 1)
            split_tokens(FG - 1)

            for name, gate, done in (("attn_out", gate1, None), ("four_out", gate2, merged)):
                with dve.Fori(0, COUNT[name]) as i:
                    def add_branch(s):
                        n = bass.ds((i * SLOTS + s) * T, T)
                        local = i + FIRST[name]
                        V.tensor_tensor(col(branch, s), gate[:, n], product(l, local, s),
                                        ALU.mult).then_inc(bank_free[s], 1)
                        dve.wait_ge(bank_free[s], l * PROJ + local + 2)
                        last = V.tensor_tensor(gate01[:, n], gate01[:, n], col(branch, s), ALU.add)
                        if done is not None:
                            last.then_inc(done, 1)
                    group(l, i + FIRST[name], add_branch)

            def residual(xs, in_, n, which):
                for m, (beg, end) in enumerate(STREAMS):
                    g = modv[:, bass.ds(n * 2 + (which * 16 + m), 1)]
                    last = V.scalar_tensor_tensor(xs[m], in_[:, beg:end], g, xs[m], ALU.mult, ALU.add)
                return last

            with dve.Fori(0, COUNT["o"]) as i:
                def add_mixer(s):
                    n = i * SLOTS + s
                    xs = [x[:, bass.ds(n * T + beg, end - beg)] for beg, end in STREAMS]
                    residual(xs, product(l, i + FIRST["o"], s), n, GATE1).then_inc(bank_free[s], 1)
                group(l, i + FIRST["o"], add_mixer)

            norm(2 * l + 2)
            modulate(l, 1)

            order.step(V.tensor_copy(index[:, :].rearrange("p (j t) -> p j t", t=BATCH),
                                     iota[:, :].unsqueeze(2).broadcast_to([P, P, BATCH])), hold=True)

            with dve.Fori(0, COUNT["pq"]) as i:
                steps = SLOTS * TT * 3 + 2
                inner = order.enter(i, 0, steps)

                def rank(s):
                    n = (l * COUNT["pq"] + i) * SLOTS + s
                    dve.wait_ge(sc_ready, n + 1 + 4)
                    carry(dve)
                    vs = [col(val, s * TT + t, TOPK) for t in range(TT)]
                    ix = [col(idx, s * TT + t, TOPK) for t in range(TT)]
                    ss = [col(col(sc, s), t, NK) for t in range(TT)]
                    s2 = [col(sc2, t, NK) for t in range(TT)]
                    for t in range(TT):
                        order.step(V.max(vs[t][:, 0:8], ss[t]), wait=(t == TT - 1), hold=True)
                    for t in range(TT):
                        V.max_index(ix[t][:, 0:8], vs[t][:, 0:8], ss[t])
                        order.step(V.match_replace(s2[t], vs[t][:, 0:8], ss[t], LOWEST), wait=(t == TT - 1), hold=True)
                    for t in range(TT):
                        order.step(V.max(vs[t][:, 8:16], s2[t]), wait=(t == TT - 1), hold=True)
                    for t in range(TT):
                        last = V.max_index(ix[t][:, 8:16], vs[t][:, 8:16], s2[t])
                    last.then_inc(sc_used, 1)
                group(l, i + FIRST["pq"], rank)
                dve.wait_ge(sc_used, (l * COUNT["pq"] + i + 1) * SLOTS + 4)
                for dst, src in ((vals, val), (idxs, idx)):
                    out = dst[:, :].rearrange("p (t h r) -> p h t r", t=TT, r=TOPK)[:, bass.ds(i * SLOTS, SLOTS), :, :]
                    order.step(V.tensor_copy(out, src[:, :].rearrange("p (h t r) -> p h t r", h=SLOTS, r=TOPK)))
                order.leave(inner, COUNT["pq"], steps)

            with dve.Fori(0, TT) as t:
                steps = 44
                inner = order.enter(t, 0, steps)
                width = 2 * PH * TOPK
                vt = vals[:, bass.ds(t * width, width)].rearrange("p (h c r) -> p h c r", h=PH, c=2)
                it = idxs[:, bass.ds(t * width, width)].rearrange("p (h c r) -> p h c r", h=PH, c=2)
                grid = [P, PH, TOPK, TOPK]
                order.step(V.tensor_tensor(cand[:, :].rearrange("p (h a b) -> p h a b", h=PH, a=TOPK),
                                           vt[:, :, 0, :].unsqueeze(3).broadcast_to(grid),
                                           vt[:, :, 1, :].unsqueeze(2).broadcast_to(grid), ALU.add), hold=True)
                n2 = TOPK * TOPK
                for r in range(2):
                    src = cand if r == 0 else cand2
                    for h in range(PH):
                        order.step(V.max(col(best, h, TOPK)[:, 8 * r:8 * r + 8], col(src, h, n2)), wait=(h == PH - 1), hold=True)
                    for h in range(PH):
                        b8, c = col(best, h, TOPK)[:, 8 * r:8 * r + 8], col(src, h, n2)
                        ins = V.max_index(col(pos, h, TOPK)[:, 8 * r:8 * r + 8], b8, c)
                        if r == 0:
                            ins = V.match_replace(col(cand2, h, n2), b8, c, LOWEST)
                        order.step(ins, wait=(h == PH - 1), hold=True)
                b3 = best[:, :].rearrange("p (h r) -> p h r", h=PH)
                order.step(V.tensor_copy(gsum[:, 0:PH], b3[:, :, 0]))
                V.tensor_tensor(b3, b3, gsum[:, 0:PH].unsqueeze(2).broadcast_to([P, PH, TOPK]),
                                ALU.subtract).then_inc(top_shifted, 1)
                V.tensor_scalar(pos_ab[:, 0:HK], pos[:, :], 4, None, ALU.logical_shift_right)
                order.step(V.tensor_scalar(pos_ab[:, HK:2 * HK], pos[:, :], 15, None, ALU.bitwise_and))
                order.step(V.tensor_copy(pos_f[:, :], pos_ab[:, :]))
                eq3 = [col(eq, c, HK * TOPK).rearrange("p (n j) -> p n j", j=TOPK) for c in range(2)]
                for c in range(2):
                    order.step(V.tensor_tensor(eq3[c], col(pos_f, c, HK).unsqueeze(2).broadcast_to([P, HK, TOPK]),
                                               iota[:, 0:TOPK].unsqueeze(1).broadcast_to([P, HK, TOPK]),
                                               ALU.is_equal), wait=(c == 1))
                for c in range(2):
                    e4 = col(eq, c, HK * TOPK).rearrange("p (h k j) -> p h k j", h=PH, k=TOPK)
                    order.step(V.tensor_tensor(e4, e4, it[:, :, c, :].unsqueeze(2).broadcast_to(grid), ALU.mult),
                               wait=(c == 1))
                dve.wait_ge(route_tr, l * TT + t + 1)
                for c in range(2):
                    V.tensor_reduce(col(route, c, HK), eq3[c], AX.X, ALU.add)
                dve.wait_ge(top_exp, l * TT + t + 1)
                order.step(V.tensor_reduce(gsum[:, 0:PH], b3, AX.X, ALU.add))
                order.step(V.reciprocal(gsum[:, PH:2 * PH], gsum[:, 0:PH]))
                V.tensor_tensor(col(route, 2, HK).rearrange("p (h r) -> p h r", h=PH), b3,
                                gsum[:, PH:2 * PH].unsqueeze(2).broadcast_to([P, PH, TOPK]),
                                ALU.mult).then_inc(route_ready, 1)
                dve.wait_ge(gate_hi, l * TT + t + 1)
                g1, g2, g3 = [gate_t[:, bass.ds(t * P + c * T, P)] for c in range(PARTS)]
                order.step(V.tensor_tensor(rest[:, :], col(bank[4], 2, P), g1, ALU.subtract))
                order.step(V.tensor_copy(g2, rest[:, :]))
                V.tensor_tensor(g3, rest[:, :], g2, ALU.subtract).then_inc(route_done, 1)
                order.leave(inner, TT, steps)

            dve.wait_ge(route_done, (l + 1) * TT + 1)

            def one_hots(chunk, turn, batches):
                for r in batches:
                    n = (l * CHUNKS + chunk) * NB + turn * PER_PAIR + r
                    dve.wait_ge(gate_mm, n + 1)
                    for out, w, row, c0, done in ((eq1, CHUNK, 0, chunk * CHUNK, eq_ready),
                                                  (hot2, P, 1, 0, hot2_ready)):
                        tokens = bass.ds(turn * (PER_PAIR * BATCH) + r * BATCH + row * T, BATCH)
                        V.tensor_tensor(col(out, r, BATCH * w).rearrange("p (j t) -> p j t", t=BATCH),
                                        index[:, c0 * BATCH:(c0 + w) * BATCH].rearrange("p (j t) -> p j t", t=BATCH),
                                        route_t[:, tokens].unsqueeze(1).broadcast_to([P, w, BATCH]),
                                        ALU.is_equal).then_inc(done, 1)
                    if by_vector(chunk, r):
                        gate_products(V, l, chunk, turn, r)

            peer = l * GROUPS + FIRST["peer"]

            def gated(j, b, gelu, gate):
                n = l * NK + j
                dve.wait_ge(gelu_ready, n + 1)
                dve.wait_ge(ahi_ready, n + 1)
                V.tensor_tensor(col(act_f, b), gelu, gates[:, bass.ds(gate * T, T)], ALU.mult).then_inc(act_ready, 1)
                dve.wait_ge(ahi_ready, n + 1 + 2)
                V.tensor_tensor(col(a_lo, b), col(act_f, b), col(a_hi, b).bitcast(F32),
                                ALU.subtract).then_inc(alo_ready, 1)

            def pair(i, chunk, last=False):
                work = plan(i, chunk)

                def hot(n):
                    if work[n]:
                        one_hots(chunk + 1, *work[n])

                def gated_of(b):
                    gated(2 * i + b, b, col(gel, b), 2 * i + (b + (chunk % 2 - chunk) * CHUNK))
                gated_of(0)
                hot(0)
                if chunk:
                    hot(1)
                split_panel_lo(dve, peer + i, 3)
                if not chunk:
                    hot(1)
                gated_of(1)
                hot(2)
                if not last:
                    split_panel_lo(dve, peer + i + 1, 1)
                hot(3)

            carry(dve)
            with dve.Fori(0, PAIRS) as i:
                one_hots(0, i, (0, 1, 2))

            def gated_early(i, s):
                j = i * SLOTS + s
                gated(j, s % 2, gel_early[:, bass.ds(j * T, T)], j)

            def early_outputs(i, first=False):
                for s in range(SLOTS):
                    gated_early(i, s)
                    if s % 2 == 0 and not (first and s == 0):
                        split_panel_lo(dve, peer + EARLY_G + i, s + 1)

            dve.wait_ge(gate_copied, (l * CHUNKS + 1) * NB + 1)
            early_outputs(0, first=True)
            carry(dve)
            with dve.Fori(1, EARLY_G) as i:
                early_outputs(i)
            split_panel_lo(dve, peer + 2 * EARLY_G, 1)
            for chunk in range(CHUNKS):
                if chunk:
                    dve.wait_ge(gate_copied, (l * CHUNKS + chunk + 1) * NB + 1)
                carry(dve)
                with dve.Fori(*pairs_of(chunk)) as i:
                    pair(i, chunk)
            pair(LAST_PAIR, CHUNKS - 1, last=True)

            dve.wait_ge(panel_used[1], after_use(peer + LAST_PAIR, 3))
            for t in range(TT):
                V.tensor_copy(col(y_nat, 2 * t + 1, 512), bank[3 + 2 * t][:, :]).then_inc(y_dve, 1)
            for kk in range(KT):
                dve.wait_ge(yt_ready, l * KT + kk + 1)
                xs = [col(x, kk)[:, beg:end] for beg, end in STREAMS]
                for m, (beg, end) in enumerate(STREAMS):
                    c = (GATE2 * KT + kk) * 2 + m
                    last = V.scalar_tensor_tensor(xs[m], bank[kk % 2][:, beg:end], modv[:, c:c + 1], xs[m],
                                                  ALU.mult, ALU.add)
                last.then_inc(x_updated, 1)
            order.leave(layer, DEPTH, LAYER_STEPS)

        norm(2 * DEPTH + 1)
        for kk in range(KT):
            V.scalar_tensor_tensor(col(hf, kk), col(x, kk), gfin[:, kk:kk + 1], rstd[:, :], ALU.mult,
                                   ALU.mult).then_inc(out_ready, 1)

    block_cm.__exit__(None, None, None)


def kernel(**inputs):
    import numpy as np
    import concourse.bacc as bacc
    from concourse import mybir as _mybir
    from concourse.bass_utils import run_bass_kernel_spmd

    a = {name: np.asarray(value) for name, value in inputs.items()}

    def features_first(t):
        n = t.shape[0]
        return t.reshape(n, KT, P).transpose(2, 1, 0).reshape(P, KT * n)

    def columns(w):
        n = w.shape[1]
        return w.reshape(KT, P, n // P, P).transpose(2, 1, 0, 3).reshape(n // P, P, D)

    panels = np.empty((DEPTH * GROUPS * SLOTS, P, D), np.float32)
    w_mod = a["w_mod"].reshape(DEPTH, D, N_MOD * KT, P).transpose(0, 2, 3, 1)
    blocks = [w_mod[0, :2 * KT]]
    for l in range(DEPTH):
        blocks += [w_mod[l, 2 * KT:], w_mod[(l + 1) % DEPTH, :2 * KT]]
    mod_panels = np.concatenate(blocks)
    for l in range(DEPTH):
        w_in = columns(a["w_in"][l]).reshape(10, KT, P, D)
        cb, cc, cx, q, k, v, f, g0, g1, g2 = w_in
        u = a["peer_u"][l].reshape(NK, P, KT, P).transpose(0, 3, 2, 1).reshape(NK, P, D)
        vv = a["peer_v"][l].reshape(NK, P, D)
        e = EARLY
        uv = np.empty((2 * NK, P, D), np.float32)
        uv[:e], uv[e:2 * e - 1] = u[:e], vv[:e - 1]
        uv[2 * e - 1:2 * NK - 2:2], uv[2 * e:2 * NK - 1:2] = u[e:], vv[e - 1:-1]
        uv[2 * NK - 1] = vv[NK - 1]
        parts = (np.stack([cc, cx], 1).reshape(2 * KT, P, D), cb,
                 np.concatenate([q, k, v, f]), np.concatenate([g0, g1, g2]), columns(a["w_conv_out"][l]),
                 columns(a["w_attn_out"][l]), columns(a["w_four_out"][l]), columns(a["w_o"][l]),
                 columns(a["w_pq"][l]), uv)
        at = l * GROUPS * SLOTS
        for part in parts:
            panels[at:at + len(part)] = part
            at += len(part)

    def per_feature(t):
        return t.reshape(-1, KT, P).transpose(2, 0, 1).reshape(P, -1)

    vecs = np.concatenate([np.concatenate([per_feature(a["b_mod"][l].reshape(N_MOD, D)), per_feature(a["g_mix"][l][None]),
                                     per_feature(a["g_ffn"][l][None]), per_feature(a["conv_w"][l])], 1)
                           for l in range(DEPTH)], 1)
    rows = TS // GRID_W
    dr = np.arange(rows)[None, :] - np.arange(rows)[:, None] + 7
    dc = np.arange(GRID_W)[None, :] - np.arange(GRID_W)[:, None] + WIN - 1
    padded = np.zeros(a["rpb"].shape[:3] + (2 * WIN,), np.float32)
    padded[..., :2 * WIN - 1] = a["rpb"]
    dc = np.where((dc < 0) | (dc > 2 * WIN - 2), 2 * WIN - 1, dc)
    table = padded[:, :, dr[:, None, :, None], dc[None, :, None, :]]
    table = table.reshape(DEPTH * HEADS, 2, P, TS).transpose(0, 2, 1, 3).reshape(DEPTH * HEADS, P, 2 * TS)
    c = np.arange(GRID_W)
    c0 = np.clip(c - WIN // 2, 0, GRID_W - WIN)
    window = np.where((c[None, :] >= c0[:, None]) & (c[None, :] < c0[:, None] + WIN), 0.0, -1e30)
    window = np.concatenate([window, window]).astype(np.float32)

    def transform(n):
        angle = 2 * np.pi * (np.outer(np.arange(n), np.arange(n)) % n) / n
        return np.cos(angle) / np.sqrt(n), np.sin(angle) / np.sqrt(n)

    cd, sd = transform(FD)
    cp, s_p = transform(TP)
    cs, ss = transform(TS)
    two = lambda m, w: m.reshape(2, P, w).transpose(1, 0, 2).reshape(P, 2 * w)
    tables = np.concatenate([two(np.concatenate([cd, sd], 1), 512), cp, -s_p,
                             two(np.concatenate([cs, -ss], 1), 2 * TS)], 1).astype(np.float32)

    ins = {
        "panels": panels,
        "mod_panels": mod_panels,
        "x_in": features_first(np.concatenate([a["x_prompt"][0], a["x_sample"][0]])),
        "c_in": np.concatenate([a["c_ctx"], a["c"][0]])[None],
        "vecs": vecs,
        "g_final": per_feature(a["g_final"][None]),
        "k_cache": a["cache_k"][0].transpose(0, 3, 2, 1).reshape(DEPTH, DH, HEADS * CTX),
        "v_cache": a["cache_v"][0].reshape(DEPTH, CTX, HEADS * DH),
        "bias_in": table,
        "mask_in": window,
        "dft_in": tables,
        "sub_keys": a["sub_keys"].transpose(0, 4, 1, 2, 3).reshape(DEPTH, P, 2 * PH * NK),
        "ident_in": np.eye(P, dtype=np.float32),
        "iota_in": np.tile(np.arange(P, dtype=np.float32), (P, 1)),
    }
    outs = {"y_out": (P, KT * T), "new_k": (DEPTH, DH, HEADS, TP), "new_v": (DEPTH, TP, HEADS, DH)}
    nc = bacc.Bacc("TRN2", target_bir_lowering=False, num_devices=1, dynamic_dma_scratch_size=1024)
    ins = {name: np.ascontiguousarray(value) for name, value in ins.items()}
    aps = {name: nc.dram_tensor(name, value.shape, _mybir.dt.float32, kind="ExternalInput").ap()
           for name, value in ins.items()}
    aps |= {name: nc.dram_tensor(name, shape, _mybir.dt.float32, kind="ExternalOutput").ap()
            for name, shape in outs.items()}
    build(nc, **aps)
    got = run_bass_kernel_spmd(nc, [ins], core_ids=[0]).results[0]
    y = got["y_out"].reshape(P, KT, T).transpose(2, 1, 0).reshape(T, D)
    new_k = got["new_k"].transpose(0, 3, 2, 1)[None]
    return y[None, :TP], y[None, TP:], new_k, got["new_v"][None]
```
